# Optimizing a Trainium2 kernel written in Bass

```python
import math
import jax, jax.numpy as jnp
from jax import lax
import numpy as np

D_MODEL = 1024
BATCH = 1
SEQ = 512
DEPTH = 2
DEC_BATCH = 8
DEC_SEQ = 16
PAST_LEN = 1024

CHUNK = 64
N_MIXERS = 2
N_GLA_LAYERS = (DEPTH + 1) // 2
N_GDN_LAYERS = DEPTH // 2
DEEPNORM_ALPHA = (2.0 * DEPTH) ** 0.25
DEEPNORM_BETA = (8.0 * DEPTH) ** -0.25
LN_EPS = 1e-5
RMS_EPS = 1e-6
L2_EPS = 1e-6
FFN_RES = 0.5
GLA_HEADS = 4
GLA_DK = D_MODEL // 2 // GLA_HEADS
GLA_DV = D_MODEL // GLA_HEADS
GLA_GATE_RANK = 16
GLA_GATE_TAU = 16.0
GLA_QK_W = GLA_HEADS * GLA_DK
GLA_V_W = GLA_HEADS * GLA_DV
GLA_IN = 2 * GLA_QK_W + 2 * GLA_V_W
GDN_HEAD_DIM = 128
GDN_QK_HEADS = D_MODEL // GDN_HEAD_DIM
GDN_V_HEADS = 2 * GDN_QK_HEADS
GDN_KEY_W = GDN_QK_HEADS * GDN_HEAD_DIM
GDN_VAL_W = GDN_V_HEADS * GDN_HEAD_DIM
GDN_CONV = 4
GDN_CONV_DIM = 2 * GDN_KEY_W + GDN_VAL_W
GDN_IN = GDN_CONV_DIM + GDN_VAL_W + 2 * GDN_V_HEADS
D_FF = ((8 * D_MODEL // 3 + 127) // 128) * 128

kernel_name = 'hybrid_gla_gdn_macaron_stream_step'

def layer_norm(x, g, b):
    xf = x.astype(jnp.float32)
    mu = jnp.mean(xf, -1, keepdims=True)
    var = jnp.mean(jnp.square(xf - mu), -1, keepdims=True)
    return ((xf - mu) * lax.rsqrt(var + LN_EPS) * g + b).astype(x.dtype)

def rms_norm(x, g):
    xf = x.astype(jnp.float32)
    return xf * lax.rsqrt(jnp.mean(xf * xf, -1, keepdims=True) + RMS_EPS) * g

def l2_norm(x):
    xf = x.astype(jnp.float32)
    return xf * lax.rsqrt(jnp.sum(xf * xf, -1, keepdims=True) + L2_EPS)

def swiglu_ffn(x, w_gu, w_d):
    gate, up = jnp.split(x @ w_gu, 2, axis=-1)
    return (jax.nn.silu(gate) * up) @ w_d

def to_chunks(a, chunk):
    b, t = a.shape[:2]
    a = a.reshape((b, t // chunk, chunk) + a.shape[2:])
    return jnp.moveaxis(a, (1, 3), (0, 2))

def from_chunks(a):
    a = jnp.moveaxis(a, (0, 2), (1, 3))
    b, n, c, h, d = a.shape
    return a.reshape(b, n * c, h, d)

def gla_recurrence(q, k, v, log_a, s0, chunk):
    mask = jnp.tril(jnp.ones((chunk, chunk), bool))

    def step(s, inp):
        qc, kc, vc, gc = inp
        bcum = jnp.cumsum(gc, axis=2)
        b_last = bcum[:, :, -1:, :]
        q_dec = qc * jnp.exp(bcum)
        k_inv = kc * jnp.exp(-bcum)
        att = jnp.where(mask, jnp.einsum('bhid,bhjd->bhij', q_dec, k_inv), 0.0)
        o = jnp.einsum('bhij,bhjv->bhiv', att, vc) + jnp.einsum('bhid,bhdv->bhiv', q_dec, s)
        k_end = kc * jnp.exp(b_last - bcum)
        s = jnp.exp(b_last[:, :, 0, :])[..., None] * s + jnp.einsum('bhjd,bhjv->bhdv', k_end, vc)
        return s, o

    f32 = jnp.float32
    xs = (to_chunks(q.astype(f32), chunk), to_chunks(k.astype(f32), chunk),
          to_chunks(v.astype(f32), chunk), to_chunks(log_a.astype(f32), chunk))
    s, o = lax.scan(step, s0.astype(f32), xs)
    return from_chunks(o), s

def gated_delta_recurrence(q, k, v, g, beta, s0, chunk):
    dk = q.shape[-1]
    tril_incl = jnp.tril(jnp.ones((chunk, chunk), bool))
    strict = jnp.tril(jnp.ones((chunk, chunk), bool), -1)
    eye = jnp.eye(chunk, dtype=jnp.float32)

    def step(s, inp):
        qc, kc, vc, gc, bc = inp
        gcum = jnp.cumsum(gc, axis=-1)
        diff = gcum[..., :, None] - gcum[..., None, :]
        decay = jnp.where(tril_incl, jnp.exp(jnp.where(tril_incl, diff, 0.0)), 0.0)
        kb = kc * bc[..., None]
        m = jnp.where(strict, jnp.einsum('bhid,bhjd->bhij', kb, kc) * decay, 0.0)
        rhs = jnp.concatenate([kb * jnp.exp(gcum)[..., None], vc * bc[..., None]], axis=-1)
        sol = lax.linalg.triangular_solve(eye + m, rhs, left_side=True, lower=True, unit_diagonal=True)
        w, u = sol[..., :dk], sol[..., dk:]
        v_new = u - jnp.einsum('bhid,bhdv->bhiv', w, s)
        att = jnp.einsum('bhid,bhjd->bhij', qc, kc) * decay
        o = (jnp.einsum('bhid,bhdv->bhiv', qc * jnp.exp(gcum)[..., None], s)
             + jnp.einsum('bhij,bhjv->bhiv', att, v_new))
        g_last = gcum[..., -1]
        k_end = kc * jnp.exp(g_last[..., None] - gcum)[..., None]
        s = jnp.exp(g_last)[..., None, None] * s + jnp.einsum('bhjd,bhjv->bhdv', k_end, v_new)
        return s, o

    f32 = jnp.float32
    xs = (to_chunks(q.astype(f32), chunk), to_chunks(k.astype(f32), chunk), to_chunks(v.astype(f32), chunk),
          to_chunks(g.astype(f32), chunk), to_chunks(beta.astype(f32), chunk))
    s, o = lax.scan(step, s0.astype(f32), xs)
    return from_chunks(o), s

def gla_mixer(x, s0, w_in, w_a1, w_a2, b_a, norm_g, w_o, chunk):
    b, t, _ = x.shape
    q, k, v, r = jnp.split(x @ w_in, [GLA_QK_W, 2 * GLA_QK_W, 2 * GLA_QK_W + GLA_V_W], axis=-1)
    q = q.reshape(b, t, GLA_HEADS, GLA_DK) * (GLA_DK ** -0.5)
    k = k.reshape(b, t, GLA_HEADS, GLA_DK)
    v = v.reshape(b, t, GLA_HEADS, GLA_DV)
    gate_logits = ((x @ w_a1) @ w_a2 + b_a).astype(jnp.float32)
    log_a = (jax.nn.log_sigmoid(gate_logits) / GLA_GATE_TAU).reshape(b, t, GLA_HEADS, GLA_DK)
    o, s = gla_recurrence(q, k, v, log_a, s0, chunk)
    o = rms_norm(o, norm_g).reshape(b, t, GLA_V_W) * jax.nn.silu(r.astype(jnp.float32))
    return o.astype(x.dtype) @ w_o, s

def gdn_mixer(x, s0, conv_hist, w_in, conv_w, a_log, dt_bias, norm_g, w_o, chunk):
    b, t, _ = x.shape
    qkv, z, a, bt = jnp.split(x @ w_in, [GDN_CONV_DIM, GDN_CONV_DIM + GDN_VAL_W,
                                         GDN_CONV_DIM + GDN_VAL_W + GDN_V_HEADS], axis=-1)
    xp = jnp.concatenate([conv_hist.astype(qkv.dtype), qkv], axis=1)
    conv = xp[:, 0:t] * conv_w[0]
    for j in range(1, GDN_CONV):
        conv = conv + xp[:, j:j + t] * conv_w[j]
    new_hist = xp[:, t:]
    qkv = jax.nn.silu(conv)
    q, k, v = jnp.split(qkv, [GDN_KEY_W, 2 * GDN_KEY_W], axis=-1)
    rep = GDN_V_HEADS // GDN_QK_HEADS
    q = jnp.repeat(l2_norm(q.reshape(b, t, GDN_QK_HEADS, GDN_HEAD_DIM)) * (GDN_HEAD_DIM ** -0.5), rep, axis=2)
    k = jnp.repeat(l2_norm(k.reshape(b, t, GDN_QK_HEADS, GDN_HEAD_DIM)), rep, axis=2)
    v = v.reshape(b, t, GDN_V_HEADS, GDN_HEAD_DIM)
    beta = jax.nn.sigmoid(bt.astype(jnp.float32))
    g = -jnp.exp(a_log) * jax.nn.softplus(a.astype(jnp.float32) + dt_bias)
    o, s = gated_delta_recurrence(q, k, v, g, beta, s0, chunk)
    zg = jax.nn.silu(z.astype(jnp.float32)).reshape(b, t, GDN_V_HEADS, GDN_HEAD_DIM)
    o = (rms_norm(o, norm_g) * zg).reshape(b, t, GDN_VAL_W)
    return o.astype(x.dtype) @ w_o, s, new_hist

def trunk(x, s_gla, s_gdn, conv_hist, ln_g, ln_b, ffn1_w_gu, ffn1_w_d, ffn2_w_gu, ffn2_w_d,
          gla_w_in, gla_w_a1, gla_w_a2, gla_b_a, gla_norm_g, gla_w_o,
          gdn_w_in, gdn_conv_w, gdn_a_log, gdn_dt_bias, gdn_norm_g, gdn_w_o):
    chunk = min(CHUNK, x.shape[1])
    new_gla, new_gdn, new_conv = [], [], []
    for i in range(DEPTH):
        x = layer_norm(DEEPNORM_ALPHA * x + FFN_RES * swiglu_ffn(x, ffn1_w_gu[i], ffn1_w_d[i]), ln_g[i, 0], ln_b[i, 0])
        j = i // N_MIXERS
        if i % N_MIXERS == 0:
            y, s = gla_mixer(x, s_gla[:, j], gla_w_in[j], gla_w_a1[j], gla_w_a2[j], gla_b_a[j],
                             gla_norm_g[j], gla_w_o[j], chunk)
            new_gla.append(s)
        else:
            y, s, c = gdn_mixer(x, s_gdn[:, j], conv_hist[:, j], gdn_w_in[j], gdn_conv_w[j], gdn_a_log[j],
                                gdn_dt_bias[j], gdn_norm_g[j], gdn_w_o[j], chunk)
            new_gdn.append(s)
            new_conv.append(c)
        x = layer_norm(DEEPNORM_ALPHA * x + y, ln_g[i, 1], ln_b[i, 1])
        x = layer_norm(DEEPNORM_ALPHA * x + FFN_RES * swiglu_ffn(x, ffn2_w_gu[i], ffn2_w_d[i]), ln_g[i, 2], ln_b[i, 2])
    return x, jnp.stack(new_gla, 1), jnp.stack(new_gdn, 1), jnp.stack(new_conv, 1)

def setup_inputs(seed: int = 0) -> dict:
    key = jax.random.key(seed)
    ks = jax.random.split(key, 24)
    f32 = jnp.float32

    def nrm(k, shape, scale):
        return jax.random.normal(k, shape, f32) * scale

    dt = jnp.exp(jax.random.uniform(ks[22], (N_GDN_LAYERS, GDN_V_HEADS), f32, math.log(1e-3), math.log(1e-1)))
    return {
        'x_prompt': nrm(ks[0], (BATCH, SEQ, D_MODEL), 1.0),
        'x_sample': nrm(ks[1], (DEC_BATCH, DEC_SEQ, D_MODEL), 1.0),
        'state_gla': nrm(ks[2], (DEC_BATCH, N_GLA_LAYERS, GLA_HEADS, GLA_DK, GLA_DV), 0.5),
        'state_gdn': nrm(ks[3], (DEC_BATCH, N_GDN_LAYERS, GDN_V_HEADS, GDN_HEAD_DIM, GDN_HEAD_DIM), 0.5),
        'state_gdn_conv': nrm(ks[4], (DEC_BATCH, N_GDN_LAYERS, GDN_CONV - 1, GDN_CONV_DIM), 1.0),
        'ln_g': 1.0 + nrm(ks[5], (DEPTH, 3, D_MODEL), 0.02),
        'ln_b': nrm(ks[6], (DEPTH, 3, D_MODEL), 0.02),
        'ffn1_w_gu': nrm(ks[7], (DEPTH, D_MODEL, 2 * D_FF), D_MODEL ** -0.5),
        'ffn1_w_d': nrm(ks[8], (DEPTH, D_FF, D_MODEL), D_FF ** -0.5 * DEEPNORM_BETA),
        'ffn2_w_gu': nrm(ks[9], (DEPTH, D_MODEL, 2 * D_FF), D_MODEL ** -0.5),
        'ffn2_w_d': nrm(ks[10], (DEPTH, D_FF, D_MODEL), D_FF ** -0.5 * DEEPNORM_BETA),
        'gla_w_in': nrm(ks[11], (N_GLA_LAYERS, D_MODEL, GLA_IN), D_MODEL ** -0.5),
        'gla_w_a1': nrm(ks[12], (N_GLA_LAYERS, D_MODEL, GLA_GATE_RANK), D_MODEL ** -0.5),
        'gla_w_a2': nrm(ks[13], (N_GLA_LAYERS, GLA_GATE_RANK, GLA_QK_W), GLA_GATE_RANK ** -0.5),
        'gla_b_a': nrm(ks[14], (N_GLA_LAYERS, GLA_QK_W), 0.1),
        'gla_norm_g': 1.0 + nrm(ks[15], (N_GLA_LAYERS, GLA_DV), 0.02),
        'gla_w_o': nrm(ks[16], (N_GLA_LAYERS, GLA_V_W, D_MODEL), GLA_V_W ** -0.5 * DEEPNORM_BETA),
        'gdn_w_in': nrm(ks[17], (N_GDN_LAYERS, D_MODEL, GDN_IN), D_MODEL ** -0.5),
        'gdn_conv_w': nrm(ks[18], (N_GDN_LAYERS, GDN_CONV, GDN_CONV_DIM), GDN_CONV ** -0.5),
        'gdn_a_log': jnp.log(jax.random.uniform(ks[19], (N_GDN_LAYERS, GDN_V_HEADS), f32, 1.0, 16.0)),
        'gdn_dt_bias': dt + jnp.log(-jnp.expm1(-dt)),
        'gdn_norm_g': 1.0 + nrm(ks[20], (N_GDN_LAYERS, GDN_HEAD_DIM), 0.02),
        'gdn_w_o': nrm(ks[21], (N_GDN_LAYERS, GDN_VAL_W, D_MODEL), GDN_VAL_W ** -0.5 * DEEPNORM_BETA),
    }

def reference(x_prompt, x_sample, state_gla, state_gdn, state_gdn_conv, ln_g, ln_b,
              ffn1_w_gu, ffn1_w_d, ffn2_w_gu, ffn2_w_d,
              gla_w_in, gla_w_a1, gla_w_a2, gla_b_a, gla_norm_g, gla_w_o,
              gdn_w_in, gdn_conv_w, gdn_a_log, gdn_dt_bias, gdn_norm_g, gdn_w_o):
    f32 = jnp.float32
    nb = x_prompt.shape[0]
    zero_gla = jnp.zeros((nb, N_GLA_LAYERS, GLA_HEADS, GLA_DK, GLA_DV), f32)
    zero_gdn = jnp.zeros((nb, N_GDN_LAYERS, GDN_V_HEADS, GDN_HEAD_DIM, GDN_HEAD_DIM), f32)
    zero_conv = jnp.zeros((nb, N_GDN_LAYERS, GDN_CONV - 1, GDN_CONV_DIM), x_prompt.dtype)
    y_prompt, gla_p, gdn_p, conv_p = trunk(
        x_prompt, zero_gla, zero_gdn, zero_conv, ln_g, ln_b, ffn1_w_gu, ffn1_w_d, ffn2_w_gu, ffn2_w_d,
        gla_w_in, gla_w_a1, gla_w_a2, gla_b_a, gla_norm_g, gla_w_o,
        gdn_w_in, gdn_conv_w, gdn_a_log, gdn_dt_bias, gdn_norm_g, gdn_w_o)
    y_sample, gla_s, gdn_s, conv_s = trunk(
        x_sample, state_gla, state_gdn, state_gdn_conv, ln_g, ln_b, ffn1_w_gu, ffn1_w_d, ffn2_w_gu, ffn2_w_d,
        gla_w_in, gla_w_a1, gla_w_a2, gla_b_a, gla_norm_g, gla_w_o,
        gdn_w_in, gdn_conv_w, gdn_a_log, gdn_dt_bias, gdn_norm_g, gdn_w_o)
    return (y_prompt, y_sample, gla_p, gdn_p, conv_p, gla_s, gdn_s, conv_s)


_drawn_inputs = setup_inputs


def setup_inputs(seed=0):
    import zlib

    import numpy as np

    out = dict(_drawn_inputs(seed))
    spreads = {}
    factors = {'gla_norm_g': 8.0, 'gdn_norm_g': 8.0}
    for name, (base, spread) in spreads.items():
        noise = np.random.default_rng([zlib.crc32(name.encode()), seed]).standard_normal(out[name].shape)
        drawn = base * np.exp(spread * noise) if base else spread * noise
        out[name] = __import__('jax').numpy.asarray(drawn.astype(out[name].dtype))
    for name, factor in factors.items():
        out[name] = (out[name] * factor).astype(out[name].dtype)
    return out
```

```python
from contextlib import ExitStack

import numpy as np

import concourse.bass as bass
from concourse import mybir

F32 = mybir.dt.float32
F32R = mybir.dt.float32r
U32 = mybir.dt.uint32
ALU = mybir.AluOpType
ACT = mybir.ActivationFunctionType

P = 128
D = 1024
KT = D // P
SEQ = 512
STREAMS, SLEN = 8, 16
TOK = SEQ + STREAMS * SLEN
TT = TOK // P
HALF = TOK // 2
PT = SEQ // P
DEPTH = 2
D_FF = 2816
FT = D_FF // P
GROUPS = (8, 7, 7)
N_FFN = 2 * DEPTH
GLA_HEADS = 4
GLA_CHUNK = 64
NCK = SEQ // GLA_CHUNK
GATE_TAU = 16.0
RANK = 16
GDN_KH = 8
GDN_VH = 16
CONV = 4
HIST = CONV - 1
XPW = HIST + SEQ + STREAMS * (HIST + SLEN)
XS0 = HIST + SEQ
LEVELS = 7
STREAM_LEVELS = 4
LN_EPS, RMS_EPS, L2_EPS = 1e-5, 1e-6, 1e-6
ALPHA = (2.0 * DEPTH) ** 0.25
NEG = -1.0e30

PLAN = [("ffn", 0), ("gla", 0), ("ffn", 1), ("ffn", 2), ("gdn", 0), ("ffn", 3)]

CH_FFN = 2 * FT + len(GROUPS) * KT
CH_GLA = GLA_HEADS * 6 + KT
CH_GDN = 2 * (GDN_KH // 2 * 6 + KT)
N_CHUNKS = sum({"ffn": CH_FFN, "gla": CH_GLA, "gdn": CH_GDN}[kind] for kind, _ in PLAN)

C_ID, C_ONES, C_L128, C_L64, C_L16, C_NEG128, C_NEG16, C_BO16 = (P * i for i in range(8))
C_MASK = 8 * P
C_M8 = C_MASK + LEVELS * P
C_MEAN = C_M8 + STREAMS
N_CONST = C_MEAN + 8


def constants():
    t = np.arange(P)
    row, col = t[:, None], t[None, :]
    out = np.zeros((P, N_CONST), np.float32)
    out[:, C_ID:C_ID + P] = row == col
    out[:, C_ONES:C_ONES + P] = 1.0
    for at, n in ((C_L128, P), (C_L64, GLA_CHUNK), (C_L16, SLEN)):
        out[:, at:at + P] = (row <= col) & (row // n == col // n)
    out[:, C_NEG128:C_NEG128 + P] = np.where(out[:, C_L128:C_L128 + P] > 0, 0.0, NEG)
    out[:, C_NEG16:C_NEG16 + P] = np.where(out[:, C_L16:C_L16 + P] > 0, 0.0, NEG)
    out[:, C_BO16:C_BO16 + P] = row // SLEN == col // SLEN
    for lv in range(LEVELS):
        s = 2 ** lv
        out[:, C_MASK + lv * P:C_MASK + (lv + 1) * P] = (
            (row // (2 * s) == col // (2 * s)) & ((col // s) % 2 == 1) & ((row // s) % 2 == 0))
    out[:, C_M8:C_M8 + STREAMS] = row // SLEN == np.arange(STREAMS)[None, :]
    out[:, C_MEAN] = 1.0 / D
    return out




def build(nc, wstream, x_in, consts, ln_cols, w_a1, w_a2, b_a, norm_cols, w_ab, a_dt, conv_w, hist_in,
          gla_s, gdn_s, y_out, gla_p_out, gdn_p_out, hist_out, gla_s_out, gdn_s_out):
    with ExitStack() as ctx:
        def sb(name, shape, dt=F32):
            return ctx.enter_context(nc.sbuf_tensor(name, shape, dt))

        x = sb("x", [P, KT, TOK])
        xh = sb("xh", [P, KT, TOK], F32R)
        xl = sb("xl", [P, KT, TOK], F32R)
        hh = sb("hh", [P, 8, TOK], F32R)
        hl = sb("hl", [P, 8, TOK], F32R)
        raw = sb("raw", [P, 2, D])
        wh = sb("wh", [P, 2, D], F32R)
        wl = sb("wl", [P, 2, D], F32R)
        cs = sb("cs", [P, N_CONST])
        lnc = sb("lnc", [P, DEPTH * 3, 2, KT])
        nrm = sb("nrm", [P, 4])
        small = sb("small", [P, 192])
        gq = sb("gq", [P, 896])
        convw = sb("convw", [P, GDN_KH, 4 * CONV])
        hist = sb("hist", [P, GDN_KH, 4 * STREAMS * HIST])
        newh = sb("newh", [P, GDN_KH, 4 * (STREAMS + 1) * HIST])
        work = sb("work", [P, 16384])
        gem = ctx.enter_context(nc.psum_tensor("gem", [P, 2, 2, 512], F32))
        msc = ctx.enter_context(nc.psum_tensor("msc", [P, 4, 512], F32))

        def view(at, *shape):
            n = int(np.prod(shape))
            v = work[:, at:at + n]
            if len(shape) == 1:
                return v
            names = "abcd"[:len(shape)]
            return v.rearrange(f"p ({' '.join(names)}) -> p {' '.join(names)}",
                               **{k: s for k, s in zip(names[1:], shape[1:])})

        def const(at, n=P):
            return cs[:, at:at + n]

        ident, ones = const(C_ID), const(C_ONES)

        def over_tiles(m, n):
            return m.unsqueeze(1).broadcast_to([P, n, P])

        class Signal:

            def __init__(self, name, per=1, by=1):
                self.sem = ctx.enter_context(nc.semaphore(name))
                self.per, self.by = per, by

            def at(self, step, j=0):
                return (number(step) * self.per + j + 1) * self.by

        class Tile:

            def __init__(self, b, per, i, j):
                self.n = i * per + (b + j)
                self.half = i * (per // 2) + (b + j) // 2

        def tile(b, per, i, j):
            return b + per * i + j if isinstance(i, int) else Tile(b, per, i, j)

        def number(T):
            return T.n if isinstance(T, Tile) else T

        def half(T):
            return T // 2 if isinstance(T, int) else T.half

        loaded = [Signal("chunk_loaded_even", by=16), Signal("chunk_loaded_odd", by=16)]
        hi_ready = Signal("chunk_hi_ready")
        lo_ready = Signal("chunk_lo_ready")
        tile_done = Signal("tile_done")
        evacuated = [Signal("even_tile_evacuated"), Signal("odd_tile_evacuated")]

        inputs_loaded = Signal("inputs_loaded", by=16)
        start_split = Signal("start_split")

        base, first_tile = {}, 0
        for kind, occ in PLAN:
            base[kind, occ] = first_tile
            first_tile += {"ffn": CH_FFN, "gla": CH_GLA, "gdn": CH_GDN}[kind]
        LN_OF = {("ffn", 0): 0, ("gla", 0): 1, ("ffn", 1): 2, ("ffn", 2): 3, ("gdn", 0): 4, ("ffn", 3): 5}

        def load_params(eng):
            n = 0
            for dst, src in ((x[:], x_in), (cs[:], consts), (lnc[:], ln_cols), (nrm[:], norm_cols)):
                eng.dma_start(dst, src).then_inc(inputs_loaded.sem, inputs_loaded.by)
                n += 1
            return n
        N_IN = 4

        def pe_tile(pe, T, par, kts, rh, rl, before=None):
            if not (isinstance(T, int) and T < 2):
                pe.wait_ge(evacuated[par].sem, evacuated[par].at(half(T) - 1))
            pe.wait_ge(lo_ready.sem, lo_ready.at(T))
            for k in range(kts):
                if before:
                    before(k)
                w_hi, w_lo = wh[:, par, k * P:(k + 1) * P], wl[:, par, k * P:(k + 1) * P]
                for n, (w, r) in enumerate(((w_hi, rh), (w_hi, rl), (w_lo, rh))):
                    for s in range(2):
                        mm = pe.matmul(gem[:, par, s, 0:HALF], w, r[:, k, s * HALF:(s + 1) * HALF],
                                       start=(k == 0 and n == 0), stop=(k == kts - 1 and n == 2))
            mm.then_inc(tile_done.sem, tile_done.by)

        def slot(par):
            return gem[:, par, :, 0:HALF]

        def halves(ap):
            return ap.rearrange("p (s n) -> p s n", s=2)

        def act_split(act, T, par):
            if isinstance(T, int) and T + 2 >= N_CHUNKS:
                return
            nxt = half(T) + 1
            act.wait_ge(loaded[par].sem, loaded[par].at(nxt))
            if not (isinstance(T, int) and T < 0):
                act.wait_ge(tile_done.sem, tile_done.at(T))
            act.copy(wh[:, par, :], raw[:, par, :]).then_inc(hi_ready.sem, hi_ready.by)

        def loop(eng, n, body, first=0, peel_first=False, peel_last=False):
            lo, hi = 0, n
            if peel_first:
                body(0)
                lo = 1
            if peel_last:
                hi = n - 1
            if hi - lo == 1:
                body(lo)
            elif hi > lo:
                with eng.Fori(lo, hi) as i:
                    body(i)
            if peel_last:
                body(n - 1)

        def sp_supply(sp):
            def body(i):
                for par in range(2):
                    T = tile(0, 2, i, par)
                    if not isinstance(T, int) or T >= 2:
                        sp.wait_ge(lo_ready.sem, lo_ready.at(number(T)) - 2)
                    sp.dma_start(raw[:, par, :], wstream[number(T)]).then_inc(loaded[par].sem, loaded[par].by)
            loop(sp, N_CHUNKS // 2, body, peel_first=True)

        def pool_supply(pool):
            def body(i):
                for par in range(2):
                    T = tile(0, 2, i, par)
                    pool.wait_ge(hi_ready.sem, hi_ready.at(T))
                    pool.tensor_tensor(wl[:, par, :], raw[:, par, :], wh[:, par, :].bitcast(F32),
                                              ALU.subtract)\
                       .then_inc(lo_ready.sem, lo_ready.by)
            loop(pool, N_CHUNKS // 2, body)

        gate = view(0, TOK)
        hid = view(TOK, TOK)
        zsum, zsqs, zsq = view(2 * TOK, TOK), view(3 * TOK, TOK), view(4 * TOK, TOK)
        hid_hi = Signal("hidden_hi_ready")
        hid_lo = Signal("hidden_lo_ready")

        def ffn_parts(occ):
            b, f0 = base["ffn", occ], 0
            for g, n in enumerate(GROUPS):
                yield g, n, occ * FT + f0, b, b + 2 * n
                b += 2 * n + KT
                f0 += n

        def pe_ffn(pe, occ):
            for g, n, f0, b_up, b_down in ffn_parts(occ):
                def up(i):
                    for par in range(2):
                        pe_tile(pe, tile(b_up, 2, i, par), par, KT, xh, xl, before=xsplit_wait(pe, "ffn", occ))
                loop(pe, n, up, peel_first=(occ == 0 and g == 0))

                def down(i):
                    for par in range(2):
                        def need(k):
                            if k == 0:
                                pe.wait_ge(hid_lo.sem, hid_lo.at(f0 + n - 2))
                            if k == n - 1:
                                pe.wait_ge(hid_lo.sem, hid_lo.at(f0 + n - 1))
                        pe_tile(pe, tile(b_down, 2, i, par), par, n, hh, hl, before=need)
                loop(pe, KT // 2, down)

        def act_ffn(act, occ):
            for g, n, f0, b_up, b_down in ffn_parts(occ):
                def up(i):
                    T = tile(b_up, 2, i, 0)
                    act.wait_ge(tile_done.sem, tile_done.at(T))
                    if not (isinstance(T, int) and T < 2):
                        act.wait_ge(evacuated[1].sem, evacuated[1].at(half(T) - 1))
                    act.activation(halves(gate), slot(0), ACT.Silu).then_inc(evacuated[0].sem, evacuated[0].by)
                    act_split(act, T, 0)
                    act_split(act, tile(b_up, 2, i, 1), 1)
                loop(act, n, up, peel_first=(occ == 0 and g == 0))
                last = g == len(GROUPS) - 1

                def down(i):
                    for par in range(2):
                        T = tile(b_down, 2, i, par)
                        act_split(act, T, par)
                        if last:
                            act_square(act, ("ffn", occ), T, par, i)
                loop(act, KT // 2, down, peel_first=last, peel_last=(b_down + KT == N_CHUNKS))

        def dve_ffn(dve, occ):
            for g, n, f0, b_up, b_down in ffn_parts(occ):
                def up(i):
                    T = tile(b_up, 2, i, 1)
                    dve.wait_ge(evacuated[0].sem, evacuated[0].at(half(T)))
                    dve.wait_ge(tile_done.sem, tile_done.at(T))
                    if not (isinstance(i, int) and f0 + i < 1):
                        dve.wait_ge(hid_lo.sem, hid_lo.at(f0 + i - 1))
                    dve.tensor_tensor(halves(hid), halves(gate), slot(1), ALU.mult)\
                       .then_inc(evacuated[1].sem, 1)
                    dve.wait_ge(evacuated[1].sem, evacuated[1].at(half(T)))
                    dve.tensor_copy(hh[:, i, :], hid).then_inc(hid_hi.sem, 1)
                    dve.wait_ge(hid_hi.sem, hid_hi.at(f0 + i))
                    dve.tensor_tensor(hl[:, i, :], hid, hh[:, i, :].bitcast(F32), ALU.subtract)\
                       .then_inc(hid_lo.sem, 1)
                loop(dve, n, up, peel_first=(occ == 0 and g == 0))
                dve_down(dve, ("ffn", occ), b_down, 2.0 * ALPHA if g == 0 else 1.0,
                         stats=g == len(GROUPS) - 1)

        sq_ready = Signal("z_square_ready")
        sum_ready = Signal("z_sums_ready", per=2)

        def act_square(act, ph, T, par, i):
            k = i * 2 + (KT * LN_OF[ph] + par)
            act.wait_ge(evacuated[par].sem, evacuated[par].at(half(T)))
            if not (isinstance(k, int) and k < 1):
                act.wait_ge(sum_ready.sem, sum_ready.at(k - 1, 1))
            act.activation(zsq, x[:, i * 2 + par, :], ACT.Square).then_inc(sq_ready.sem, sq_ready.by)

        def dve_down(dve, ph, b_down, scale, stats):
            def body(i):
                for par in range(2):
                    T = tile(b_down, 2, i, par)
                    xt = x[:, i * 2 + par, :]
                    dve.wait_ge(tile_done.sem, tile_done.at(T))
                    dve.scalar_tensor_tensor(out=halves(xt), in0=halves(xt), scalar=scale, in1=slot(par),
                                             op0=ALU.mult, op1=ALU.add).then_inc(evacuated[par].sem, 1)
                    if not stats:
                        continue
                    k = i * 2 + (KT * LN_OF[ph] + par)
                    dve.wait_ge(evacuated[par].sem, evacuated[par].at(half(T)))
                    if isinstance(i, int) and i * 2 + par == 0:
                        dve.tensor_copy(zsum, xt).then_inc(sum_ready.sem, sum_ready.by)
                        dve.wait_ge(sq_ready.sem, sq_ready.at(k))
                        dve.tensor_copy(zsqs, zsq).then_inc(sum_ready.sem, sum_ready.by)
                    else:
                        dve.wait_ge(sum_ready.sem, sum_ready.at(k - 1, 1))
                        dve.tensor_tensor(zsum, zsum, xt, ALU.add).then_inc(sum_ready.sem, sum_ready.by)
                        dve.wait_ge(sq_ready.sem, sq_ready.at(k))
                        dve.tensor_tensor(zsqs, zsqs, zsq, ALU.add).then_inc(sum_ready.sem, sum_ready.by)
            loop(dve, KT // 2, body, peel_first=stats)

        st = small[:, 0:16].rearrange("p (a t) -> p a t", a=2)
        rstd, nmr, tmp5 = small[:, 16:21], small[:, 24:29], small[:, 32:37]
        diag_r, diag_n = view(2 * TOK, TT, P), view(3 * TOK, TT, P)
        norm_a, norm_b = view(5 * TOK, 2, TOK), view(7 * TOK, 2, TOK)
        stat_mm = Signal("ln_stats_multiplied")
        stat_step = Signal("ln_stats_step", per=6)
        std_ready = Signal("ln_std_ready")
        diag_ready = Signal("ln_diag_ready", per=2)
        bc_ready = Signal("ln_broadcast_ready")
        scaled = Signal("ln_tile_scaled", per=KT)
        shifted = Signal("ln_tile_shifted", per=KT)
        x_ready = Signal("x_tile_ready", per=KT)
        xh_ready = Signal("x_hi_ready", per=KT)
        xl_ready = Signal("x_lo_ready", per=KT)

        def pe_ln(pe, ph):
            L = LN_OF[ph]
            pe.wait_ge(sum_ready.sem, sum_ready.at(KT * L + KT - 1, 1))
            for a, src in ((0, zsum), (1, zsqs)):
                for t in range(TT):
                    mm = pe.matmul(msc[:, 0, a * 8 + t:a * 8 + t + 1], src[:, t * P:(t + 1) * P],
                                   cs[:, C_MEAN:C_MEAN + 1], start=True, stop=True)
            mm.then_inc(stat_mm.sem, stat_mm.by)
            pe.wait_ge(diag_ready.sem, diag_ready.at(L, 1))
            for b, dg in ((0, diag_r), (2, diag_n)):
                flat = dg.rearrange("p t n -> p (t n)")
                for s in range(2):
                    mm = pe.matmul(msc[:, b + s, 0:HALF], ones, flat[:, s * HALF:(s + 1) * HALF], start=True, stop=True)
            mm.then_inc(bc_ready.sem, bc_ready.by)

        def act_ln(act, ph):
            L = LN_OF[ph]
            act.wait_ge(stat_step.sem, stat_step.at(L, 3))
            act.activation(rstd, tmp5, ACT.Sqrt).then_inc(std_ready.sem, std_ready.by)
            for k in range(KT):
                act.wait_ge(shifted.sem, shifted.at(L, k))
                g, b = lnc[:, L, 0, k:k + 1], lnc[:, L, 1, k:k + 1]
                act.activation(xh[:, k, :], norm_b[:, k % 2, :], ACT.Identity, scale=g, bias=b)\
                   .then_inc(xh_ready.sem, xh_ready.by)
                act.activation(x[:, k, :], norm_b[:, k % 2, :], ACT.Identity, scale=g, bias=b)\
                   .then_inc(x_ready.sem, x_ready.by)

        def dve_ln(dve, ph):
            L = LN_OF[ph]
            dve.wait_ge(stat_mm.sem, stat_mm.at(L))
            dve.tensor_copy(st[:, :, 0:TT], msc[:, 0, 0:16].rearrange("p (a t) -> p a t", a=2)[:, :, 0:TT])\
               .then_inc(stat_step.sem, stat_step.by)
            dve.wait_ge(stat_step.sem, stat_step.at(L, 0))
            dve.tensor_tensor(tmp5, st[:, 0, 0:TT], st[:, 0, 0:TT], ALU.mult).then_inc(stat_step.sem, stat_step.by)
            dve.wait_ge(stat_step.sem, stat_step.at(L, 1))
            dve.tensor_tensor(tmp5, st[:, 1, 0:TT], tmp5, ALU.subtract).then_inc(stat_step.sem, stat_step.by)
            dve.wait_ge(stat_step.sem, stat_step.at(L, 2))
            eps = LN_EPS * (4.0 if ph[0] == "ffn" else 1.0)
            dve.tensor_scalar(tmp5, tmp5, 0.0, eps, ALU.max, ALU.add).then_inc(stat_step.sem, stat_step.by)
            dve.wait_ge(std_ready.sem, std_ready.at(L))
            dve.reciprocal(rstd, rstd).then_inc(stat_step.sem, stat_step.by)
            dve.wait_ge(stat_step.sem, stat_step.at(L, 4))
            dve.scalar_tensor_tensor(out=nmr, in0=st[:, 0, 0:TT], scalar=-1.0, in1=rstd, op0=ALU.mult,
                                            op1=ALU.mult)\
               .then_inc(stat_step.sem, stat_step.by)
            dve.tensor_tensor(diag_r, over_tiles(ident, TT), rstd.unsqueeze(2).broadcast_to([P, TT, P]),
                                     ALU.mult)\
               .then_inc(diag_ready.sem, diag_ready.by)
            dve.wait_ge(stat_step.sem, stat_step.at(L, 5))
            dve.tensor_tensor(diag_n, over_tiles(ident, TT), nmr.unsqueeze(2).broadcast_to([P, TT, P]),
                                     ALU.mult)\
               .then_inc(diag_ready.sem, diag_ready.by)
            dve.wait_ge(bc_ready.sem, bc_ready.at(L))

            def lo_part(k):
                dve.wait_ge(x_ready.sem, x_ready.at(L, k))
                dve.tensor_tensor(xl[:, k, :], x[:, k, :], xh[:, k, :].bitcast(F32), ALU.subtract)\
                   .then_inc(xl_ready.sem, xl_ready.by)
            for k in range(KT):
                dve.tensor_tensor(halves(norm_a[:, k % 2, :]), halves(x[:, k, :]), msc[:, 0:2, 0:HALF], ALU.mult)\
                   .then_inc(scaled.sem, scaled.by)
                dve.wait_ge(scaled.sem, scaled.at(L, k))
                if k >= 2:
                    dve.wait_ge(x_ready.sem, x_ready.at(L, k - 2))
                dve.tensor_tensor(halves(norm_b[:, k % 2, :]), halves(norm_a[:, k % 2, :]), msc[:, 2:4, 0:HALF],
                                         ALU.add)\
                   .then_inc(shifted.sem, shifted.by)
                if k >= 1:
                    lo_part(k - 1)
            lo_part(KT - 1)

        def xsplit_wait(pe, kind, occ):
            prev = PLAN.index((kind, occ)) - 1

            def need(k):
                if prev < 0:
                    pe.wait_ge(start_split.sem, start_split.at(1, k))
                else:
                    pe.wait_ge(xl_ready.sem, xl_ready.at(LN_OF[PLAN[prev]], k))
            return need
        start_split.per = KT

        flat = msc[:].rearrange("p b n -> p (b n)")
        pair = [flat[:, 0:TOK], flat[:, 2 * 512:2 * 512 + TOK]]

        def tiles5(ap):
            return ap.rearrange("p (t n) -> p t n", t=TT)

        def col(t, n=P):
            return slice(t * n, (t + 1) * n)

        def bc(ap, n):
            return ap.unsqueeze(2).broadcast_to([P, ap.shape[1], n])

        def transposes(pe, out, src, signal):
            for t in range(TT):
                mm = pe.transpose(out[:, col(t)], src[:, col(t)], ident)
            mm.then_inc(signal.sem, signal.by)

        def pe_half_tile(pe, T, par, f, before=None):
            if f == 0:
                pe.wait_ge(evacuated[par].sem, evacuated[par].at(half(T) - 1))
                pe.wait_ge(lo_ready.sem, lo_ready.at(T))
            for k in range(f * KT // 2, (f + 1) * KT // 2):
                if before:
                    before(k)
                w_hi, w_lo = wh[:, par, col(k)], wl[:, par, col(k)]
                for n, (w, r) in enumerate(((w_hi, xh), (w_hi, xl), (w_lo, xh))):
                    for s in range(2):
                        mm = pe.matmul(gem[:, par, s, 0:HALF], w, r[:, k, s * HALF:(s + 1) * HALF],
                                       start=(k == 0 and n == 0), stop=(k == KT - 1 and n == 2))
            if f:
                mm.then_inc(tile_done.sem, tile_done.by)

        def pe_projection(pe, b_down, ready, last_step):
            def down(i):
                for par in range(2):
                    def need(k):
                        if k == 0:
                            pe.wait_ge(ready.sem, ready.at(last_step - 1, 1))
                        if k == KT - 2:
                            pe.wait_ge(ready.sem, ready.at(last_step, 1))
                    pe_tile(pe, tile(b_down, 2, i, par), par, KT, hh, hl, before=need)
            loop(pe, KT // 2, down)

        def act_projection(act, ph, b_down, stats):
            def down(i):
                for par in range(2):
                    T = tile(b_down, 2, i, par)
                    act_split(act, T, par)
                    if stats:
                        act_square(act, ph, T, par, i)
            loop(act, KT // 2, down, peel_first=stats, peel_last=(b_down + KT == N_CHUNKS))

        a_in = [view(j * TOK, TOK) for j in range(4)]
        a_z = [view((4 + j) * TOK, TOK) for j in range(2)]
        a_bs, a_e, a_en, a_kd, a_qd, a_ki = (view(j * TOK, TOK) for j in range(6, 12))
        a_og = a_bs
        a_ket = view(12 * TOK, TT, P)
        a_att = view(13 * TOK, TT, P)
        a_vt = view(14 * TOK, TT, 2 * P)
        a_lah = view(16 * TOK, TT, P)
        a_o = view(16 * TOK, TT, 2 * P)
        a_sin = view(18 * TOK, STREAMS, 2, P)
        a_s = view(18 * TOK + 2048, 2 * P)
        a_vx = view(8 * TOK, STREAMS, P)
        a_f = view(8 * TOK, 2, P)
        a_sq = view(8 * TOK + 1024, 2 * P)
        a_la = view(18 * TOK + 2304, TT, 512)
        a_rank = view(10 * TOK, TOK)
        a_abs = view(8 * TOK, 2, 512)
        a_w1 = view(18 * TOK, KT, RANK)
        a_w2 = view(18 * TOK + 128, 512)
        a_b = view(18 * TOK + 640, 512)
        a_ss, a_std = small[:, 40:45], small[:, 48:53]

        gla = {n: Signal("gla_" + n, per=p) for n, p in dict(
            rank_mm=1, rank=1, logit_mm=TT, logit_act=3 * TT, la=TT, zeroed=1,
            lah=1, bc_mm=1, bs=1, v_mm=2, v=2, exp=2, kdiff=1, kexp=1, dec=3, ke_mm=1, ke=1, att_mm=1, att=1,
            s_zero=1, intra=TT, u_mm=NCK, o_mm=NCK, state=NCK, o=TT, qs_mm=1, qs=1, vx=2, su_mm=2, s_dec=2, s_new=2,
            sq=1, ss=1, std=1, rs=1, on=1, og_mm=2, og=2, split=2, mid=1).items()}
        a_param = Signal("gla_params_loaded", by=16)
        a_sld = Signal("gla_state_loaded", by=16)
        a_sst = Signal("gla_state_stored", per=2, by=16)

        def gla_tile(i, s, j, last):
            order = (4, 5, 0, 1, 2, 3).index(j)
            return tile(base["gla", 0] + 4, 6, i, order)

        GLA_FILL = (4, 5, 0, 1, 2, 3)

        def pe_gla(pe, occ):
            b = base["gla", 0]
            L = LN_OF["ffn", 0]
            need = xsplit_wait(pe, "gla", 0)

            def first(j):
                pe_half_tile(pe, b + j, j % 2, 0, need)
                pe_half_tile(pe, b + j, j % 2, 1, need)
            first(0)
            pe.wait_ge(a_param.sem, 3 * 16)
            pe.wait_ge(x_ready.sem, x_ready.at(L, KT - 1))
            for s in range(2):
                for k in range(KT):
                    mm = pe.matmul(msc[0:RANK, s, 0:HALF], a_w1[:, k, :], x[:, k, s * HALF:(s + 1) * HALF],
                                   start=(k == 0), stop=(k == KT - 1))
            mm.then_inc(gla["rank_mm"].sem, gla["rank_mm"].by)
            first(1)
            pe.wait_ge(gla["rank"].sem, gla["rank"].at(0))
            for t in range(TT):
                if t >= 2:
                    pe.wait_ge(gla["la"].sem, gla["la"].at(0, t - 2))
                bank = msc[:, 2 + t % 2, :]
                pe.matmul(bank, a_rank[0:RANK, col(t)], a_w2[0:RANK, :], start=True, stop=False)
                pe.matmul(bank, ones[0:1, :], a_b[0:1, :], start=False, stop=True).then_inc(gla["logit_mm"].sem, gla["logit_mm"].by)
            first(2)
            first(3)

            def body(i, last=False):
                h = i

                def fill(n):
                    j = GLA_FILL[n // 2]
                    if not (last and j < 4):
                        pe_half_tile(pe, gla_tile(i, h, j, last), (n // 2) % 2, n % 2)
                pe.wait_ge(gla["lah"].sem, gla["lah"].at(h))
                for t in range(TT):
                    mm = pe.matmul(flat[:, col(t)], a_lah[:, t, :], const(C_L64 if t < PT else C_L16),
                                   start=True, stop=True)
                mm.then_inc(gla["bc_mm"].sem, gla["bc_mm"].by)
                fill(0)
                pe.wait_ge(evacuated[0].sem, evacuated[0].at(half(v_tile(i, 2))))
                transposes(pe, pair[1], a_in[2], gla["v_mm"])
                pe.wait_ge(gla["bs"].sem, gla["bs"].at(h))
                pe.wait_ge(evacuated[1].sem, evacuated[1].at(half(v_tile(i, 3))))
                transposes(pe, pair[0], a_in[3], gla["v_mm"])
                fill(1)
                pe.wait_ge(gla["dec"].sem, gla["dec"].at(h, 2))
                pe.wait_ge(gla["v"].sem, gla["v"].at(h, 1))
                transposes(pe, pair[0], a_kd, gla["ke_mm"])
                for t in range(TT):
                    mm = pe.matmul(pair[1][:, col(t)], a_ki[:, col(t)], a_qd[:, col(t)], start=True, stop=True)
                mm.then_inc(gla["att_mm"].sem, gla["att_mm"].by)
                fill(2)
                pe.wait_ge(gla["ke"].sem, gla["ke"].at(h))
                pe.wait_ge(gla["att"].sem, gla["att"].at(h))
                for n in range(NCK):
                    t, c = n // 2, n % 2
                    rows = slice(GLA_CHUNK * c, GLA_CHUNK * (c + 1))
                    o = msc[:, t % 2, 0:2 * P]
                    if c == 0:
                        if t >= 2:
                            pe.wait_ge(gla["o"].sem, gla["o"].at(h, t - 2))
                        pe.matmul(o, a_att[:, t, :], a_vt[:, t, :], start=True, stop=True, skip_group_check=True)
                    if n >= 2:
                        pe.wait_ge(gla["state"].sem, gla["state"].at(h, n - 2))
                    pe.matmul(msc[:, 2 + c, 0:2 * P], a_ket[rows, t, :], a_vt[rows, t, :],
                                     start=True, stop=True)\
                       .then_inc(gla["u_mm"].sem, gla["u_mm"].by)
                    if n == 0:
                        pe.wait_ge(gla["s_zero"].sem, gla["s_zero"].at(h))
                    else:
                        pe.wait_ge(gla["state"].sem, gla["state"].at(h, n - 1))
                    pe.matmul(msc[rows, t % 2, 0:2 * P], a_qd[:, n * GLA_CHUNK:(n + 1) * GLA_CHUNK], a_s,
                                     start=False, stop=True, skip_group_check=True)\
                       .then_inc(gla["o_mm"].sem, gla["o_mm"].by)
                    if n < 7:
                        fill(3 + n)
                pe.wait_ge(a_sld.sem, a_sld.at(h))
                pe.wait_ge(gla["state"].sem, gla["state"].at(h, NCK - 1))
                for d in range(2):
                    for s in range(STREAMS):
                        c0 = SEQ + s * SLEN
                        mm = pe.matmul(msc[:, 2, d * P + s * SLEN:d * P + (s + 1) * SLEN], a_sin[:, s, d, :],
                                       a_qd[:, c0:c0 + SLEN], start=True, stop=True)
                mm.then_inc(gla["qs_mm"].sem, gla["qs_mm"].by)
                fill(10)
                pe.wait_ge(gla["o"].sem, gla["o"].at(h, PT - 2))
                pe.wait_ge(gla["qs"].sem, gla["qs"].at(h))
                pe.matmul(msc[:, 0, 0:2 * P], a_att[:, PT, :], a_vt[:, PT, :], start=True, stop=True,
                          skip_group_check=True)
                for d in range(2):
                    mm = pe.matmul(msc[:, 0, d * P:(d + 1) * P], a_f[:, d, :], ident, start=False, stop=True,
                                   skip_group_check=True)
                mm.then_inc(gla["mid"].sem, gla["mid"].by)
                for d in range(2):
                    pe.wait_ge(gla["vx"].sem, gla["vx"].at(h, d))
                    if d == 1:
                        pe.wait_ge(gla["s_new"].sem, gla["s_new"].at(h, 0))
                    for g in range(2):
                        mm = pe.matmul(msc[:, 2 + g, :], a_ket[:, PT, :],
                                       a_vx[:, 4 * g:4 * g + 4, :].rearrange("p s n -> p (s n)"),
                                       start=True, stop=True)
                    mm.then_inc(gla["su_mm"].sem, gla["su_mm"].by)
                fill(11)
                pe.wait_ge(gla["on"].sem, gla["on"].at(h))
                pe.wait_ge(gla["s_new"].sem, gla["s_new"].at(h, 1))
                for d in range(2):
                    for t in range(TT):
                        mm = pe.transpose(pair[d][:, col(t)], a_o[:, t, d * P:(d + 1) * P], ident)
                    mm.then_inc(gla["og_mm"].sem, gla["og_mm"].by)
            gla_loop(pe, body)
            pe_projection(pe, b + GLA_HEADS * 6, gla["split"], GLA_HEADS - 1)

        def v_tile(i, j):
            return tile(base["gla", 0], 6, i, j)

        def gla_loop(eng, body):
            with eng.Fori(0, GLA_HEADS - 1) as i:
                body(i)
            body(GLA_HEADS - 1, last=True)

        def act_gla(act, occ):
            b = base["gla", 0]

            def copy_in(T, par, j):
                act.wait_ge(tile_done.sem, tile_done.at(T))
                act.copy(halves(a_in[j]), slot(par)).then_inc(evacuated[par].sem, evacuated[par].by)
                act_split(act, T, par)
            copy_in(b, 0, 0)
            act.wait_ge(gla["rank_mm"].sem, gla["rank_mm"].at(0))
            act.copy(a_rank[0:RANK, :].rearrange("p (s n) -> p s n", s=2), msc[0:RANK, 0:2, 0:HALF])\
               .then_inc(gla["rank"].sem, gla["rank"].by)
            copy_in(b + 1, 1, 1)
            for t in range(TT):
                ab = a_abs[:, t % 2, :]
                act.wait_ge(gla["logit_mm"].sem, gla["logit_mm"].at(0, t))
                if t >= 2:
                    act.wait_ge(gla["la"].sem, gla["la"].at(0, t - 2))
                act.activation(ab, msc[:, 2 + t % 2, :], ACT.Abs).then_inc(gla["logit_act"].sem, gla["logit_act"].by)
                act.wait_ge(gla["logit_act"].sem, gla["logit_act"].at(0, 3 * t))
                act.activation(ab, ab, ACT.Exp, scale=-1.0).then_inc(gla["logit_act"].sem, gla["logit_act"].by)
                act.wait_ge(gla["logit_act"].sem, gla["logit_act"].at(0, 3 * t + 1))
                act.activation(ab, ab, ACT.Ln, bias=ones[:, 0:1]).then_inc(gla["logit_act"].sem, gla["logit_act"].by)
            copy_in(b + 2, 0, 2)
            copy_in(b + 3, 1, 3)

            def body(i, last=False):
                h = i

                def fill(n):
                    j = GLA_FILL[n // 2]
                    if n % 2 == 0 or (last and j < 4):
                        return
                    par = (n // 2) % 2
                    T = gla_tile(i, h, j, last)
                    act.wait_ge(tile_done.sem, tile_done.at(T))
                    if j >= 4:
                        act.activation(halves(a_z[j - 4]), slot(par), ACT.Silu).then_inc(evacuated[par].sem, evacuated[par].by)
                    else:
                        act.copy(halves(a_in[j]), slot(par)).then_inc(evacuated[par].sem, evacuated[par].by)
                    act_split(act, T, par)
                act.dma_start(a_sin.rearrange("p s d n -> p s (d n)"), gla_s[h]).then_inc(a_sld.sem, a_sld.by)
                act.wait_ge(gla["v_mm"].sem, gla["v_mm"].at(h, 0))
                act.copy(a_vt[:, :, 0:P], tiles5(pair[1])).then_inc(gla["v"].sem, gla["v"].by)
                act.wait_ge(gla["v_mm"].sem, gla["v_mm"].at(h, 1))
                act.copy(a_vt[:, :, P:2 * P], tiles5(pair[0])).then_inc(gla["v"].sem, gla["v"].by)
                act.wait_ge(gla["bs"].sem, gla["bs"].at(h))
                act.activation(a_e, a_bs, ACT.Exp, scale=1.0 / GATE_TAU).then_inc(gla["exp"].sem, gla["exp"].by)
                act.activation(a_en, a_bs, ACT.Exp, scale=-1.0 / GATE_TAU).then_inc(gla["exp"].sem, gla["exp"].by)
                act.wait_ge(gla["kdiff"].sem, gla["kdiff"].at(h))
                act.activation(a_kd, a_kd, ACT.Exp, scale=1.0 / GATE_TAU).then_inc(gla["kexp"].sem, gla["kexp"].by)
                fill(0)
                fill(1)
                act.wait_ge(gla["ke_mm"].sem, gla["ke_mm"].at(h))
                act.copy(a_ket, tiles5(pair[0])).then_inc(gla["ke"].sem, gla["ke"].by)
                fill(2)
                for n in range(NCK):
                    if n % 2:
                        act.wait_ge(gla["o_mm"].sem, gla["o_mm"].at(h, n))
                        act.copy(a_o[:, n // 2, :], msc[:, (n // 2) % 2, 0:2 * P]).then_inc(gla["o"].sem, gla["o"].by)
                    if n < 7:
                        fill(3 + n)
                act.wait_ge(gla["qs_mm"].sem, gla["qs_mm"].at(h))
                act.copy(a_f, msc[:, 2, 0:2 * P].rearrange("p (d n) -> p d n", d=2)).then_inc(gla["qs"].sem, gla["qs"].by)
                fill(10)
                act.wait_ge(gla["mid"].sem, gla["mid"].at(h))
                act.copy(a_o[:, PT, :], msc[:, 0, 0:2 * P]).then_inc(gla["o"].sem, gla["o"].by)
                for t in range(TT):
                    act.wait_ge(gla["o"].sem, gla["o"].at(h, t))
                    if t:
                        act.wait_ge(gla["sq"].sem, h * TT + t)
                    ins = act.activation(a_sq, a_o[:, t, :], ACT.Square, accum_out=a_ss[:, t:t + 1])
                    ins.then_inc(gla["sq"].sem, 1)
                act.wait_ge(gla["ss"].sem, gla["ss"].at(h))
                act.activation(a_std, a_ss, ACT.Sqrt).then_inc(gla["std"].sem, gla["std"].by)
                fill(11)
                act.wait_ge(gla["s_new"].sem, gla["s_new"].at(h, 1))
                act.dma_start(gla_s_out[h], a_sin.rearrange("p s d n -> p s (d n)")).then_inc(a_sst.sem, a_sst.by)
                act.dma_start(gla_p_out[h], a_s).then_inc(a_sst.sem, a_sst.by)
                act.wait_ge(a_sst.sem, a_sst.at(h, 1))
            gla_loop(act, body)
            act_projection(act, ("gla", 0), b + GLA_HEADS * 6, stats=True)

        def dve_gla(dve, occ):
            b = base["gla", 0]
            dve.memset(a_att, 0.0).then_inc(gla["zeroed"].sem, gla["zeroed"].by)
            for t in range(TT):
                dve.wait_ge(gla["logit_act"].sem, gla["logit_act"].at(0, 3 * t + 2))
                dve.scalar_tensor_tensor(out=a_la[:, t, :], in0=msc[:, 2 + t % 2, :], scalar=0.0,
                                                in1=a_abs[:, t % 2, :], op0=ALU.min, op1=ALU.subtract)\
                   .then_inc(gla["la"].sem, gla["la"].by)

            def body(i, last=False):
                h = i
                dve.wait_ge(gla["la"].sem, gla["la"].at(0, TT - 1))
                dve.tensor_copy(a_lah, a_la[:, :, bass.ts(h, P)]).then_inc(gla["lah"].sem, gla["lah"].by)
                dve.wait_ge(gla["bc_mm"].sem, gla["bc_mm"].at(h))
                dve.tensor_copy(a_bs, pair[0]).then_inc(gla["bs"].sem, gla["bs"].by)
                dve.wait_ge(gla["bs"].sem, gla["bs"].at(h))
                pb, sb_ = a_bs[:, 0:SEQ], a_bs[:, SEQ:TOK]
                pb3, sb3 = pb.rearrange("p (c n) -> p c n", n=GLA_CHUNK), sb_.rearrange("p (c n) -> p c n", n=SLEN)
                pk3 = a_kd[:, 0:SEQ].rearrange("p (c n) -> p c n", n=GLA_CHUNK)
                sk3 = a_kd[:, SEQ:TOK].rearrange("p (c n) -> p c n", n=SLEN)
                dve.tensor_tensor(pk3, pb3[:, :, GLA_CHUNK - 1:GLA_CHUNK].broadcast_to([P, NCK, GLA_CHUNK]), pb3,
                                  ALU.subtract)
                dve.tensor_tensor(sk3, sb3[:, :, SLEN - 1:SLEN].broadcast_to([P, STREAMS, SLEN]), sb3,
                                         ALU.subtract)\
                   .then_inc(gla["kdiff"].sem, gla["kdiff"].by)
                dve.wait_ge(gla["exp"].sem, gla["exp"].at(h, 1))
                dve.wait_ge(evacuated[1].sem, evacuated[1].at(half(v_tile(i, 1))))
                dve.scalar_tensor_tensor(out=a_qd, in0=a_in[0], scalar=float(P) ** -0.5, in1=a_e,
                                                op0=ALU.mult, op1=ALU.mult)\
                   .then_inc(gla["dec"].sem, gla["dec"].by)
                dve.tensor_tensor(a_ki, a_in[1], a_en, ALU.mult).then_inc(gla["dec"].sem, gla["dec"].by)
                dve.wait_ge(gla["kexp"].sem, gla["kexp"].at(h))
                dve.tensor_tensor(a_kd, a_in[1], a_kd, ALU.mult).then_inc(gla["dec"].sem, gla["dec"].by)
                dve.wait_ge(gla["zeroed"].sem, gla["zeroed"].at(0))
                dve.wait_ge(a_sld.sem, a_sld.at(h))
                dve.wait_ge(gla["att_mm"].sem, gla["att_mm"].at(h))
                dve.memset(a_s, 0.0).then_inc(gla["s_zero"].sem, gla["s_zero"].by)
                dve.copy_predicated(a_att[:, 0:PT, :], over_tiles(const(C_L64), PT).bitcast(U32),
                                    tiles5(pair[1])[:, 0:PT, :])
                dve.copy_predicated(a_att[:, PT, :], const(C_L16).bitcast(U32), pair[1][:, SEQ:TOK])\
                   .then_inc(gla["att"].sem, gla["att"].by)
                for n in range(NCK):
                    dve.wait_ge(gla["u_mm"].sem, gla["u_mm"].at(h, n))
                    dve.wait_ge(gla["o_mm"].sem, gla["o_mm"].at(h, n))
                    end = (n + 1) * GLA_CHUNK - 1
                    if n == 0:
                        dve.wait_ge(gla["s_zero"].sem, gla["s_zero"].at(h))
                    else:
                        dve.wait_ge(gla["state"].sem, gla["state"].at(h, n - 1))
                    dve.scalar_tensor_tensor(out=a_s, in0=a_s, scalar=a_e[:, end:end + 1],
                                                    in1=msc[:, 2 + n % 2, 0:2 * P], op0=ALU.mult, op1=ALU.add)\
                       .then_inc(gla["state"].sem, gla["state"].by)
                dve.wait_ge(gla["qs_mm"].sem, gla["qs_mm"].at(h))
                dve.wait_ge(gla["mid"].sem, gla["mid"].at(h))
                ends = a_e[:, SEQ:TOK].rearrange("p (s n) -> p s n", n=SLEN)[:, :, SLEN - 1:SLEN]\
                    .broadcast_to([P, STREAMS, P])
                for d in range(2):
                    if d:
                        dve.wait_ge(gla["su_mm"].sem, gla["su_mm"].at(h, 0))
                    v = a_vt[:, PT, d * P:(d + 1) * P].unsqueeze(1).broadcast_to([P, STREAMS, P])
                    m = bc(cs[:, C_M8:C_M8 + STREAMS], P)
                    dve.tensor_tensor(a_vx, v, m, ALU.mult).then_inc(gla["vx"].sem, gla["vx"].by)
                    dve.tensor_tensor(a_sin[:, :, d, :], a_sin[:, :, d, :], ends, ALU.mult).then_inc(gla["s_dec"].sem, gla["s_dec"].by)
                    dve.wait_ge(gla["su_mm"].sem, gla["su_mm"].at(h, d))
                    dve.wait_ge(gla["s_dec"].sem, gla["s_dec"].at(h, d))
                    dve.tensor_tensor(a_sin[:, :, d, :], a_sin[:, :, d, :],
                                             msc[:, 2:4, :].rearrange("p b (s n) -> p (b s) n", n=P), ALU.add)\
                       .then_inc(gla["s_new"].sem, gla["s_new"].by)
                dve.wait_ge(gla["sq"].sem, (h + 1) * TT)
                dve.tensor_scalar(a_ss, a_ss, 1.0 / (2 * P), RMS_EPS, ALU.mult, ALU.add).then_inc(gla["ss"].sem, gla["ss"].by)
                dve.wait_ge(gla["std"].sem, gla["std"].at(h))
                dve.reciprocal(a_std, a_std).then_inc(gla["rs"].sem, gla["rs"].by)
                dve.wait_ge(gla["rs"].sem, gla["rs"].at(h))
                dve.tensor_tensor(a_o, a_o, bc(a_std, 2 * P), ALU.mult).then_inc(gla["on"].sem, gla["on"].by)
                for d in range(2):
                    dve.wait_ge(gla["og_mm"].sem, gla["og_mm"].at(h, d))
                    dve.wait_ge(evacuated[d].sem, evacuated[d].at(half(gla_tile(i, h, 4 + d, last))))
                    if d:
                        dve.wait_ge(gla["split"].sem, gla["split"].at(h, 0))
                    dve.scalar_tensor_tensor(out=a_og, in0=pair[d], scalar=nrm[:, d:d + 1], in1=a_z[d],
                                                    op0=ALU.mult, op1=ALU.mult)\
                       .then_inc(gla["og"].sem, gla["og"].by)
                    split_hidden(dve, a_og, h, d, h, gla)
            gla_loop(dve, body)
            dve_down(dve, ("gla", 0), b + GLA_HEADS * 6, ALPHA, stats=True)

        split_hi = Signal("mixed_hi_ready")

        def split_hidden(dve, src, slot_pair, d, step, S):
            to = slot_pair * 2 + d
            k = step * 2 + (d + (0 if S is gla else 2 * GLA_HEADS))
            dve.wait_ge(S["og"].sem, S["og"].at(step, d))
            dve.tensor_copy(hh[:, to, :], src).then_inc(split_hi.sem, 1)
            dve.wait_ge(split_hi.sem, k + 1)
            dve.tensor_tensor(hl[:, to, :], src, hh[:, to, :].bitcast(F32), ALU.subtract)\
               .then_inc(S["split"].sem, S["split"].by)

        NU = 2 * TT
        d_in = [view(j * TOK, TOK) for j in range(4)]
        d_xp, d_acc = view(4 * TOK, XPW), view(4 * TOK + XPW, XPW)
        AT = 4 * TOK + 2 * XPW
        d_kk, d_qk = view(AT, TOK), view(AT + TOK, TOK)
        d_qt = view(AT, TT, P)
        d_z = [d_kk, d_qk]
        AT += 2 * TOK
        d_kq = view(AT, 2, TOK)
        AT += 2 * TOK
        d_kt = view(AT, TT, P)
        AT += TOK
        d_vt = view(AT, 2, TT, P)
        AT += 2 * TOK
        d_at = view(AT, NU, P)
        AT += NU * P
        d_U = view(AT, NU, P)
        AT += NU * P
        d_dt = view(AT, NU, P)
        d_P = d_dt
        d_o = view(AT, TT, 2, P)
        d_og = [view(AT, TOK), view(AT + TOK, TOK)]
        AT += NU * P
        d_T, d_Ml, d_M = view(AT, NU, P), view(AT + NU * P, NU, P), view(AT + 2 * NU * P, NU, P)
        d_sin = view(AT, 2, STREAMS, P)
        d_vx = view(AT + 2048, STREAMS, P)
        d_w, d_vn, d_ke = (view(AT + 3072 + j * 2 * P, 2, P) for j in range(3))
        d_f = view(AT + 3072, 2, 2, P)
        AT += 3 * NU * P
        d_s = view(AT, 2, P)
        assert AT + 2 * P <= 16384
        d_sqs = small[:, 64:64 + P]

        GN = ("g", "beta", "eg", "ke", "ngc", "neg_eg", "egl")
        NQ = len(GN)
        d_gq = gq[:, 0:NQ * TT * GDN_VH].rearrange("p (a t h) -> p a t h", a=NQ, t=TT)
        at2 = NQ * TT * GDN_VH
        d_egs = gq[:, at2:at2 + STREAMS * GDN_VH].rearrange("p (s h) -> p s h", s=STREAMS)
        at2 += STREAMS * GDN_VH
        d_hq = gq[:, at2:at2 + NQ * TT * 2].rearrange("p (a t h) -> p a t h", a=NQ, t=TT)
        at2 += NQ * TT * 2
        d_hegs = gq[:, at2:at2 + STREAMS * 2].rearrange("p (s h) -> p s h", s=STREAMS)
        at2 += STREAMS * 2
        d_ss, d_rs = gq[:, at2:at2 + NU], gq[:, at2 + NU:at2 + 2 * NU]
        d_os, d_ors = gq[:, at2 + 2 * NU:at2 + 3 * NU], gq[:, at2 + 3 * NU:at2 + 4 * NU]
        at2 += 4 * NU
        d_adt = gq[:, at2:at2 + 32].rearrange("p (a h) -> p a h", a=2)
        at2 += 32
        assert at2 <= 896
        d_wab = newh[:].rearrange("p h n -> p (h n)")[:, GDN_KH * 108 - KT * 32:].rearrange(
            "p (k n) -> p k n", k=KT)
        TH = TT * GDN_VH
        d_y, d_l, d_glast = (view(8 * TOK + j * P, TH).rearrange("p (t h) -> p t h", t=TT) for j in range(3))

        def num(name, t, v):
            return d_hq[:, GN.index(name), t, v:v + 1]

        gdn = {n: Signal("gdn_" + n, per=p) for n, p in dict(
            ab_mm=1, gates=7, gact=5, cum_mm=1, cact=3, copied=1, zero=1, cum=1, neg=1, conv_h=1,
            hq=1, qk_mm=2, sq=NU, ss=1, std=1, rs=2, qt=1, kt=1, v_mm=2, v=2, kq_mm=2, kq=2, kk_mm=1, kk=1, qkm_mm=1,
            qkm=1, dt_mm=2, dt=2, att=2, m0=2, m=2, ml=21, tr_mm=3, p_mm=18, p=18, x_mm=15, y_mm=18, t=18, u=21,
            s_zero=1, ks_mm=TT, f_mm=1, f=2, w=TT, a=TT, ke=TT, tw_mm=TT, vn=TT, o_mm=TT, o=TT, su_mm=PT, state=PT,
            vx=2, ssu_mm=2, s_dec=2, s_new=2, osq=NU, oss=1, ostd=1, ors=1, on=1, og_mm=2, og=2, split=2).items()}
        d_param = Signal("gdn_params_loaded", by=16)
        d_sld = Signal("gdn_state_loaded", by=16)
        d_sst = Signal("gdn_state_stored", per=2, by=16)
        conv_step = Signal("conv_step", per=4)
        conv_done = Signal("conv_done")
        conv_act = Signal("conv_silu_done")
        hist_stored = Signal("hist_stored", by=16)
        CHAINS = ((slice(0, 4), 0, LEVELS), (slice(4, 8), 2, LEVELS), (slice(8, 10), 0, STREAM_LEVELS))

        def gdn_start(s_half):
            return base["gdn", 0] + 4 + s_half * (4 * 6 + KT)

        def gdn_tile(hf, i, n, last):
            return tile(gdn_start(hf), 6, i, n - 4 if last else n)

        def unit(v, t):
            return 4 * v + t if t < PT else 8 + v

        def chain_items():
            for lv in range(LEVELS):
                for c, (us, bank, n) in enumerate(CHAINS):
                    if lv < n:
                        yield lv, c, us, bank, n

        ML = {}
        for lv, c, us, bank, n in chain_items():
            ML[lv, c] = len(ML)
        PX = {k: i for i, k in enumerate(k for k in ML if k[0] > 0)}
        XX = {k: i for i, k in enumerate(k for k in ML if k[0] > 0 and k[0] < CHAINS[k[1]][2] - 1)}
        gdn["ml"].per, gdn["u"].per = len(ML), len(ML)
        gdn["p_mm"].per = gdn["p"].per = gdn["y_mm"].per = len(PX)
        gdn["x_mm"].per = len(XX)
        gdn["t"].per = len(CHAINS) + len(XX)
        TX = {**{(0, c): c for c in range(3)}, **{k: 3 + i for k, i in XX.items()}}

        def pe_gdn(pe, occ):
            b = base["gdn", 0]
            need = xsplit_wait(pe, "gdn", 0)
            L = LN_OF[PLAN[PLAN.index(("gdn", 0)) - 1]]

            def first(j):
                pe_half_tile(pe, b + j, j % 2, 0, need)
                pe_half_tile(pe, b + j, j % 2, 1, need)
            first(0)
            pe.wait_ge(d_param.sem, 4 * 16)
            pe.wait_ge(x_ready.sem, x_ready.at(L, KT - 1))
            for t in range(TT):
                for k in range(KT):
                    mm = pe.matmul(msc[:, 0, t * 32:(t + 1) * 32], x[:, k, col(t)], d_wab[:, k, :],
                                   start=(k == 0), stop=(k == KT - 1))
            mm.then_inc(gdn["ab_mm"].sem, gdn["ab_mm"].by)
            first(1)
            first(2)
            pe.wait_ge(gdn["gates"].sem, gdn["gates"].at(0, 6))
            for t in range(TT):
                pe.matmul(msc[:, 1, t * 16:(t + 1) * 16], const(C_L128 if t < PT else C_L16), d_gq[:, 0, t, :],
                          start=True, stop=True)
            for t in range(TT):
                pe.matmul(msc[:, 2, t * 16:(t + 1) * 16], ones if t < PT else const(C_BO16), d_gq[:, 0, t, :],
                          start=True, stop=True)
            for s in range(STREAMS):
                mm = pe.matmul(msc[:, 3, s * 16:(s + 1) * 16],
                               cs[:, C_M8 + s:C_M8 + s + 1].broadcast_to([P, P]), d_gq[:, 0, PT, :],
                               start=True, stop=True)
            mm.then_inc(gdn["cum_mm"].sem, gdn["cum_mm"].by)
            first(3)

            def body(hf, i, last=False):
                s = i + 4 * hf

                def fill(n):
                    if not (last and n < 8):
                        pe_half_tile(pe, gdn_tile(hf, i, n // 2, last), (n // 2) % 2, n % 2)
                pe.wait_ge(gdn["hq"].sem, gdn["hq"].at(s))
                for j in range(2):
                    pe.wait_ge(conv_act.sem, conv_act.at(s * 4 + j))
                    transposes(pe, pair[j], d_in[j], gdn["qk_mm"])
                fill(0)
                fill(1)
                for j, free in ((0, gdn["qt"]), (1, gdn["kt"])):
                    pe.wait_ge(conv_act.sem, conv_act.at(s * 4 + 2 + j))
                    pe.wait_ge(free.sem, free.at(s))
                    transposes(pe, pair[j], d_in[2 + j], gdn["v_mm"])
                pe.wait_ge(gdn["v"].sem, gdn["v"].at(s, 0))
                transposes(pe, pair[0], d_qt.rearrange("p t n -> p (t n)"), gdn["kq_mm"])
                pe.wait_ge(gdn["v"].sem, gdn["v"].at(s, 1))
                transposes(pe, pair[1], d_kt.rearrange("p t n -> p (t n)"), gdn["kq_mm"])
                fill(2)
                pe.wait_ge(gdn["kq"].sem, gdn["kq"].at(s, 1))
                for out, j, signal in ((0, 0, gdn["kk_mm"]), (1, 1, gdn["qkm_mm"])):
                    for t in range(TT):
                        mm = pe.matmul(pair[out][:, col(t)], d_kq[:, 0, col(t)], d_kq[:, j, col(t)],
                                       start=True, stop=True)
                    mm.then_inc(signal.sem, signal.by)
                for v, free in ((0, gdn["kk"]), (1, gdn["qkm"])):
                    pe.wait_ge(free.sem, free.at(s))
                    for t in range(TT):
                        tri, neg = (C_L128, C_NEG128) if t < PT else (C_L16, C_NEG16)
                        pe.matmul(pair[v][:, col(t)], num("g", t, v).broadcast_to([P, P]), const(tri),
                                  start=True, stop=False)
                        mm = pe.matmul(pair[v][:, col(t)], ident, const(neg), start=False, stop=True)
                    mm.then_inc(gdn["dt_mm"].sem, gdn["dt_mm"].by)
                fill(3)
                for lv, c, us, bank, n in chain_items():
                    units = range(us.start, us.stop)
                    out0, out1 = msc[:, bank, :], msc[:, bank + 1, :]
                    if lv == 0:
                        pe.wait_ge(gdn["ml"].sem, gdn["ml"].at(s, ML[lv, c]))
                        if c == 2:
                            pe.wait_ge(gdn["t"].sem, gdn["t"].at(s, TX[0, 0]))
                        else:
                            pe.wait_ge(gdn["dt"].sem, gdn["dt"].at(s, c))
                        for k, u in enumerate(units):
                            mm = pe.transpose(out0[:, col(k)], d_Ml[:, u, :], ident)
                        mm.then_inc(gdn["tr_mm"].sem, gdn["tr_mm"].by)
                        continue
                    pe.wait_ge(gdn["ml"].sem, gdn["ml"].at(s, ML[lv, c]))
                    before = [(lv - 1, c)] + {0: [(lv - 1, 2)], 1: [], 2: [(lv, 0)]}[c]
                    pe.wait_ge(gdn["t"].sem, gdn["t"].at(s, max(TX[k] for k in before if k in TX)))
                    pe.wait_ge(gdn["u"].sem, gdn["u"].at(s, max(ML[k] for k in before if k in ML)))
                    for k, u in enumerate(units):
                        mm = pe.matmul(out0[:, col(k)], d_Ml[:, u, :], d_T[:, u, :], start=True, stop=True)
                    mm.then_inc(gdn["p_mm"].sem, gdn["p_mm"].by)
                    if c == 0 and lv <= 3:
                        fill(3 + lv)
                    pe.wait_ge(gdn["p"].sem, gdn["p"].at(s, PX[lv, c]))
                    if (lv, c) in XX:
                        for k, u in enumerate(units):
                            mm = pe.matmul(out1[:, col(k)], d_U[:, u, :], d_P[:, u, :], start=True, stop=True)
                        mm.then_inc(gdn["x_mm"].sem, gdn["x_mm"].by)
                    for k, u in enumerate(units):
                        mm = pe.matmul(out0[:, col(k)], d_P[:, u, :], d_U[:, u, :], start=True, stop=True)
                    mm.then_inc(gdn["y_mm"].sem, gdn["y_mm"].by)
                fill(7)
                for t in range(TT):
                    ks, qs, tw, o = (msc[:, j, 0:2 * P] for j in range(4))
                    if t == 0:
                        pe.wait_ge(gdn["s_zero"].sem, gdn["s_zero"].at(s))
                        pe.wait_ge(gdn["u"].sem, gdn["u"].at(s, ML[LEVELS - 1, 1]))
                    elif t < PT:
                        pe.wait_ge(gdn["state"].sem, gdn["state"].at(s, t - 1))
                    if t < PT:
                        both = d_s.rearrange("p v n -> p (v n)")
                        pe.matmul(ks, d_kq[:, 0, col(t)], both, start=True, stop=True)
                        pe.matmul(qs, d_kq[:, 1, col(t)], both, start=True, stop=True).then_inc(gdn["ks_mm"].sem, gdn["ks_mm"].by)
                    else:
                        pe.wait_ge(d_sld.sem, d_sld.at(s))
                        pe.wait_ge(gdn["state"].sem, gdn["state"].at(s, PT - 1))
                        for v in range(2):
                            out = msc[:, v, 0:2 * P].rearrange("p (a n) -> p a n", a=2)
                            for r in range(STREAMS):
                                c0 = r * SLEN
                                mm = pe.matmul(out[:, :, c0:c0 + SLEN], d_sin[:, v, r, :],
                                               d_kq[:, :, SEQ + c0:SEQ + c0 + SLEN], start=True, stop=True)
                        mm.then_inc(gdn["f_mm"].sem, gdn["f_mm"].by)
                        pe.wait_ge(gdn["f"].sem, gdn["f"].at(s, 1))
                        for j in range(2):
                            for v in range(2):
                                mm = pe.transpose(msc[:, j, col(v)], d_f[:, v, j, :], ident)
                        mm.then_inc(gdn["ks_mm"].sem, gdn["ks_mm"].by)
                    if t < 4:
                        fill(8 + t)
                    pe.wait_ge(gdn["w"].sem, gdn["w"].at(s, t))
                    for v in range(2):
                        mm = pe.matmul(tw[:, col(v)], d_U[:, unit(v, t), :], d_w[:, v, :], start=True, stop=True)
                    mm.then_inc(gdn["tw_mm"].sem, gdn["tw_mm"].by)
                    pe.wait_ge(gdn["vn"].sem, gdn["vn"].at(s, t))
                    for v in range(2):
                        mm = pe.matmul(o[:, col(v)], d_at[:, unit(v, t), :], d_vn[:, v, :], start=True, stop=True)
                    mm.then_inc(gdn["o_mm"].sem, gdn["o_mm"].by)
                    pe.wait_ge(gdn["ke"].sem, gdn["ke"].at(s, t))
                    if t < PT:
                        for v in range(2):
                            mm = pe.matmul(ks[:, col(v)], d_ke[:, v, :], d_vn[:, v, :], start=True, stop=True)
                        mm.then_inc(gdn["su_mm"].sem, gdn["su_mm"].by)
                for v in range(2):
                    pe.wait_ge(gdn["vx"].sem, gdn["vx"].at(s, v))
                    if v:
                        pe.wait_ge(gdn["s_new"].sem, gdn["s_new"].at(s, 0))
                    for g in range(2):
                        mm = pe.matmul(msc[:, g, :], d_ke[:, v, :],
                                       d_vx[:, 4 * g:4 * g + 4, :].rearrange("p s n -> p (s n)"),
                                       start=True, stop=True)
                    mm.then_inc(gdn["ssu_mm"].sem, gdn["ssu_mm"].by)
                pe.wait_ge(gdn["s_new"].sem, gdn["s_new"].at(s, 1))
                pe.wait_ge(gdn["on"].sem, gdn["on"].at(s))
                for v in range(2):
                    for t in range(TT):
                        mm = pe.transpose(pair[v][:, col(t)], d_o[:, t, v, :], ident)
                    mm.then_inc(gdn["og_mm"].sem, gdn["og_mm"].by)
            for hf in range(2):
                gdn_loop(pe, hf, body)
                pe_projection(pe, proj_start(hf), gdn["split"], 4 * hf + 3)

        def proj_start(hf):
            return base["gdn", 0] + (4 + 4 * 6 if hf == 0 else CH_GDN - KT)

        def gdn_loop(eng, hf, body):
            n = GDN_KH // 2 - hf
            with eng.Fori(0, n) as i:
                body(hf, i)
            if hf:
                body(hf, n, last=True)

        def act_gdn(act, occ):
            b = base["gdn", 0]

            def conv_in(T, par, tilenum, first):
                act.wait_ge(tile_done.sem, tile_done.at(T))
                if not first:
                    act.wait_ge(conv_done.sem, conv_done.at(tilenum - 1))
                act.copy(d_xp[:, HIST:HIST + HALF], gem[:, par, 0, 0:HALF])
                act.copy(d_xp[:, HIST + HALF:XS0], gem[:, par, 1, 0:SEQ - HALF])
                act.copy(d_xp[:, XS0:XPW].rearrange("p (s n) -> p s n", s=STREAMS)[:, :, HIST:],
                                gem[:, par, 1, SEQ - HALF:HALF].rearrange("p (s n) -> p s n", s=STREAMS))\
                   .then_inc(evacuated[par].sem, evacuated[par].by)
                act_split(act, T, par)

            def conv_out(j, tilenum, freed=None):
                act.wait_ge(conv_step.sem, conv_step.at(tilenum, 3))
                if freed:
                    act.wait_ge(freed[0].sem, freed[0].at(*freed[1:]))
                act.activation(d_in[j][:, 0:SEQ], d_acc[:, 0:SEQ], ACT.Silu)
                act.activation(d_in[j][:, SEQ:TOK].rearrange("p (s n) -> p s n", s=STREAMS),
                                      d_acc[:, XS0:XPW].rearrange("p (s n) -> p s n", s=STREAMS)[:, :, 0:SLEN],
                                      ACT.Silu)\
                   .then_inc(conv_act.sem, conv_act.by)
            conv_in(b, 0, 0, True)
            conv_out(0, 0)
            act.wait_ge(gdn["gates"].sem, gdn["gates"].at(0, 0))
            act.activation(d_l, d_y, ACT.Abs).then_inc(gdn["gact"].sem, gdn["gact"].by)
            act.wait_ge(gdn["gact"].sem, gdn["gact"].at(0, 0))
            act.activation(d_l, d_l, ACT.Exp, scale=-1.0).then_inc(gdn["gact"].sem, gdn["gact"].by)
            act.wait_ge(gdn["gact"].sem, gdn["gact"].at(0, 1))
            act.activation(d_l, d_l, ACT.Ln, bias=ones[:, 0:1]).then_inc(gdn["gact"].sem, gdn["gact"].by)
            act.activation(d_adt[:, 0, :], d_adt[:, 0, :], ACT.Exp).then_inc(gdn["gact"].sem, gdn["gact"].by)
            act.wait_ge(gdn["gates"].sem, gdn["gates"].at(0, 1))
            act.activation(d_gq[:, 1], d_gq[:, 1], ACT.Exp, scale=-1.0).then_inc(gdn["gact"].sem, gdn["gact"].by)
            conv_in(b + 1, 1, 1, False)
            conv_out(1, 1)
            conv_in(b + 2, 0, 2, False)
            conv_out(2, 2)
            act.wait_ge(gdn["copied"].sem, gdn["copied"].at(0))
            act.activation(d_gq[:, 2], d_gq[:, 4], ACT.Exp, scale=-1.0).then_inc(gdn["cact"].sem, gdn["cact"].by)
            act.activation(d_gq[:, 3], d_gq[:, 3], ACT.Exp).then_inc(gdn["cact"].sem, gdn["cact"].by)
            act.activation(d_egs, msc[:, 3, 0:P].rearrange("p (s h) -> p s h", s=STREAMS), ACT.Exp)
            act.activation(d_gq[:, 6], d_glast, ACT.Exp).then_inc(gdn["cact"].sem, gdn["cact"].by)
            conv_in(b + 3, 1, 3, False)
            conv_out(3, 3)

            def body(hf, i, last=False):
                s = i + 4 * hf

                def fill(n):
                    j = n // 2
                    if last and n < 8:
                        return
                    T = gdn_tile(hf, i, j, last)
                    if n % 2 == 0:
                        if 1 <= j <= 4 and not last:
                            freed = (gdn["qk_mm"], s, j - 1) if j <= 2 else (gdn["v_mm"], s, j - 3)
                            conv_out(j - 1, s * 4 + (4 + j - 1), freed)
                        return
                    if j < 4:
                        conv_in(T, j % 2, s * 4 + (4 + j), False)
                        return
                    act.wait_ge(tile_done.sem, tile_done.at(T))
                    act.wait_ge(gdn["m0"].sem, gdn["m0"].at(s, 1))
                    act.wait_ge(gdn["att"].sem, gdn["att"].at(s, 1))
                    act.activation(halves(d_z[j - 4]), slot(j % 2), ACT.Silu).then_inc(evacuated[j % 2].sem, evacuated[j % 2].by)
                    act_split(act, T, j % 2)
                for j in range(2):
                    act.wait_ge(gdn["qk_mm"].sem, gdn["qk_mm"].at(s, j))
                    for t in range(TT):
                        k = j * TT + t
                        if k:
                            act.wait_ge(gdn["sq"].sem, gdn["sq"].at(s, k - 1))
                        ins = act.activation(d_sqs, pair[j][:, col(t)], ACT.Square, accum_out=d_ss[:, k:k + 1])
                        ins.then_inc(gdn["sq"].sem, gdn["sq"].by)
                act.wait_ge(gdn["ss"].sem, gdn["ss"].at(s))
                act.activation(d_rs, d_ss, ACT.Sqrt).then_inc(gdn["std"].sem, gdn["std"].by)
                fill(0)
                fill(1)
                for j in range(2):
                    act.wait_ge(gdn["v_mm"].sem, gdn["v_mm"].at(s, j))
                    act.copy(d_vt[:, j], tiles5(pair[j])).then_inc(gdn["v"].sem, gdn["v"].by)
                for j in range(2):
                    act.wait_ge(gdn["kq_mm"].sem, gdn["kq_mm"].at(s, j))
                    act.copy(d_kq[:, 1 - j, :], pair[j]).then_inc(gdn["kq"].sem, gdn["kq"].by)
                fill(2)
                act.wait_ge(gdn["qkm_mm"].sem, gdn["qkm_mm"].at(s))
                act.copy(d_qk, pair[1]).then_inc(gdn["qkm"].sem, gdn["qkm"].by)
                for v in range(2):
                    act.wait_ge(gdn["dt_mm"].sem, gdn["dt_mm"].at(s, v))
                    for t in range(TT):
                        ins = act.activation(d_dt[:, unit(v, t), :], pair[v][:, col(t)], ACT.Exp,
                                             bias=num("ngc", t, v))
                    ins.then_inc(gdn["dt"].sem, gdn["dt"].by)
                fill(3)
                for lv, c, us, bank, n in chain_items():
                    if lv == 0:
                        continue
                    if c == 0 and lv <= 3:
                        fill(3 + lv)
                    act.wait_ge(gdn["p_mm"].sem, gdn["p_mm"].at(s, PX[lv, c]))
                    nn = (us.stop - us.start) * P
                    act.copy(d_P[:, us, :].rearrange("p u n -> p (u n)"), msc[:, bank, 0:nn]).then_inc(gdn["p"].sem, gdn["p"].by)
                fill(7)
                act.wait_ge(gdn["y_mm"].sem, gdn["y_mm"].at(s, PX[LEVELS - 1, 1]))
                act.wait_ge(gdn["u"].sem, gdn["u"].at(s, ML[LEVELS - 1, 1]))
                act.dma_start(d_sin, gdn_s[s]).then_inc(d_sld.sem, d_sld.by)
                for t in range(TT):
                    if t == PT:
                        act.wait_ge(gdn["f_mm"].sem, gdn["f_mm"].at(s))
                        for v in range(2):
                            act.copy(d_f[:, v], msc[:, v, 0:2 * P].rearrange("p (a n) -> p a n", a=2)).then_inc(gdn["f"].sem, gdn["f"].by)
                    act.wait_ge(gdn["ks_mm"].sem, gdn["ks_mm"].at(s, t))
                    if t == 0:
                        act.wait_ge(gdn["y_mm"].sem, gdn["y_mm"].at(s, PX[LEVELS - 1, 1]))
                    for v in range(2):
                        ins = act.activation(d_o[:, t, v, :], msc[:, 1, col(v)], ACT.Copy, scale=num("eg", t, v))
                    ins.then_inc(gdn["a"].sem, gdn["a"].by)
                    if t < 4:
                        fill(8 + t)
                    act.wait_ge(gdn["tw_mm"].sem, gdn["tw_mm"].at(s, t))
                    for v in range(2):
                        ins = act.activation(d_vn[:, v, :], msc[:, 2, col(v)], ACT.Copy, scale=num("beta", t, v))
                    ins.then_inc(gdn["vn"].sem, gdn["vn"].by)
                for t in range(TT):
                    for v in range(2):
                        k = 2 * t + v
                        act.wait_ge(gdn["o"].sem, gdn["o"].at(s, t))
                        if k:
                            act.wait_ge(gdn["osq"].sem, gdn["osq"].at(s, k - 1))
                        act.activation(d_sqs, d_o[:, t, v, :], ACT.Square, accum_out=d_os[:, k:k + 1])\
                           .then_inc(gdn["osq"].sem, gdn["osq"].by)
                act.wait_ge(gdn["oss"].sem, gdn["oss"].at(s))
                act.activation(d_ors, d_os, ACT.Sqrt).then_inc(gdn["ostd"].sem, gdn["ostd"].by)
                act.wait_ge(gdn["s_new"].sem, gdn["s_new"].at(s, 1))
                act.dma_start(gdn_s_out[s], d_sin).then_inc(d_sst.sem, d_sst.by)
                act.dma_start(gdn_p_out[s], d_s).then_inc(d_sst.sem, d_sst.by)
                act.wait_ge(d_sst.sem, d_sst.at(s, 1))
            for hf in range(2):
                gdn_loop(act, hf, body)
                act_projection(act, ("gdn", 0), proj_start(hf), stats=hf == 1)

        def dve_gdn(dve, occ):
            b = base["gdn", 0]

            def conv(T, par, tilenum, head, j, first=False):
                if not first:
                    dve.wait_ge(conv_act.sem, conv_act.at(tilenum - 1))
                seg = d_xp[:, XS0:XPW].rearrange("p (s n) -> p s n", s=STREAMS)
                old = hist[:, head, j * 24:(j + 1) * 24].rearrange("p (s n) -> p s n", s=STREAMS)
                dve.tensor_copy(seg[:, :, 0:HIST], old).then_inc(gdn["conv_h"].sem, gdn["conv_h"].by)
                dve.wait_ge(gdn["conv_h"].sem, gdn["conv_h"].at(tilenum))
                dve.wait_ge(evacuated[par].sem, evacuated[par].at(half(T)))
                for r in range(CONV):
                    tap = convw[:, head, j * CONV + r:j * CONV + r + 1]
                    src = d_xp[:, r:r + XPW - HIST]
                    dst = d_acc[:, 0:XPW - HIST]
                    if r == 0:
                        ins = dve.tensor_scalar(dst, src, tap, None, ALU.mult)
                    else:
                        dve.wait_ge(conv_step.sem, conv_step.at(tilenum, r - 1))
                        ins = dve.scalar_tensor_tensor(out=dst, in0=src, scalar=tap, in1=dst, op0=ALU.mult,
                                                       op1=ALU.add)
                    ins.then_inc(conv_step.sem, conv_step.by)
                new = newh[:, head, j * 27:(j + 1) * 27].rearrange("p (s n) -> p s n", s=STREAMS + 1)
                dve.tensor_copy(new[:, 0, :], d_xp[:, SEQ:SEQ + HIST])
                dve.tensor_copy(new[:, 1:, :], seg[:, :, SLEN:SLEN + HIST]).then_inc(conv_done.sem, conv_done.by)

            dve.wait_ge(d_param.sem, 4 * 16)
            dve.memset(d_xp[:, 0:HIST], 0.0).then_inc(gdn["zero"].sem, gdn["zero"].by)
            dve.wait_ge(gdn["zero"].sem, gdn["zero"].at(0))
            conv(b, 0, 0, 0, 0, first=True)
            dve.wait_ge(gdn["ab_mm"].sem, gdn["ab_mm"].at(0))
            ab = msc[:, 0, 0:TT * 32].rearrange("p (t n) -> p t n", t=TT)
            dtb = d_adt[:, 1, :].unsqueeze(1).broadcast_to([P, TT, GDN_VH])
            dve.tensor_tensor(d_y, ab[:, :, 0:GDN_VH], dtb, ALU.add).then_inc(gdn["gates"].sem, gdn["gates"].by)
            dve.tensor_copy(d_gq[:, 1], ab[:, :, GDN_VH:]).then_inc(gdn["gates"].sem, gdn["gates"].by)
            dve.wait_ge(gdn["gact"].sem, gdn["gact"].at(0, 2))
            dve.scalar_tensor_tensor(out=d_y, in0=d_y, scalar=0.0, in1=d_l, op0=ALU.max, op1=ALU.add)\
               .then_inc(gdn["gates"].sem, gdn["gates"].by)
            dve.wait_ge(gdn["gates"].sem, gdn["gates"].at(0, 2))
            dve.wait_ge(gdn["gact"].sem, gdn["gact"].at(0, 3))
            dve.tensor_tensor(d_y, d_y, d_adt[:, 0, :].unsqueeze(1).broadcast_to([P, TT, GDN_VH]), ALU.mult)\
               .then_inc(gdn["gates"].sem, gdn["gates"].by)
            dve.wait_ge(gdn["gates"].sem, gdn["gates"].at(0, 3))
            dve.tensor_scalar(d_gq[:, 0], d_y, -1.0, None, ALU.mult).then_inc(gdn["gates"].sem, gdn["gates"].by)
            dve.wait_ge(gdn["gact"].sem, gdn["gact"].at(0, 4))
            dve.tensor_scalar(d_gq[:, 1], d_gq[:, 1], 1.0, None, ALU.add).then_inc(gdn["gates"].sem, gdn["gates"].by)
            dve.wait_ge(gdn["gates"].sem, gdn["gates"].at(0, 5))
            dve.reciprocal(d_gq[:, 1], d_gq[:, 1]).then_inc(gdn["gates"].sem, gdn["gates"].by)
            conv(b + 1, 1, 1, 0, 1)
            conv(b + 2, 0, 2, 0, 2)
            dve.wait_ge(gdn["cum_mm"].sem, gdn["cum_mm"].at(0))
            cum = msc[:, 1, 0:TH].rearrange("p (t h) -> p t h", t=TT)
            glast = msc[:, 2, 0:TH].rearrange("p (t h) -> p t h", t=TT)
            dve.tensor_scalar(d_gq[:, 4], cum, -1.0, None, ALU.mult)
            dve.tensor_copy(d_glast, glast).then_inc(gdn["cum"].sem, gdn["cum"].by)
            dve.wait_ge(gdn["cum"].sem, gdn["cum"].at(0))
            dve.tensor_tensor(d_gq[:, 3], d_glast, cum, ALU.subtract).then_inc(gdn["copied"].sem, gdn["copied"].by)
            dve.wait_ge(gdn["cact"].sem, gdn["cact"].at(0, 2))
            dve.tensor_scalar(d_gq[:, 5], d_gq[:, 2], -1.0, None, ALU.mult).then_inc(gdn["neg"].sem, gdn["neg"].by)
            dve.wait_ge(gdn["neg"].sem, gdn["neg"].at(0))
            conv(b + 3, 1, 3, 0, 3)

            def body(hf, i, last=False):
                s = i + 4 * hf

                def fill(n):
                    j = n // 2
                    if n % 2 and j < 4 and not last:
                        conv(gdn_tile(hf, i, j, last), j % 2, s * 4 + (4 + j), s + 1, j)
                dve.tensor_copy(d_hegs, d_egs[:, :, bass.ds(s * 2, 2)])
                dve.tensor_copy(d_hq.rearrange("p a t h -> p (a t) h"),
                                       d_gq.rearrange("p a t h -> p (a t) h")[:, :, bass.ds(s * 2, 2)])\
                   .then_inc(gdn["hq"].sem, gdn["hq"].by)
                dve.wait_ge(gdn["sq"].sem, gdn["sq"].at(s, NU - 1))
                dve.tensor_scalar(d_ss, d_ss, L2_EPS, None, ALU.add).then_inc(gdn["ss"].sem, gdn["ss"].by)
                dve.wait_ge(gdn["std"].sem, gdn["std"].at(s))
                dve.reciprocal(d_rs, d_rs).then_inc(gdn["rs"].sem, gdn["rs"].by)
                dve.wait_ge(gdn["rs"].sem, gdn["rs"].at(s, 0))
                dve.tensor_scalar(d_rs[:, 0:TT], d_rs[:, 0:TT], float(P) ** -0.5, None, ALU.mult)\
                   .then_inc(gdn["rs"].sem, gdn["rs"].by)
                dve.wait_ge(gdn["rs"].sem, gdn["rs"].at(s, 1))
                dve.tensor_tensor(d_qt, tiles5(pair[0]), bc(d_rs[:, 0:TT], P), ALU.mult).then_inc(gdn["qt"].sem, gdn["qt"].by)
                dve.tensor_tensor(d_kt, tiles5(pair[1]), bc(d_rs[:, TT:NU], P), ALU.mult).then_inc(gdn["kt"].sem, gdn["kt"].by)
                dve.wait_ge(gdn["hq"].sem, gdn["hq"].at(s))
                fill(0)
                fill(1)
                fill(2)
                dve.wait_ge(gdn["kk_mm"].sem, gdn["kk_mm"].at(s))
                dve.tensor_copy(d_kk, pair[0]).then_inc(gdn["kk"].sem, gdn["kk"].by)
                dve.wait_ge(gdn["kk"].sem, gdn["kk"].at(s))
                dve.wait_ge(gdn["qkm"].sem, gdn["qkm"].at(s))
                kk5, qk5 = tiles5(d_kk), tiles5(d_qk)
                for v in range(2):
                    pu, su = slice(4 * v, 4 * v + 4), 8 + v
                    dve.wait_ge(gdn["dt"].sem, gdn["dt"].at(s, v))
                    dve.tensor_tensor(d_at[:, pu, :], d_dt[:, pu, :], qk5[:, 0:PT, :], ALU.mult)
                    dve.tensor_tensor(d_at[:, su, :], d_dt[:, su, :], qk5[:, PT, :], ALU.mult).then_inc(gdn["att"].sem, gdn["att"].by)
                    dve.tensor_tensor(d_M[:, pu, :], d_dt[:, pu, :], kk5[:, 0:PT, :], ALU.mult)
                    dve.tensor_tensor(d_M[:, su, :], d_dt[:, su, :], kk5[:, PT, :], ALU.mult).then_inc(gdn["m0"].sem, gdn["m0"].by)
                    dve.wait_ge(gdn["m0"].sem, gdn["m0"].at(s, v))
                    beta = d_hq[:, 1, :, v]
                    dve.tensor_tensor(d_M[:, pu, :], d_M[:, pu, :], bc(beta[:, 0:PT], P), ALU.mult)
                    dve.tensor_scalar(d_M[:, su, :], d_M[:, su, :], num("beta", PT, v), None, ALU.mult)\
                       .then_inc(gdn["m"].sem, gdn["m"].by)
                fill(3)
                for lv, c, us, bank, n in chain_items():
                    nu = us.stop - us.start
                    units = d_M[:, us, :]

                    def mask(level, c=c, us=us, nu=nu):
                        m = const(C_MASK + level * P).unsqueeze(1).broadcast_to([P, nu, P])
                        dve.tensor_tensor(d_Ml[:, us, :], d_M[:, us, :], m, ALU.mult).then_inc(gdn["ml"].sem, gdn["ml"].by)
                    if lv == 0:
                        dve.wait_ge(gdn["m"].sem, gdn["m"].at(s, 1 if c else 0))
                    else:
                        if lv == 1:
                            dve.wait_ge(gdn["u"].sem, gdn["u"].at(s, ML[0, c]))
                            dve.wait_ge(gdn["tr_mm"].sem, gdn["tr_mm"].at(s, c))
                        else:
                            dve.wait_ge(gdn["p_mm"].sem, gdn["p_mm"].at(s, PX[lv - 1, c]))
                    mask(lv)
                    if c == 0 and 1 <= lv <= 3:
                        fill(3 + lv)
                    out0 = msc[:, bank, 0:nu * P].rearrange("p (u n) -> p u n", n=P)
                    out1 = msc[:, bank + 1, 0:nu * P].rearrange("p (u n) -> p u n", n=P)
                    eye = ident.unsqueeze(1).broadcast_to([P, nu, P])
                    if lv == 0:
                        dve.wait_ge(gdn["ml"].sem, gdn["ml"].at(s, ML[lv, c]))
                        dve.tensor_tensor(d_U[:, us, :], eye, d_Ml[:, us, :], ALU.subtract).then_inc(gdn["u"].sem, gdn["u"].by)
                        dve.wait_ge(gdn["tr_mm"].sem, gdn["tr_mm"].at(s, c))
                        dve.tensor_tensor(d_T[:, us, :], eye, out0, ALU.subtract).then_inc(gdn["t"].sem, gdn["t"].by)
                        continue
                    if (lv, c) in XX:
                        dve.wait_ge(gdn["x_mm"].sem, gdn["x_mm"].at(s, XX[lv, c]))
                        dve.tensor_tensor(d_T[:, us, :], d_T[:, us, :], out1, ALU.subtract).then_inc(gdn["t"].sem, gdn["t"].by)
                    dve.wait_ge(gdn["y_mm"].sem, gdn["y_mm"].at(s, PX[lv, c]))
                    dve.tensor_tensor(d_U[:, us, :], d_U[:, us, :], out0, ALU.subtract).then_inc(gdn["u"].sem, gdn["u"].by)
                fill(7)
                dve.memset(d_s, 0.0).then_inc(gdn["s_zero"].sem, gdn["s_zero"].by)
                for t in range(TT):
                    dve.wait_ge(gdn["kt"].sem, gdn["kt"].at(s))
                    if 1 <= t < PT + 1:
                        dve.wait_ge(gdn["su_mm"].sem, gdn["su_mm"].at(s, t - 1))
                    if t == 0:
                        dve.wait_ge(gdn["y_mm"].sem, gdn["y_mm"].at(s, PX[LEVELS - 1, 1]))
                    for v in range(2):
                        ins = dve.tensor_scalar(d_ke[:, v, :], d_kt[:, t, :], num("ke", t, v), None, ALU.mult)
                    ins.then_inc(gdn["ke"].sem, gdn["ke"].by)
                    dve.wait_ge(gdn["ks_mm"].sem, gdn["ks_mm"].at(s, t))
                    for v in range(2):
                        ins = dve.scalar_tensor_tensor(out=d_w[:, v, :], in0=msc[:, 0, col(v)],
                                                       scalar=num("neg_eg", t, v), in1=d_vt[:, v, t, :],
                                                       op0=ALU.mult, op1=ALU.add)
                    ins.then_inc(gdn["w"].sem, gdn["w"].by)
                    dve.wait_ge(gdn["o_mm"].sem, gdn["o_mm"].at(s, t))
                    dve.wait_ge(gdn["a"].sem, gdn["a"].at(s, t))
                    dve.tensor_tensor(d_o[:, t], d_o[:, t],
                                             msc[:, 3, 0:2 * P].rearrange("p (v n) -> p v n", v=2), ALU.add)\
                       .then_inc(gdn["o"].sem, gdn["o"].by)
                    if t < PT:
                        dve.wait_ge(gdn["su_mm"].sem, gdn["su_mm"].at(s, t))
                        if t == 0:
                            dve.wait_ge(gdn["s_zero"].sem, gdn["s_zero"].at(s))
                        else:
                            dve.wait_ge(gdn["state"].sem, gdn["state"].at(s, t - 1))
                        for v in range(2):
                            ins = dve.scalar_tensor_tensor(out=d_s[:, v, :], in0=d_s[:, v, :],
                                                           scalar=num("egl", t, v), in1=msc[:, 0, col(v)],
                                                           op0=ALU.mult, op1=ALU.add)
                        ins.then_inc(gdn["state"].sem, gdn["state"].by)
                for v in range(2):
                    if v:
                        dve.wait_ge(gdn["ssu_mm"].sem, gdn["ssu_mm"].at(s, 0))
                    src = d_vn[:, v, :].unsqueeze(1).broadcast_to([P, STREAMS, P])
                    dve.tensor_tensor(d_vx, src, bc(cs[:, C_M8:C_M8 + STREAMS], P), ALU.mult).then_inc(gdn["vx"].sem, gdn["vx"].by)
                    dve.tensor_tensor(d_sin[:, v], d_sin[:, v], bc(d_hegs[:, :, v], P), ALU.mult)\
                       .then_inc(gdn["s_dec"].sem, gdn["s_dec"].by)
                    dve.wait_ge(gdn["ssu_mm"].sem, gdn["ssu_mm"].at(s, v))
                    dve.wait_ge(gdn["s_dec"].sem, gdn["s_dec"].at(s, v))
                    dve.tensor_tensor(d_sin[:, v], d_sin[:, v],
                                             msc[:, 0:2, :].rearrange("p b (s n) -> p (b s) n", n=P), ALU.add)\
                       .then_inc(gdn["s_new"].sem, gdn["s_new"].by)
                dve.wait_ge(gdn["osq"].sem, gdn["osq"].at(s, NU - 1))
                dve.tensor_scalar(d_os, d_os, 1.0 / P, RMS_EPS, ALU.mult, ALU.add).then_inc(gdn["oss"].sem, gdn["oss"].by)
                dve.wait_ge(gdn["ostd"].sem, gdn["ostd"].at(s))
                dve.reciprocal(d_ors, d_ors).then_inc(gdn["ors"].sem, gdn["ors"].by)
                dve.wait_ge(gdn["ors"].sem, gdn["ors"].at(s))
                flat_o = d_o.rearrange("p t v n -> p (t v) n")
                dve.tensor_tensor(flat_o, flat_o, bc(d_ors, P), ALU.mult).then_inc(gdn["on"].sem, gdn["on"].by)
                dve.wait_ge(gdn["og_mm"].sem, gdn["og_mm"].at(s, 1))
                for v in range(2):
                    dve.wait_ge(evacuated[v].sem, evacuated[v].at(half(gdn_tile(hf, i, 4 + v, last))))
                    dve.scalar_tensor_tensor(out=d_og[v], in0=pair[v], scalar=nrm[:, 2:3], in1=d_z[v],
                                                    op0=ALU.mult, op1=ALU.mult)\
                       .then_inc(gdn["og"].sem, gdn["og"].by)
                    split_hidden(dve, d_og[v], i, v, s, gdn)
            for hf in range(2):
                gdn_loop(dve, hf, body)
                dve_down(dve, ("gdn", 0), proj_start(hf), ALPHA if hf == 0 else 1.0, stats=hf == 1)
        PE_OF = {"ffn": pe_ffn, "gla": pe_gla, "gdn": pe_gdn}
        ACT_OF = {"ffn": act_ffn, "gla": act_gla, "gdn": act_gdn}
        DVE_OF = {"ffn": dve_ffn, "gla": dve_gla, "gdn": dve_gdn}
        y_stored = Signal("y_stored", by=16)
        block = ctx.enter_context(nc.Block())

        @block.sync
        def _(sp):
            load_params(sp)
            for dst, src in ((a_w1, w_a1), (a_w2[0:RANK, :], w_a2), (a_b[0:1, :], b_a)):
                sp.dma_start(dst, src).then_inc(a_param.sem, a_param.by)
            for dst, src in ((d_wab, w_ab), (d_adt, a_dt.broadcast_to([P, 2, GDN_VH])),
                             (convw[:], conv_w), (hist[:], hist_in)):
                sp.dma_start(dst, src).then_inc(d_param.sem, d_param.by)
            sp_supply(sp)
            sp.wait_ge(x_ready.sem, x_ready.at(LN_OF[PLAN[-1]], KT - 1))
            sp.dma_start(y_out, x[:]).then_inc(y_stored.sem, y_stored.by)
            sp.wait_ge(conv_done.sem, conv_done.at(4 * GDN_KH - 1))
            sp.dma_start(hist_out, newh[:]).then_inc(hist_stored.sem, hist_stored.by)
            sp.wait_ge(y_stored.sem, y_stored.at(0))
            sp.wait_ge(hist_stored.sem, hist_stored.at(0))

        @block.gpsimd
        def _(pool):
            pool_supply(pool)

        @block.scalar
        def _(act):
            act_split(act, -2, 0)
            act_split(act, -1, 1)
            for kind, occ in PLAN:
                ACT_OF[kind](act, occ)
                act_ln(act, (kind, occ))

        @block.vector
        def _(dve):
            dve.wait_ge(inputs_loaded.sem, 16 * N_IN)
            for k in range(KT):
                dve.tensor_copy(xh[:, k, :], x[:, k, :]).then_inc(start_split.sem, start_split.by)
            for k in range(KT):
                dve.wait_ge(start_split.sem, start_split.at(0, k))
                dve.tensor_tensor(xl[:, k, :], x[:, k, :], xh[:, k, :].bitcast(F32), ALU.subtract)\
                   .then_inc(start_split.sem, start_split.by)
            for kind, occ in PLAN:
                DVE_OF[kind](dve, occ)
                dve_ln(dve, (kind, occ))

        @block.tensor
        def _(pe):
            for kind, occ in PLAN:
                PE_OF[kind](pe, occ)
                pe_ln(pe, (kind, occ))


def chunk(w):
    k = w.shape[0] // P
    out = np.zeros((P, KT, P), w.dtype)
    out[:, :k] = w.reshape(k, P, P).transpose(1, 0, 2)
    return out.reshape(P, D)


def lay_weights(ins):
    out = np.zeros((N_CHUNKS, P, D), np.float32)
    n = 0

    def put(w, row, col, rows=D):
        nonlocal n
        out[n] = chunk(w[row:row + rows, col:col + P])
        n += 1

    def put_head(w, first, gates):
        for c in first:
            put(w, 0, c)
        for c in gates:
            put(w, 0, c)

    for kind, occ in PLAN:
        if kind == "ffn":
            name, layer = f"ffn{occ % 2 + 1}", occ // 2
            gu, dn, f0 = ins[name + "_w_gu"][layer], ins[name + "_w_d"][layer], 0
            for g in GROUPS:
                for f in range(f0, f0 + g):
                    put(gu, 0, f * P)
                    put(gu, 0, D_FF + f * P)
                for m in range(KT):
                    put(dn, f0 * P, m * P, g * P)
                f0 += g
        elif kind == "gla":
            w, wo = ins["gla_w_in"][0], ins["gla_w_o"][0]
            qkv = [(h * P, 512 + h * P, 1024 + 2 * h * P, 1024 + (2 * h + 1) * P) for h in range(GLA_HEADS)]
            put_head(w, qkv[0], ())
            for h in range(GLA_HEADS):
                put_head(w, (2048 + 2 * h * P, 2048 + (2 * h + 1) * P), qkv[h + 1] if h + 1 < GLA_HEADS else ())
            for m in range(KT):
                put(wo, 0, m * P)
        else:
            w, wo = ins["gdn_w_in"][0], ins["gdn_w_o"][0]
            qkv = [(h * P, 1024 + h * P, 2048 + 2 * h * P, 2048 + (2 * h + 1) * P) for h in range(GDN_KH)]
            put_head(w, qkv[0], ())
            for h in range(GDN_KH):
                put_head(w, qkv[h + 1] if h + 1 < GDN_KH else (), (4096 + 2 * h * P, 4096 + (2 * h + 1) * P))
                if h % 4 == 3:
                    for m in range(KT):
                        put(wo, (h // 4) * D, m * P)
    assert n == N_CHUNKS
    return out


def columns(a, n):
    return np.ascontiguousarray(np.moveaxis(a.reshape(a.shape[:-1] + (n, P)), -1, 0))


def kernel(**ins):
    import concourse.bacc as _bacc
    from concourse.bass_utils import run_bass_kernel_spmd as _run

    ins = {k: np.asarray(v) for k, v in ins.items()}
    tokens = np.concatenate([ins["x_prompt"].reshape(SEQ, D), ins["x_sample"].reshape(TOK - SEQ, D)], 0)
    ab = ins["gdn_w_in"][0][:, 6144:6176]
    conv = columns(ins["gdn_conv_w"][0], 32)
    hist = columns(ins["state_gdn_conv"][:, 0], 32)
    by_head = [[h, 8 + h, 16 + 2 * h, 17 + 2 * h] for h in range(GDN_KH)]
    norm = np.zeros((P, 4), np.float32)
    norm[:, 0:2] = columns(ins["gla_norm_g"][0], 2)
    norm[:, 2] = ins["gdn_norm_g"][0]
    arrays = {
        "wstream": lay_weights(ins),
        "x_in": columns(tokens, KT).transpose(0, 2, 1),
        "consts": constants(),
        "ln_cols": np.stack([columns(ins["ln_g"].reshape(6, D), KT), columns(ins["ln_b"].reshape(6, D), KT)], 2),
        "w_a1": ins["gla_w_a1"][0].reshape(KT, P, RANK).transpose(1, 0, 2),
        "w_a2": ins["gla_w_a2"][0],
        "b_a": ins["gla_b_a"],
        "norm_cols": norm,
        "w_ab": ab.reshape(KT, P, 32).transpose(1, 0, 2),
        "a_dt": np.stack([ins["gdn_a_log"], ins["gdn_dt_bias"]], 1),
        "conv_w": conv.transpose(0, 2, 1)[:, by_head].reshape(P, GDN_KH, 16),
        "hist_in": hist.transpose(0, 3, 1, 2)[:, by_head].reshape(P, GDN_KH, 96),
        "gla_s": ins["state_gla"][:, 0].transpose(1, 2, 0, 3),
        "gdn_s": ins["state_gdn"][:, 0].reshape(STREAMS, GDN_KH, 2, P, P).transpose(1, 3, 2, 0, 4),
    }
    outs = {
        "y_out": (P, KT, TOK), "gla_p_out": (4, P, 256), "gdn_p_out": (GDN_KH, P, 2, P),
        "hist_out": (P, GDN_KH, 108), "gla_s_out": (4, P, 8, 256), "gdn_s_out": (GDN_KH, P, 2, STREAMS, P),
    }
    arrays = {k: np.ascontiguousarray(v) for k, v in arrays.items()}
    nc = _bacc.Bacc("TRN2", target_bir_lowering=False, num_devices=1)
    args = [nc.dram_tensor(k, v.shape, mybir.dt.from_np(v.dtype), kind="ExternalInput").ap()
            for k, v in arrays.items()]
    args += [nc.dram_tensor(k, s, F32, kind="ExternalOutput").ap() for k, s in outs.items()]
    build(nc, *args)
    r = _run(nc, [arrays], core_ids=[0]).results[0]
    y = r["y_out"].transpose(2, 1, 0).reshape(TOK, D)
    flat = [c for head in by_head for c in head]
    hist_rows = np.empty((32, P, 9, 3), np.float32)
    hist_rows[flat] = r["hist_out"].reshape(P, 32, 9, 3).transpose(1, 0, 2, 3)
    hist_rows = hist_rows.transpose(2, 3, 0, 1).reshape(9, 1, 3, 32 * P)
    return (y[:SEQ].reshape(1, SEQ, D), y[SEQ:].reshape(STREAMS, SLEN, D),
            r["gla_p_out"].reshape(1, 1, 4, P, 256), r["gdn_p_out"].transpose(0, 2, 1, 3).reshape(1, 1, 16, P, P), hist_rows[0:1],
            r["gla_s_out"].transpose(2, 0, 1, 3)[:, None], r["gdn_s_out"].transpose(3, 0, 2, 1, 4).reshape(STREAMS, 1, 16, P, P),
            hist_rows[1:9])
```

```python
from contextlib import ExitStack

import numpy as np

import concourse.bass as bass
from concourse import mybir

F32 = mybir.dt.float32
F32R = mybir.dt.float32r
U32 = mybir.dt.uint32
ALU = mybir.AluOpType
ACT = mybir.ActivationFunctionType

P = 128
D = 1024
KT = D // P
SEQ = 512
STREAMS, SLEN = 8, 16
TOK = SEQ + STREAMS * SLEN
TT = TOK // P
HALF = TOK // 2
PT = SEQ // P
DEPTH = 2
D_FF = 2816
FT = D_FF // P
GROUPS = (8, 7, 7)
N_FFN = 2 * DEPTH
GLA_HEADS = 4
GLA_CHUNK = 64
NCK = SEQ // GLA_CHUNK
GATE_TAU = 16.0
RANK = 16
GDN_KH = 8
GDN_VH = 16
CONV = 4
HIST = CONV - 1
XPW = HIST + SEQ + STREAMS * (HIST + SLEN)
XS0 = HIST + SEQ
LEVELS = 7
STREAM_LEVELS = 4
LN_EPS, RMS_EPS, L2_EPS = 1e-5, 1e-6, 1e-6
ALPHA = (2.0 * DEPTH) ** 0.25
NEG = -1.0e30

PLAN = [("ffn", 0), ("gla", 0), ("ffn", 1), ("ffn", 2), ("gdn", 0), ("ffn", 3)]

CH_FFN = 2 * FT + len(GROUPS) * KT
CH_GLA = GLA_HEADS * 6 + KT
CH_GDN = 2 * (GDN_KH // 2 * 6 + KT)
N_CHUNKS = sum({"ffn": CH_FFN, "gla": CH_GLA, "gdn": CH_GDN}[kind] for kind, _ in PLAN)

C_ID, C_ONES, C_L128, C_L64, C_L16, C_NEG128, C_NEG16, C_BO16 = (P * i for i in range(8))
C_MASK = 8 * P
C_M8 = C_MASK + LEVELS * P
C_MEAN = C_M8 + STREAMS
N_CONST = C_MEAN + 8


def constants():
    t = np.arange(P)
    row, col = t[:, None], t[None, :]
    out = np.zeros((P, N_CONST), np.float32)
    out[:, C_ID:C_ID + P] = row == col
    out[:, C_ONES:C_ONES + P] = 1.0
    for at, n in ((C_L128, P), (C_L64, GLA_CHUNK), (C_L16, SLEN)):
        out[:, at:at + P] = (row <= col) & (row // n == col // n)
    out[:, C_NEG128:C_NEG128 + P] = np.where(out[:, C_L128:C_L128 + P] > 0, 0.0, NEG)
    out[:, C_NEG16:C_NEG16 + P] = np.where(out[:, C_L16:C_L16 + P] > 0, 0.0, NEG)
    out[:, C_BO16:C_BO16 + P] = row // SLEN == col // SLEN
    for lv in range(LEVELS):
        s = 2 ** lv
        lower = (row // (2 * s) == col // (2 * s)) & ((row // s) % 2 == 1) & ((col // s) % 2 == 0)
        out[:, C_MASK + lv * P:C_MASK + (lv + 1) * P] = lower if lv else lower.T
    out[:, C_M8:C_M8 + STREAMS] = row // SLEN == np.arange(STREAMS)[None, :]
    out[:, C_MEAN] = 1.0 / D
    return out




def build(nc, wstream, x_in, consts, ln_cols, w_a1, w_a2, b_a, norm_cols, w_ab, a_dt, conv_w, hist_in,
          gla_s, gdn_s, y_out, gla_p_out, gdn_p_out, hist_out, gla_s_out, gdn_s_out):
    with ExitStack() as ctx:
        def sb(name, shape, dt=F32):
            return ctx.enter_context(nc.sbuf_tensor(name, shape, dt))

        x = sb("x", [P, KT, TOK])
        xh = sb("xh", [P, KT, TOK], F32R)
        xl = sb("xl", [P, KT, TOK], F32R)
        hh = sb("hh", [P, 8, TOK], F32R)
        hl = sb("hl", [P, 8, TOK], F32R)
        raw = sb("raw", [P, 2, D])
        wh = sb("wh", [P, 2, D], F32R)
        wl = sb("wl", [P, 2, D], F32R)
        cs = sb("cs", [P, N_CONST])
        lnc = sb("lnc", [P, DEPTH * 3, 2, KT])
        nrm = sb("nrm", [P, 4])
        small = sb("small", [P, 192])
        gq = sb("gq", [P, 896])
        convw = sb("convw", [P, GDN_KH, 4 * CONV])
        hist = sb("hist", [P, GDN_KH, 4 * STREAMS * HIST])
        newh = sb("newh", [P, GDN_KH, 4 * (STREAMS + 1) * HIST])
        work = sb("work", [P, 16384])
        gem = ctx.enter_context(nc.psum_tensor("gem", [P, 2, 2, 512], F32))
        msc = ctx.enter_context(nc.psum_tensor("msc", [P, 4, 512], F32))

        def view(at, *shape):
            n = int(np.prod(shape))
            v = work[:, at:at + n]
            if len(shape) == 1:
                return v
            names = "abcd"[:len(shape)]
            return v.rearrange(f"p ({' '.join(names)}) -> p {' '.join(names)}",
                               **{k: s for k, s in zip(names[1:], shape[1:])})

        def const(at, n=P):
            return cs[:, at:at + n]

        ident, ones = const(C_ID), const(C_ONES)

        def over_tiles(m, n):
            return m.unsqueeze(1).broadcast_to([P, n, P])

        class Signal:

            def __init__(self, name, per=1, by=1, before=0):
                self.sem = ctx.enter_context(nc.semaphore(name))
                self.per, self.by = per, by
                self.before = before

            def at(self, step, j=0):
                return (number(step) * self.per + (j + 1 + self.before)) * self.by

        class Tile:

            def __init__(self, b, per, i, j):
                self.n = i * per + (b + j)
                self.half = i * (per // 2) + (b + j) // 2

        def tile(b, per, i, j):
            return b + per * i + j if isinstance(i, int) else Tile(b, per, i, j)

        def number(T):
            return T.n if isinstance(T, Tile) else T

        def half(T):
            return T // 2 if isinstance(T, int) else T.half

        loaded = [Signal("chunk_loaded_even", by=16), Signal("chunk_loaded_odd", by=16)]
        hi_ready = Signal("chunk_hi_ready")
        lo_ready = Signal("chunk_lo_ready")
        tile_done = Signal("tile_done")
        evacuated = [Signal("even_tile_evacuated"), Signal("odd_tile_evacuated")]

        inputs_loaded = Signal("inputs_loaded", by=16)
        start_split = Signal("start_split")

        base, first_tile = {}, 0
        for kind, occ in PLAN:
            base[kind, occ] = first_tile
            first_tile += {"ffn": CH_FFN, "gla": CH_GLA, "gdn": CH_GDN}[kind]
        LN_OF = {("ffn", 0): 0, ("gla", 0): 1, ("ffn", 1): 2, ("ffn", 2): 3, ("gdn", 0): 4, ("ffn", 3): 5}

        x_loaded = [Signal("x_first_half_loaded", by=16), Signal("x_second_half_loaded", by=16)]

        def load_start(sp):
            for h in range(2):
                sp.dma_start(raw[:, h, :], wstream[h]).then_inc(loaded[h].sem, loaded[h].by)
                ks = slice(h * KT // 2, (h + 1) * KT // 2)
                sp.dma_start(x[:, ks, :], x_in[:, ks, :]).then_inc(x_loaded[h].sem, x_loaded[h].by)
            for dst, src in ((cs[:], consts), (lnc[:], ln_cols), (nrm[:], norm_cols)):
                sp.dma_start(dst, src).then_inc(inputs_loaded.sem, inputs_loaded.by)
        N_IN = 3

        def pe_tile(pe, T, par, kts, rh, rl, before=None):
            if not (isinstance(T, int) and T < 2):
                pe.wait_ge(evacuated[par].sem, evacuated[par].at(half(T) - 1))
            pe.wait_ge(lo_ready.sem, lo_ready.at(T))
            for k in range(kts):
                if before:
                    before(k)
                w_hi, w_lo = wh[:, par, k * P:(k + 1) * P], wl[:, par, k * P:(k + 1) * P]
                for n, (w, r) in enumerate(((w_hi, rh), (w_hi, rl), (w_lo, rh))):
                    for s in range(2):
                        mm = pe.matmul(gem[:, par, s, 0:HALF], w, r[:, k, s * HALF:(s + 1) * HALF],
                                       start=(k == 0 and n == 0), stop=(k == kts - 1 and n == 2))
            mm.then_inc(tile_done.sem, tile_done.by)

        def slot(par):
            return gem[:, par, :, 0:HALF]

        def halves(ap):
            return ap.rearrange("p (s n) -> p s n", s=2)

        def act_split(act, T, par):
            if isinstance(T, int) and T + 2 >= N_CHUNKS:
                return
            nxt = half(T) + 1
            act.wait_ge(loaded[par].sem, loaded[par].at(nxt))
            if not (isinstance(T, int) and T < 0):
                act.wait_ge(tile_done.sem, tile_done.at(T))
            act.copy(wh[:, par, :], raw[:, par, :]).then_inc(hi_ready.sem, hi_ready.by)

        def loop(eng, n, body, peel_first=False, peel_last=False):
            lo, hi = 0, n
            if peel_first:
                body(0)
                lo = 1
            if peel_last:
                hi = n - 1
            if hi - lo == 1:
                body(lo)
            elif hi > lo:
                with eng.Fori(lo, hi) as i:
                    body(i)
            if peel_last:
                body(n - 1)

        def sp_supply(sp):
            with sp.Fori(1, N_CHUNKS // 2) as i:
                for par in range(2):
                    T = tile(0, 2, i, par)
                    sp.wait_ge(lo_ready.sem, lo_ready.at(T) - 2)
                    sp.dma_start(raw[:, par, :], wstream[number(T)]).then_inc(loaded[par].sem, loaded[par].by)

        def pool_supply(pool, first, end):
            def body(i):
                for par in range(2):
                    T = tile(first, 2, i, par)
                    pool.wait_ge(hi_ready.sem, hi_ready.at(T))
                    pool.tensor_tensor(wl[:, par, :], raw[:, par, :], wh[:, par, :].bitcast(F32),
                                              ALU.subtract)\
                       .then_inc(lo_ready.sem, lo_ready.by)
            loop(pool, (end - first) // 2, body)

        gate = view(0, TOK)
        hid = view(TOK, TOK)
        zsum, zsqs, zsq = view(2 * TOK, TOK), view(3 * TOK, TOK), view(4 * TOK, TOK)
        hid_hi = Signal("hidden_hi_ready")
        hid_lo = Signal("hidden_lo_ready")

        def ffn_parts(occ):
            b, f0 = base["ffn", occ], 0
            for g, n in enumerate(GROUPS):
                yield g, n, occ * FT + f0, b, b + 2 * n
                b += 2 * n + KT
                f0 += n

        def pe_ffn(pe, occ):
            for g, n, f0, b_up, b_down in ffn_parts(occ):
                def up(i):
                    if g == 0 and isinstance(i, int) and i == 0:
                        return pe_first_pair(pe, "ffn", occ)
                    for par in range(2):
                        pe_tile(pe, tile(b_up, 2, i, par), par, KT, xh, xl)
                loop(pe, n, up, peel_first=g == 0)

                def down(i):
                    for par in range(2):
                        def need(k):
                            if k == 0:
                                pe.wait_ge(hid_lo.sem, hid_lo.at(f0 + n - 2))
                            if k == n - 1:
                                pe.wait_ge(hid_lo.sem, hid_lo.at(f0 + n - 1))
                        pe_tile(pe, tile(b_down, 2, i, par), par, n, hh, hl, before=need)
                loop(pe, KT // 2, down)

        def act_ffn(act, occ):
            for g, n, f0, b_up, b_down in ffn_parts(occ):
                def up(i):
                    T = tile(b_up, 2, i, 0)
                    act.wait_ge(tile_done.sem, tile_done.at(T))
                    act_split(act, T, 0)
                    if not (isinstance(T, int) and T < 2):
                        act.wait_ge(evacuated[1].sem, evacuated[1].at(half(T) - 1))
                    act.activation(halves(gate), slot(0), ACT.Silu).then_inc(evacuated[0].sem, evacuated[0].by)
                    act_split(act, tile(b_up, 2, i, 1), 1)
                loop(act, n, up, peel_first=(occ == 0 and g == 0))
                last = g == len(GROUPS) - 1

                def down(i):
                    for par in range(2):
                        T = tile(b_down, 2, i, par)
                        act_split(act, T, par)
                        if last:
                            act_square(act, ("ffn", occ), T, par, i)
                loop(act, KT // 2, down, peel_first=last, peel_last=(b_down + KT == N_CHUNKS))

        def dve_ffn(dve, occ):
            for g, n, f0, b_up, b_down in ffn_parts(occ):
                def up(i):
                    T = tile(b_up, 2, i, 1)
                    dve.wait_ge(evacuated[0].sem, evacuated[0].at(half(T)))
                    dve.wait_ge(tile_done.sem, tile_done.at(T))
                    if not (isinstance(i, int) and f0 + i < 1):
                        dve.wait_ge(hid_lo.sem, hid_lo.at(f0 + i - 1))
                    dve.tensor_tensor(halves(hid), halves(gate), slot(1), ALU.mult)\
                       .then_inc(evacuated[1].sem, 1)
                    dve.wait_ge(evacuated[1].sem, evacuated[1].at(half(T)))
                    dve.tensor_copy(hh[:, i, :], hid).then_inc(hid_hi.sem, 1)
                    dve.wait_ge(hid_hi.sem, hid_hi.at(f0 + i))
                    dve.tensor_tensor(hl[:, i, :], hid, hh[:, i, :].bitcast(F32), ALU.subtract)\
                       .then_inc(hid_lo.sem, 1)
                loop(dve, n, up, peel_first=(occ == 0 and g == 0))
                dve_down(dve, ("ffn", occ), b_down, 2.0 * ALPHA if g == 0 else 1.0,
                         stats=g == len(GROUPS) - 1)

        sq_ready = Signal("z_square_ready")
        sum_ready = Signal("z_sums_ready", per=2)

        def act_square(act, ph, T, par, i):
            k = i * 2 + (KT * LN_OF[ph] + par)
            act.wait_ge(evacuated[par].sem, evacuated[par].at(half(T)))
            if not (isinstance(k, int) and k < 1):
                act.wait_ge(sum_ready.sem, sum_ready.at(k - 1, 1))
            act.activation(zsq, x[:, i * 2 + par, :], ACT.Square).then_inc(sq_ready.sem, sq_ready.by)

        def dve_down(dve, ph, b_down, scale, stats):
            def body(i):
                for par in range(2):
                    T = tile(b_down, 2, i, par)
                    xt = x[:, i * 2 + par, :]
                    dve.wait_ge(tile_done.sem, tile_done.at(T))
                    dve.scalar_tensor_tensor(out=halves(xt), in0=halves(xt), scalar=scale, in1=slot(par),
                                             op0=ALU.mult, op1=ALU.add).then_inc(evacuated[par].sem, 1)
                    if not stats:
                        continue
                    k = i * 2 + (KT * LN_OF[ph] + par)
                    dve.wait_ge(evacuated[par].sem, evacuated[par].at(half(T)))
                    if isinstance(i, int) and i * 2 + par == 0:
                        dve.tensor_copy(zsum, xt).then_inc(sum_ready.sem, sum_ready.by)
                        dve.wait_ge(sq_ready.sem, sq_ready.at(k))
                        dve.tensor_copy(zsqs, zsq).then_inc(sum_ready.sem, sum_ready.by)
                    else:
                        dve.wait_ge(sum_ready.sem, sum_ready.at(k - 1, 1))
                        dve.tensor_tensor(zsum, zsum, xt, ALU.add).then_inc(sum_ready.sem, sum_ready.by)
                        dve.wait_ge(sq_ready.sem, sq_ready.at(k))
                        dve.tensor_tensor(zsqs, zsqs, zsq, ALU.add).then_inc(sum_ready.sem, sum_ready.by)
            loop(dve, KT // 2, body, peel_first=stats)

        st = small[:, 0:16].rearrange("p (a t) -> p a t", a=2)
        rstd, nmr, tmp5 = small[:, 16:21], small[:, 24:29], small[:, 32:37]
        diag_r, diag_n = view(2 * TOK, TT, P), view(3 * TOK, TT, P)
        norm_a, norm_b = view(5 * TOK, 2, TOK), view(7 * TOK, 2, TOK)
        stat_mm = Signal("ln_stats_multiplied")
        stat_step = Signal("ln_stats_step", per=6)
        std_ready = Signal("ln_std_ready")
        diag_ready = Signal("ln_diag_ready", per=2)
        bc_ready = Signal("ln_broadcast_ready", per=2)
        scaled = Signal("ln_tile_scaled", per=KT)
        shifted = Signal("ln_tile_shifted", per=KT)
        x_ready = Signal("x_tile_ready", per=KT)
        xh_ready = Signal("x_hi_ready", per=KT)
        xl_ready = Signal("x_lo_ready", per=KT)

        def pe_ln(pe, ph):
            L = LN_OF[ph]
            for a, src in ((0, zsum), (1, zsqs)):
                pe.wait_ge(sum_ready.sem, sum_ready.at(KT * L + KT - 1, a))
                for t in range(TT):
                    mm = pe.matmul(msc[:, 0, a * 8 + t:a * 8 + t + 1], src[:, t * P:(t + 1) * P],
                                   cs[:, C_MEAN:C_MEAN + 1], start=True, stop=True)
            mm.then_inc(stat_mm.sem, stat_mm.by)
            for j, (b, dg) in enumerate(((0, diag_r), (2, diag_n))):
                flat = dg.rearrange("p t n -> p (t n)")
                pe.wait_ge(diag_ready.sem, diag_ready.at(L, j))
                for s in range(2):
                    mm = pe.matmul(msc[:, b + s, 0:HALF], ones, flat[:, s * HALF:(s + 1) * HALF], start=True, stop=True)
                mm.then_inc(bc_ready.sem, bc_ready.by)

        def act_ln(act, ph):
            L = LN_OF[ph]
            act.wait_ge(stat_step.sem, stat_step.at(L, 3))
            act.activation(rstd, tmp5, ACT.Sqrt).then_inc(std_ready.sem, std_ready.by)
            for k in range(KT):
                act.wait_ge(shifted.sem, shifted.at(L, k))
                g, b = lnc[:, L, 0, k:k + 1], lnc[:, L, 1, k:k + 1]
                if ph != PLAN[-1]:
                    act.activation(xh[:, k, :], norm_b[:, k % 2, :], ACT.Identity, scale=g, bias=b)\
                       .then_inc(xh_ready.sem, xh_ready.by)
                act.activation(x[:, k, :], norm_b[:, k % 2, :], ACT.Identity, scale=g, bias=b)\
                   .then_inc(x_ready.sem, x_ready.by)

        def dve_ln(dve, ph):
            L = LN_OF[ph]
            dve.wait_ge(stat_mm.sem, stat_mm.at(L))
            dve.tensor_copy(st[:, :, 0:TT], msc[:, 0, 0:16].rearrange("p (a t) -> p a t", a=2)[:, :, 0:TT])\
               .then_inc(stat_step.sem, stat_step.by)
            dve.wait_ge(stat_step.sem, stat_step.at(L, 0))
            dve.tensor_tensor(tmp5, st[:, 0, 0:TT], st[:, 0, 0:TT], ALU.mult).then_inc(stat_step.sem, stat_step.by)
            dve.wait_ge(stat_step.sem, stat_step.at(L, 1))
            dve.tensor_tensor(tmp5, st[:, 1, 0:TT], tmp5, ALU.subtract).then_inc(stat_step.sem, stat_step.by)
            dve.wait_ge(stat_step.sem, stat_step.at(L, 2))
            eps = LN_EPS * (4.0 if ph[0] == "ffn" else 1.0)
            dve.tensor_scalar(tmp5, tmp5, 0.0, eps, ALU.max, ALU.add).then_inc(stat_step.sem, stat_step.by)
            dve.wait_ge(std_ready.sem, std_ready.at(L))
            dve.reciprocal(rstd, rstd).then_inc(stat_step.sem, stat_step.by)
            dve.wait_ge(stat_step.sem, stat_step.at(L, 4))
            dve.tensor_tensor(diag_r, over_tiles(ident, TT), rstd.unsqueeze(2).broadcast_to([P, TT, P]),
                                     ALU.mult)\
               .then_inc(diag_ready.sem, diag_ready.by)
            dve.scalar_tensor_tensor(out=nmr, in0=st[:, 0, 0:TT], scalar=-1.0, in1=rstd, op0=ALU.mult,
                                            op1=ALU.mult)\
               .then_inc(stat_step.sem, stat_step.by)
            dve.wait_ge(stat_step.sem, stat_step.at(L, 5))
            dve.tensor_tensor(diag_n, over_tiles(ident, TT), nmr.unsqueeze(2).broadcast_to([P, TT, P]),
                                     ALU.mult)\
               .then_inc(diag_ready.sem, diag_ready.by)
            dve.wait_ge(bc_ready.sem, bc_ready.at(L, 0))

            for k in range(KT):
                dve.tensor_tensor(halves(norm_a[:, k % 2, :]), halves(x[:, k, :]), msc[:, 0:2, 0:HALF], ALU.mult)\
                   .then_inc(scaled.sem, scaled.by)
                dve.wait_ge(scaled.sem, scaled.at(L, k))
                if k == 0:
                    dve.wait_ge(bc_ready.sem, bc_ready.at(L, 1))
                if k >= 2:
                    dve.wait_ge(x_ready.sem, x_ready.at(L, k - 2))
                dve.tensor_tensor(halves(norm_b[:, k % 2, :]), halves(norm_a[:, k % 2, :]), msc[:, 2:4, 0:HALF],
                                         ALU.add)\
                   .then_inc(shifted.sem, shifted.by)

        def pool_ln(pool, ph):
            for k in range(KT):
                pool.wait_ge(x_ready.sem, x_ready.at(LN_OF[ph], k))
                pool.tensor_tensor(xl[:, k, :], x[:, k, :], xh[:, k, :].bitcast(F32), ALU.subtract)\
                    .then_inc(xl_ready.sem, xl_ready.by)

        def xsplit_wait(pe, kind, occ):
            prev = PLAN.index((kind, occ)) - 1

            def need(k, part):
                if prev < 0:
                    pe.wait_ge(start_split.sem, start_split.at(k, part))
                elif part == 0:
                    pe.wait_ge(xh_ready.sem, xh_ready.at(LN_OF[PLAN[prev]], k))
                else:
                    pe.wait_ge(xl_ready.sem, xl_ready.at(LN_OF[PLAN[prev]], k))
            return need
        start_split.per = 2

        flat = msc[:].rearrange("p b n -> p (b n)")
        pair = [flat[:, 0:TOK], flat[:, 2 * 512:2 * 512 + TOK]]

        def tiles5(ap):
            return ap.rearrange("p (t n) -> p t n", t=TT)

        def col(t, n=P):
            return slice(t * n, (t + 1) * n)

        def bc(ap, n):
            return ap.unsqueeze(2).broadcast_to([P, ap.shape[1], n])

        def transposes(pe, out, src, signal):
            for t in range(TT):
                mm = pe.transpose(out[:, col(t)], src[:, col(t)], ident)
            mm.then_inc(signal.sem, signal.by)

        def pe_tile_parts(pe, T, par, parts, need=None):
            if parts[0] == 0:
                if not (isinstance(T, int) and T < 2):
                    pe.wait_ge(evacuated[par].sem, evacuated[par].at(half(T) - 1))
                pe.wait_ge(lo_ready.sem, lo_ready.at(T))
            for k in parts:
                w_hi, w_lo = wh[:, par, col(k)], wl[:, par, col(k)]
                for n, (w, r) in enumerate(((w_hi, xh), (w_lo, xh), (w_hi, xl))):
                    if need and n != 1:
                        need(k, n // 2)
                    for s in range(2):
                        mm = pe.matmul(gem[:, par, s, 0:HALF], w, r[:, k, s * HALF:(s + 1) * HALF],
                                       start=(k == 0 and n == 0), stop=(k == KT - 1 and n == 2))
            if parts[-1] == KT - 1:
                mm.then_inc(tile_done.sem, tile_done.by)

        def pe_first_pair(pe, kind, occ):
            need, b = xsplit_wait(pe, kind, occ), base[kind, occ]
            for k in range(KT // 2):
                pe_tile_parts(pe, b, 0, [k], need)
                pe_tile_parts(pe, b + 1, 1, [k])
            pe_tile_parts(pe, b, 0, range(KT // 2, KT), need)
            pe_tile_parts(pe, b + 1, 1, range(KT // 2, KT))

        def pe_projection(pe, b_down, ready, last_step):
            def down(i):
                for par in range(2):
                    def need(k):
                        if k == 0:
                            pe.wait_ge(ready.sem, ready.at(last_step - 1, 1))
                        if k == KT - 2:
                            pe.wait_ge(ready.sem, ready.at(last_step, 1))
                    pe_tile(pe, tile(b_down, 2, i, par), par, KT, hh, hl, before=need)
            loop(pe, KT // 2, down)

        def act_projection(act, ph, b_down, stats):
            def down(i):
                for par in range(2):
                    T = tile(b_down, 2, i, par)
                    act_split(act, T, par)
                    if stats:
                        act_square(act, ph, T, par, i)
            loop(act, KT // 2, down, peel_first=stats, peel_last=(b_down + KT == N_CHUNKS))

        a_in = [view(j * TOK, TOK) for j in range(4)]
        a_z = [view((4 + j) * TOK, TOK) for j in range(2)]
        a_bs, a_e, a_en, a_kd, a_qd, a_ki = (view(j * TOK, TOK) for j in range(6, 12))
        a_og = a_bs
        a_ket = view(12 * TOK, TT, P)
        a_att = view(13 * TOK, TT, P)
        a_vt = view(14 * TOK, TT, 2 * P)
        a_lah = view(16 * TOK, TT, P)
        a_o = view(16 * TOK, TT, 2 * P)
        a_sin = view(18 * TOK, STREAMS, 2, P)
        a_s = view(18 * TOK + 2048, 2 * P)
        a_vx = view(8 * TOK, STREAMS, P)
        a_f = view(8 * TOK, 2, P)
        a_sq = view(8 * TOK + 1024, 2 * P)
        a_la = view(18 * TOK + 2304, TT, 512)
        a_rank = view(10 * TOK, TOK)
        a_abs = view(8 * TOK, 2, 512)
        a_w1 = view(18 * TOK, KT, RANK)
        a_w2 = view(18 * TOK + 128, 512)
        a_b = view(18 * TOK + 640, 512)
        a_ss, a_std = small[:, 40:45], small[:, 48:53]

        gla = {n: Signal("gla_" + n, per=p) for n, p in dict(
            rank_mm=1, rank=1, logit_mm=TT, logit_act=3 * TT, la=TT, zeroed=1,
            lah=1, bc_mm=1, bs=1, v_mm=2, v=2, exp=2, kdiff=1, kexp=1, dec=3, ke_mm=1, ke=1, att_mm=1, att=1,
            s_zero=1, u_mm=NCK, o_mm=NCK, state=NCK, o=TT, qs_mm=1, qs=1, vx=2, su_mm=2, s_dec=2, s_new=2,
            sq=1, ss=1, std=1, rs=1, on=1, og_mm=2, og=2, split=2, mid=1).items()}
        a_param = Signal("gla_params_loaded", by=16)
        a_sld = Signal("gla_state_loaded", by=16)
        a_sst = Signal("gla_state_stored", per=2, by=16)

        GLA_ORDER = (4, 5, 0, 1, 2, 3)

        def gla_tile(i, j):
            return tile(base["gla", 0] + 4, 6, i, GLA_ORDER.index(j))

        def pe_gla(pe, occ):
            b = base["gla", 0]
            L = LN_OF["ffn", 0]

            def first(j):
                pe_tile_parts(pe, b + j, j % 2, range(KT))
            pe_first_pair(pe, "gla", 0)
            pe.wait_ge(a_param.sem, 3 * 16)
            pe.wait_ge(x_ready.sem, x_ready.at(L, KT - 1))
            for s in range(2):
                for k in range(KT):
                    mm = pe.matmul(msc[0:RANK, s, 0:HALF], a_w1[:, k, :], x[:, k, s * HALF:(s + 1) * HALF],
                                   start=(k == 0), stop=(k == KT - 1))
            mm.then_inc(gla["rank_mm"].sem, gla["rank_mm"].by)
            pe.wait_ge(gla["rank"].sem, gla["rank"].at(0))
            for t in range(TT):
                if t >= 2:
                    pe.wait_ge(gla["la"].sem, gla["la"].at(0, t - 2))
                bank = msc[:, 2 + t % 2, :]
                pe.matmul(bank, a_rank[0:RANK, col(t)], a_w2[0:RANK, :], start=True, stop=False)
                pe.matmul(bank, ones[0:1, :], a_b[0:1, :], start=False, stop=True).then_inc(gla["logit_mm"].sem, gla["logit_mm"].by)
                if t:
                    pe_tile_parts(pe, b + 2, 0, range(2 * t - 2, 2 * t))
            first(3)

            def body(i, last=False):
                h = i

                def parts(a, b):
                    for n in range(a, b):
                        j = GLA_ORDER[n // KT]
                        if not (last and j < 4):
                            pe_tile_parts(pe, gla_tile(i, j), n // KT % 2, [n % KT])
                parts(0, 7)
                pe.wait_ge(gla["lah"].sem, gla["lah"].at(h))
                for t in range(TT):
                    mm = pe.matmul(flat[:, col(t)], a_lah[:, t, :], const(C_L64 if t < PT else C_L16),
                                   start=True, stop=True)
                mm.then_inc(gla["bc_mm"].sem, gla["bc_mm"].by)
                parts(7, 9)
                pe.wait_ge(evacuated[0].sem, evacuated[0].at(half(v_tile(i, 2))))
                transposes(pe, pair[1], a_in[2], gla["v_mm"])
                pe.wait_ge(gla["bs"].sem, gla["bs"].at(h))
                pe.wait_ge(evacuated[1].sem, evacuated[1].at(half(v_tile(i, 3))))
                transposes(pe, pair[0], a_in[3], gla["v_mm"])
                parts(9, 14)
                pe.wait_ge(gla["dec"].sem, gla["dec"].at(h, 2))
                pe.wait_ge(gla["v"].sem, gla["v"].at(h, 1))
                transposes(pe, pair[0], a_kd, gla["ke_mm"])
                for t in range(TT):
                    mm = pe.matmul(pair[1][:, col(t)], a_ki[:, col(t)], a_qd[:, col(t)], start=True, stop=True)
                mm.then_inc(gla["att_mm"].sem, gla["att_mm"].by)
                parts(14, 16)
                pe.wait_ge(gla["ke"].sem, gla["ke"].at(h))
                pe.wait_ge(gla["att"].sem, gla["att"].at(h))
                for n in range(NCK):
                    t, c = n // 2, n % 2
                    rows = slice(GLA_CHUNK * c, GLA_CHUNK * (c + 1))
                    o = msc[:, t % 2, 0:2 * P]
                    if c == 0:
                        if t >= 2:
                            pe.wait_ge(gla["o"].sem, gla["o"].at(h, t - 2))
                        pe.matmul(o, a_att[:, t, :], a_vt[:, t, :], start=True, stop=True, skip_group_check=True)
                    if n >= 2:
                        pe.wait_ge(gla["state"].sem, gla["state"].at(h, n - 2))
                    pe.matmul(msc[:, 2 + c, 0:2 * P], a_ket[rows, t, :], a_vt[rows, t, :],
                                     start=True, stop=True)\
                       .then_inc(gla["u_mm"].sem, gla["u_mm"].by)
                    if n == 0:
                        pe.wait_ge(gla["s_zero"].sem, gla["s_zero"].at(h))
                    else:
                        pe.wait_ge(gla["state"].sem, gla["state"].at(h, n - 1))
                    pe.matmul(msc[rows, t % 2, 0:2 * P], a_qd[:, n * GLA_CHUNK:(n + 1) * GLA_CHUNK], a_s,
                                     start=False, stop=True, skip_group_check=True)\
                       .then_inc(gla["o_mm"].sem, gla["o_mm"].by)
                    if n < 7:
                        parts(16 + 3 * n, 19 + 3 * n)
                pe.wait_ge(a_sld.sem, a_sld.at(h))
                pe.wait_ge(gla["state"].sem, gla["state"].at(h, NCK - 1))
                for d in range(2):
                    for s in range(STREAMS):
                        c0 = SEQ + s * SLEN
                        mm = pe.matmul(msc[:, 2, d * P + s * SLEN:d * P + (s + 1) * SLEN], a_sin[:, s, d, :],
                                       a_qd[:, c0:c0 + SLEN], start=True, stop=True)
                mm.then_inc(gla["qs_mm"].sem, gla["qs_mm"].by)
                parts(37, 40)
                pe.wait_ge(gla["o"].sem, gla["o"].at(h, PT - 2))
                pe.wait_ge(gla["qs"].sem, gla["qs"].at(h))
                pe.matmul(msc[:, 0, 0:2 * P], a_att[:, PT, :], a_vt[:, PT, :], start=True, stop=True,
                          skip_group_check=True)
                for d in range(2):
                    mm = pe.matmul(msc[:, 0, d * P:(d + 1) * P], a_f[:, d, :], ident, start=False, stop=True,
                                   skip_group_check=True)
                mm.then_inc(gla["mid"].sem, gla["mid"].by)
                parts(40, 43)
                for d in range(2):
                    pe.wait_ge(gla["vx"].sem, gla["vx"].at(h, d))
                    if d == 1:
                        pe.wait_ge(gla["s_new"].sem, gla["s_new"].at(h, 0))
                    for g in range(2):
                        mm = pe.matmul(msc[:, 2 + g, :], a_ket[:, PT, :],
                                       a_vx[:, 4 * g:4 * g + 4, :].rearrange("p s n -> p (s n)"),
                                       start=True, stop=True)
                    mm.then_inc(gla["su_mm"].sem, gla["su_mm"].by)
                    if d == 0:
                        parts(43, 46)
                parts(46, 48)
                pe.wait_ge(gla["on"].sem, gla["on"].at(h))
                pe.wait_ge(gla["s_new"].sem, gla["s_new"].at(h, 1))
                for d in range(2):
                    for t in range(TT):
                        mm = pe.transpose(pair[d][:, col(t)], a_o[:, t, d * P:(d + 1) * P], ident)
                    mm.then_inc(gla["og_mm"].sem, gla["og_mm"].by)
            gla_loop(pe, body)
            pe_projection(pe, b + GLA_HEADS * 6, gla["split"], GLA_HEADS - 1)

        def v_tile(i, j):
            return tile(base["gla", 0], 6, i, j)

        def gla_loop(eng, body):
            with eng.Fori(0, GLA_HEADS - 1) as i:
                body(i)
            body(GLA_HEADS - 1, last=True)

        def act_gla(act, occ):
            b = base["gla", 0]

            def copy_in(T, par, j):
                act.wait_ge(tile_done.sem, tile_done.at(T))
                act.copy(halves(a_in[j]), slot(par)).then_inc(evacuated[par].sem, evacuated[par].by)
                act_split(act, T, par)
            copy_in(b, 0, 0)
            act.wait_ge(gla["rank_mm"].sem, gla["rank_mm"].at(0))
            act.copy(a_rank[0:RANK, :].rearrange("p (s n) -> p s n", s=2), msc[0:RANK, 0:2, 0:HALF])\
               .then_inc(gla["rank"].sem, gla["rank"].by)
            copy_in(b + 1, 1, 1)
            for t in range(TT):
                ab = a_abs[:, t % 2, :]
                act.wait_ge(gla["logit_mm"].sem, gla["logit_mm"].at(0, t))
                if t >= 2:
                    act.wait_ge(gla["la"].sem, gla["la"].at(0, t - 2))
                act.activation(ab, msc[:, 2 + t % 2, :], ACT.Abs).then_inc(gla["logit_act"].sem, gla["logit_act"].by)
                act.wait_ge(gla["logit_act"].sem, gla["logit_act"].at(0, 3 * t))
                act.activation(ab, ab, ACT.Exp, scale=-1.0).then_inc(gla["logit_act"].sem, gla["logit_act"].by)
                act.wait_ge(gla["logit_act"].sem, gla["logit_act"].at(0, 3 * t + 1))
                act.activation(ab, ab, ACT.Ln, bias=ones[:, 0:1]).then_inc(gla["logit_act"].sem, gla["logit_act"].by)
            copy_in(b + 2, 0, 2)
            copy_in(b + 3, 1, 3)

            def body(i, last=False):
                h = i

                def tile_out(n):
                    j, par = GLA_ORDER[n], n % 2
                    if last and j < 4:
                        return
                    T = gla_tile(i, j)
                    act.wait_ge(tile_done.sem, tile_done.at(T))
                    if j >= 4:
                        act.activation(halves(a_z[j - 4]), slot(par), ACT.Silu).then_inc(evacuated[par].sem, evacuated[par].by)
                    else:
                        act.copy(halves(a_in[j]), slot(par)).then_inc(evacuated[par].sem, evacuated[par].by)
                    act_split(act, T, par)
                act.dma_start(a_sin.rearrange("p s d n -> p s (d n)"), gla_s[h]).then_inc(a_sld.sem, a_sld.by)
                act.wait_ge(gla["v_mm"].sem, gla["v_mm"].at(h, 0))
                act.copy(a_vt[:, :, 0:P], tiles5(pair[1])).then_inc(gla["v"].sem, gla["v"].by)
                act.wait_ge(gla["v_mm"].sem, gla["v_mm"].at(h, 1))
                act.copy(a_vt[:, :, P:2 * P], tiles5(pair[0])).then_inc(gla["v"].sem, gla["v"].by)
                act.wait_ge(gla["bs"].sem, gla["bs"].at(h))
                act.activation(a_e, a_bs, ACT.Exp, scale=1.0 / GATE_TAU).then_inc(gla["exp"].sem, gla["exp"].by)
                act.activation(a_en, a_bs, ACT.Exp, scale=-1.0 / GATE_TAU).then_inc(gla["exp"].sem, gla["exp"].by)
                act.wait_ge(gla["kdiff"].sem, gla["kdiff"].at(h))
                act.activation(a_kd, a_kd, ACT.Exp, scale=1.0 / GATE_TAU).then_inc(gla["kexp"].sem, gla["kexp"].by)
                tile_out(0)
                act.wait_ge(gla["ke_mm"].sem, gla["ke_mm"].at(h))
                act.copy(a_ket, tiles5(pair[0])).then_inc(gla["ke"].sem, gla["ke"].by)
                tile_out(1)
                for n in range(NCK):
                    if n % 2:
                        act.wait_ge(gla["o_mm"].sem, gla["o_mm"].at(h, n))
                        act.copy(a_o[:, n // 2, :], msc[:, (n // 2) % 2, 0:2 * P]).then_inc(gla["o"].sem, gla["o"].by)
                    if n in (2, 5):
                        tile_out(2 if n == 2 else 3)
                act.wait_ge(gla["qs_mm"].sem, gla["qs_mm"].at(h))
                act.copy(a_f, msc[:, 2, 0:2 * P].rearrange("p (d n) -> p d n", d=2)).then_inc(gla["qs"].sem, gla["qs"].by)
                tile_out(4)
                act.wait_ge(gla["mid"].sem, gla["mid"].at(h))
                act.copy(a_o[:, PT, :], msc[:, 0, 0:2 * P]).then_inc(gla["o"].sem, gla["o"].by)
                for t in range(TT):
                    act.wait_ge(gla["o"].sem, gla["o"].at(h, t))
                    if t:
                        act.wait_ge(gla["sq"].sem, h * TT + t)
                    ins = act.activation(a_sq, a_o[:, t, :], ACT.Square, accum_out=a_ss[:, t:t + 1])
                    ins.then_inc(gla["sq"].sem, 1)
                act.wait_ge(gla["ss"].sem, gla["ss"].at(h))
                act.activation(a_std, a_ss, ACT.Sqrt).then_inc(gla["std"].sem, gla["std"].by)
                tile_out(5)
                act.wait_ge(gla["s_new"].sem, gla["s_new"].at(h, 1))
                act.dma_start(gla_s_out[h], a_sin.rearrange("p s d n -> p s (d n)")).then_inc(a_sst.sem, a_sst.by)
                act.dma_start(gla_p_out[h], a_s).then_inc(a_sst.sem, a_sst.by)
                act.wait_ge(a_sst.sem, a_sst.at(h, 1))
            gla_loop(act, body)
            act_projection(act, ("gla", 0), b + GLA_HEADS * 6, stats=True)

        def dve_gla(dve, occ):
            b = base["gla", 0]
            dve.memset(a_att, 0.0).then_inc(gla["zeroed"].sem, gla["zeroed"].by)
            for t in range(TT):
                dve.wait_ge(gla["logit_act"].sem, gla["logit_act"].at(0, 3 * t + 2))
                dve.scalar_tensor_tensor(out=a_la[:, t, :], in0=msc[:, 2 + t % 2, :], scalar=0.0,
                                                in1=a_abs[:, t % 2, :], op0=ALU.min, op1=ALU.subtract)\
                   .then_inc(gla["la"].sem, gla["la"].by)

            def body(i, last=False):
                h = i
                dve.wait_ge(gla["la"].sem, gla["la"].at(0, TT - 1))
                dve.tensor_copy(a_lah, a_la[:, :, bass.ts(h, P)]).then_inc(gla["lah"].sem, gla["lah"].by)
                dve.wait_ge(gla["bc_mm"].sem, gla["bc_mm"].at(h))
                dve.tensor_copy(a_bs, pair[0]).then_inc(gla["bs"].sem, gla["bs"].by)
                dve.wait_ge(gla["bs"].sem, gla["bs"].at(h))
                pb, sb_ = a_bs[:, 0:SEQ], a_bs[:, SEQ:TOK]
                pb3, sb3 = pb.rearrange("p (c n) -> p c n", n=GLA_CHUNK), sb_.rearrange("p (c n) -> p c n", n=SLEN)
                pk3 = a_kd[:, 0:SEQ].rearrange("p (c n) -> p c n", n=GLA_CHUNK)
                sk3 = a_kd[:, SEQ:TOK].rearrange("p (c n) -> p c n", n=SLEN)
                dve.tensor_tensor(pk3, pb3[:, :, GLA_CHUNK - 1:GLA_CHUNK].broadcast_to([P, NCK, GLA_CHUNK]), pb3,
                                  ALU.subtract)
                dve.tensor_tensor(sk3, sb3[:, :, SLEN - 1:SLEN].broadcast_to([P, STREAMS, SLEN]), sb3,
                                         ALU.subtract)\
                   .then_inc(gla["kdiff"].sem, gla["kdiff"].by)
                dve.wait_ge(gla["exp"].sem, gla["exp"].at(h, 1))
                dve.wait_ge(evacuated[1].sem, evacuated[1].at(half(v_tile(i, 1))))
                dve.scalar_tensor_tensor(out=a_qd, in0=a_in[0], scalar=float(P) ** -0.5, in1=a_e,
                                                op0=ALU.mult, op1=ALU.mult)\
                   .then_inc(gla["dec"].sem, gla["dec"].by)
                dve.tensor_tensor(a_ki, a_in[1], a_en, ALU.mult).then_inc(gla["dec"].sem, gla["dec"].by)
                dve.wait_ge(gla["kexp"].sem, gla["kexp"].at(h))
                dve.tensor_tensor(a_kd, a_in[1], a_kd, ALU.mult).then_inc(gla["dec"].sem, gla["dec"].by)
                dve.wait_ge(gla["zeroed"].sem, gla["zeroed"].at(0))
                dve.wait_ge(a_sld.sem, a_sld.at(h))
                dve.wait_ge(gla["att_mm"].sem, gla["att_mm"].at(h))
                dve.memset(a_s, 0.0).then_inc(gla["s_zero"].sem, gla["s_zero"].by)
                dve.copy_predicated(a_att[:, 0:PT, :], over_tiles(const(C_L64), PT).bitcast(U32),
                                    tiles5(pair[1])[:, 0:PT, :])
                dve.copy_predicated(a_att[:, PT, :], const(C_L16).bitcast(U32), pair[1][:, SEQ:TOK])\
                   .then_inc(gla["att"].sem, gla["att"].by)
                for n in range(NCK):
                    dve.wait_ge(gla["u_mm"].sem, gla["u_mm"].at(h, n))
                    dve.wait_ge(gla["o_mm"].sem, gla["o_mm"].at(h, n))
                    end = (n + 1) * GLA_CHUNK - 1
                    if n == 0:
                        dve.wait_ge(gla["s_zero"].sem, gla["s_zero"].at(h))
                    else:
                        dve.wait_ge(gla["state"].sem, gla["state"].at(h, n - 1))
                    dve.scalar_tensor_tensor(out=a_s, in0=a_s, scalar=a_e[:, end:end + 1],
                                                    in1=msc[:, 2 + n % 2, 0:2 * P], op0=ALU.mult, op1=ALU.add)\
                       .then_inc(gla["state"].sem, gla["state"].by)
                dve.wait_ge(gla["qs_mm"].sem, gla["qs_mm"].at(h))
                dve.wait_ge(gla["mid"].sem, gla["mid"].at(h))
                ends = a_e[:, SEQ:TOK].rearrange("p (s n) -> p s n", n=SLEN)[:, :, SLEN - 1:SLEN]\
                    .broadcast_to([P, STREAMS, P])
                for d in range(2):
                    if d:
                        dve.wait_ge(gla["su_mm"].sem, gla["su_mm"].at(h, 0))
                    v = a_vt[:, PT, d * P:(d + 1) * P].unsqueeze(1).broadcast_to([P, STREAMS, P])
                    m = bc(cs[:, C_M8:C_M8 + STREAMS], P)
                    dve.tensor_tensor(a_vx, v, m, ALU.mult).then_inc(gla["vx"].sem, gla["vx"].by)
                    dve.tensor_tensor(a_sin[:, :, d, :], a_sin[:, :, d, :], ends, ALU.mult).then_inc(gla["s_dec"].sem, gla["s_dec"].by)
                    dve.wait_ge(gla["su_mm"].sem, gla["su_mm"].at(h, d))
                    dve.wait_ge(gla["s_dec"].sem, gla["s_dec"].at(h, d))
                    dve.tensor_tensor(a_sin[:, :, d, :], a_sin[:, :, d, :],
                                             msc[:, 2:4, :].rearrange("p b (s n) -> p (b s) n", n=P), ALU.add)\
                       .then_inc(gla["s_new"].sem, gla["s_new"].by)
                dve.wait_ge(gla["sq"].sem, (h + 1) * TT)
                dve.tensor_scalar(a_ss, a_ss, 1.0 / (2 * P), RMS_EPS, ALU.mult, ALU.add).then_inc(gla["ss"].sem, gla["ss"].by)
                dve.wait_ge(gla["std"].sem, gla["std"].at(h))
                dve.reciprocal(a_std, a_std).then_inc(gla["rs"].sem, gla["rs"].by)
                dve.wait_ge(gla["rs"].sem, gla["rs"].at(h))
                dve.tensor_tensor(a_o, a_o, bc(a_std, 2 * P), ALU.mult).then_inc(gla["on"].sem, gla["on"].by)
                for d in range(2):
                    dve.wait_ge(gla["og_mm"].sem, gla["og_mm"].at(h, d))
                    dve.wait_ge(evacuated[d].sem, evacuated[d].at(half(gla_tile(i, 4 + d))))
                    if d:
                        dve.wait_ge(gla["split"].sem, gla["split"].at(h, 0))
                    dve.scalar_tensor_tensor(out=a_og, in0=pair[d], scalar=nrm[:, d:d + 1], in1=a_z[d],
                                                    op0=ALU.mult, op1=ALU.mult)\
                       .then_inc(gla["og"].sem, gla["og"].by)
                    split_hidden(dve, a_og, h, d, h, gla)
            gla_loop(dve, body)
            dve_down(dve, ("gla", 0), b + GLA_HEADS * 6, ALPHA, stats=True)

        split_hi = Signal("mixed_hi_ready")

        def split_hidden(dve, src, slot_pair, d, step, S):
            to = slot_pair * 2 + d
            k = step * 2 + (d + (0 if S is gla else 2 * GLA_HEADS))
            dve.wait_ge(S["og"].sem, S["og"].at(step, d))
            dve.tensor_copy(hh[:, to, :], src).then_inc(split_hi.sem, 1)
            dve.wait_ge(split_hi.sem, k + 1)
            dve.tensor_tensor(hl[:, to, :], src, hh[:, to, :].bitcast(F32), ALU.subtract)\
               .then_inc(S["split"].sem, S["split"].by)

        NU = 2 * TT
        d_in = [view(j * TOK, TOK) for j in range(4)]
        d_xp, d_acc = view(4 * TOK, XPW), view(4 * TOK + XPW, XPW)
        AT = 4 * TOK + 2 * XPW
        d_qk = view(AT + TOK, TOK)
        d_qt = view(AT, TT, P)
        d_z = [view(AT, TOK), d_qk]
        AT += 2 * TOK
        d_kq = view(AT, 2, TOK)
        AT += 2 * TOK
        d_kt = view(AT, TT, P)
        AT += TOK
        d_vt = view(AT, 2, TT, P)
        AT += 2 * TOK
        d_at = view(AT, NU, P)
        AT += NU * P
        d_og = [view(AT - NU * P, TOK), view(AT - NU * P + TOK, TOK)]
        d_U = view(AT, NU, P)
        AT += NU * P
        d_dt = view(AT, NU, P)
        d_o = view(AT, TT, 2, P)
        AT += NU * P
        d_T, d_P, d_M = view(AT, NU, P), view(AT + NU * P, NU, P), view(AT + 2 * NU * P, NU, P)
        d_sin = view(AT, 2, STREAMS, P)
        d_vx = view(AT + 2048, STREAMS, P)
        d_f, d_ws = view(AT + 2048, 2, 2, P), view(AT + 2048 + 4 * P, 2, P)
        d_w, d_vn, d_ke = (view(AT + 3072 + j * 2 * P, 2, P) for j in range(3))
        AT += 3 * NU * P
        d_s = view(AT, 2, P)
        assert AT + 2 * P <= 16384
        d_sqs = small[:, 64:64 + P]

        GN = ("g", "beta", "eg", "ke", "ngc", "neg_eg", "egl")
        NQ = len(GN)
        d_gq = gq[:, 0:NQ * TT * GDN_VH].rearrange("p (a t h) -> p a t h", a=NQ, t=TT)
        at2 = NQ * TT * GDN_VH
        d_egs = gq[:, at2:at2 + STREAMS * GDN_VH].rearrange("p (s h) -> p s h", s=STREAMS)
        at2 += STREAMS * GDN_VH
        d_hq = gq[:, at2:at2 + NQ * TT * 2].rearrange("p (a t h) -> p a t h", a=NQ, t=TT)
        at2 += NQ * TT * 2
        d_hegs = gq[:, at2:at2 + STREAMS * 2].rearrange("p (s h) -> p s h", s=STREAMS)
        at2 += STREAMS * 2
        d_ss, d_rs = gq[:, at2:at2 + NU], gq[:, at2 + NU:at2 + 2 * NU]
        d_os, d_ors = gq[:, at2 + 2 * NU:at2 + 3 * NU], gq[:, at2 + 3 * NU:at2 + 4 * NU]
        at2 += 4 * NU
        d_adt = gq[:, at2:at2 + 32].rearrange("p (a h) -> p a h", a=2)
        at2 += 32
        assert at2 <= 896
        d_wab = newh[:].rearrange("p h n -> p (h n)")[:, GDN_KH * 108 - KT * 32:].rearrange(
            "p (k n) -> p k n", k=KT)
        TH = TT * GDN_VH
        d_y, d_l, d_glast = (view(8 * TOK + j * P, TH).rearrange("p (t h) -> p t h", t=TT) for j in range(3))

        def num(name, t, v):
            return d_hq[:, GN.index(name), t, v:v + 1]

        gdn = {n: Signal("gdn_" + n, per=p) for n, p in dict(
            ab_mm=1, gates=7, gact=5, cum_mm=1, cact=3, copied=1, zero=1, cum=1, neg=1, conv_h=1,
            hq=1, qk_mm=2, sq=NU, ss=1, std=1, rs=2, qt=1, kt=1, v_mm=2, v=2, kq_mm=2, kq=2, kk_mm=1, kk=2, qkm_mm=1,
            qkm=1, dt_mm=2, dt=2, att=2, m=2, ml=3, tr_mm=3, p_mm=18, p=18, x_mm=15, y_mm=18, t0=3, t=15, u=21,
            s_zero=1, ks_mm=TT, f_mm=2, f=2, w=TT, a=TT, ke=TT, tw_mm=TT, vn=TT, o_mm=TT, o=TT, su_mm=PT, state=PT,
            vx=2, ssu_mm=2, s_dec=2, s_new=2, osq=NU, oss=1, ostd=1, ors=1, on=1, og_mm=2, og=2, split=2).items()}
        d_param = Signal("gdn_params_loaded", by=16)
        d_sld = Signal("gdn_state_loaded", by=16)
        d_sst = Signal("gdn_state_stored", per=2, by=16, before=1)
        gdn["s_new"].before = gdn["og"].before = 1
        conv_step = Signal("conv_step", per=4)
        conv_done = Signal("conv_done")
        conv_act = Signal("conv_silu_done")
        hist_stored = Signal("hist_stored", by=16)
        Z_PARTS = 4 * KT
        LEVEL_PARTS = {1: (18, 19), 2: (19, 24), 3: (24, 26), 4: (26, 26), 5: (26, 30), 6: (30, 32)}
        SEQ_PARTS = ((32, 33, 34, 35), (35, 35, 36, 37), (37, 37, 38, 39), (39, 39, 40, 40))
        CHAINS = ((slice(0, 4), 0, LEVELS), (slice(4, 8), 2, LEVELS), (slice(8, 10), 0, STREAM_LEVELS))

        def gdn_start(s_half):
            return base["gdn", 0] + 4 + s_half * (4 * 6 + KT)

        def gdn_tile(hf, i, n, last):
            return tile(gdn_start(hf), 6, i, n - 4 if last else n)

        def unit(v, t):
            return 4 * v + t if t < PT else 8 + v

        def chain_items():
            for lv in range(LEVELS):
                for c, (us, bank, n) in enumerate(CHAINS):
                    if lv < n:
                        yield lv, c, us, bank, n

        ML = {}
        for lv, c, us, bank, n in chain_items():
            ML[lv, c] = len(ML)
        PX = {k: i for i, k in enumerate(k for k in ML if k[0] > 0)}
        XX = {k: i for i, k in enumerate(k for k in ML if k[0] > 0 and k[0] < CHAINS[k[1]][2] - 1)}
        gdn["u"].per = len(ML)
        gdn["p_mm"].per = gdn["p"].per = gdn["y_mm"].per = len(PX)
        gdn["x_mm"].per = gdn["t"].per = len(XX)

        def pe_gdn(pe, occ):
            b = base["gdn", 0]
            L = LN_OF[PLAN[PLAN.index(("gdn", 0)) - 1]]

            def first(j):
                pe_tile_parts(pe, b + j, j % 2, range(KT))
            pe_first_pair(pe, "gdn", 0)
            pe.wait_ge(d_param.sem, 4 * 16)
            pe.wait_ge(x_ready.sem, x_ready.at(L, KT - 1))
            for t in range(TT):
                for k in range(KT):
                    mm = pe.matmul(msc[:, 0, t * 32:(t + 1) * 32], x[:, k, col(t)], d_wab[:, k, :],
                                   start=(k == 0), stop=(k == KT - 1))
            mm.then_inc(gdn["ab_mm"].sem, gdn["ab_mm"].by)
            first(2)
            pe.wait_ge(gdn["gates"].sem, gdn["gates"].at(0, 6))
            for t in range(TT):
                pe.matmul(msc[:, 1, t * 16:(t + 1) * 16], const(C_L128 if t < PT else C_L16), d_gq[:, 0, t, :],
                          start=True, stop=True)
            for t in range(TT):
                pe.matmul(msc[:, 2, t * 16:(t + 1) * 16], ones if t < PT else const(C_BO16), d_gq[:, 0, t, :],
                          start=True, stop=True)
            for s in range(STREAMS):
                mm = pe.matmul(msc[:, 3, s * 16:(s + 1) * 16],
                               cs[:, C_M8 + s:C_M8 + s + 1].broadcast_to([P, P]), d_gq[:, 0, PT, :],
                               start=True, stop=True)
            mm.then_inc(gdn["cum_mm"].sem, gdn["cum_mm"].by)
            first(3)
            pe.wait_ge(gdn["neg"].sem, gdn["neg"].at(0))
            pe.wait_ge(gdn["cact"].sem, gdn["cact"].at(0, 2))

            def body(hf, i, last=False):
                s = i + 4 * hf

                def parts(a, b):
                    for n in range(Z_PARTS if last else 0, 6 * KT):
                        if a <= n < b:
                            pe_tile_parts(pe, gdn_tile(hf, i, n // KT, last), n // KT % 2, [n % KT])
                parts(0, 1)
                pe.wait_ge(gdn["s_new"].sem, gdn["s_new"].at(s - 1, 1))
                pe.wait_ge(conv_act.sem, conv_act.at(s * 4))
                transposes(pe, pair[0], d_in[0], gdn["qk_mm"])
                pe.wait_ge(gdn["og"].sem, gdn["og"].at(s - 1, 1))
                pe.wait_ge(conv_act.sem, conv_act.at(s * 4 + 1))
                transposes(pe, pair[1], d_in[1], gdn["qk_mm"])
                parts(1, 8)
                for j, free in ((0, gdn["qt"]), (1, gdn["kt"])):
                    pe.wait_ge(conv_act.sem, conv_act.at(s * 4 + 2 + j))
                    pe.wait_ge(free.sem, free.at(s))
                    transposes(pe, pair[j], d_in[2 + j], gdn["v_mm"])
                parts(8, 9)
                pe.wait_ge(gdn["v"].sem, gdn["v"].at(s, 0))
                transposes(pe, pair[0], d_qt.rearrange("p t n -> p (t n)"), gdn["kq_mm"])
                pe.wait_ge(gdn["v"].sem, gdn["v"].at(s, 1))
                transposes(pe, pair[1], d_kt.rearrange("p t n -> p (t n)"), gdn["kq_mm"])
                parts(9, 11)
                pe.wait_ge(gdn["kq"].sem, gdn["kq"].at(s, 1))
                for out, j, signal in ((0, 0, gdn["kk_mm"]), (1, 1, gdn["qkm_mm"])):
                    for t in range(TT):
                        mm = pe.matmul(pair[out][:, col(t)], d_kq[:, 0, col(t)], d_kq[:, j, col(t)],
                                       start=True, stop=True)
                    mm.then_inc(signal.sem, signal.by)
                parts(11, 12)
                pe.wait_ge(gdn["hq"].sem, gdn["hq"].at(s))
                for v, free, j in ((0, gdn["kk"], 1), (1, gdn["qkm"], 0)):
                    pe.wait_ge(free.sem, free.at(s, j))
                    for t in range(TT):
                        tri, neg = (C_L128, C_NEG128) if t < PT else (C_L16, C_NEG16)
                        pe.matmul(pair[v][:, col(t)], num("g", t, v).broadcast_to([P, P]), const(tri),
                                  start=True, stop=False)
                        mm = pe.matmul(pair[v][:, col(t)], ident, const(neg), start=False, stop=True)
                    mm.then_inc(gdn["dt_mm"].sem, gdn["dt_mm"].by)
                parts(12, 16)
                for c, (us, bank, n) in enumerate(CHAINS):
                    pe.wait_ge(gdn["ml"].sem, gdn["ml"].at(s, c))
                    if c == 2:
                        parts(16, 17)
                    else:
                        pe.wait_ge(gdn["dt"].sem, gdn["dt"].at(s, c))
                    for k, u in enumerate(range(us.start, us.stop)):
                        mm = pe.transpose(msc[:, bank + c // 2, col(k)], d_P[:, u, :], ident)
                    mm.then_inc(gdn["tr_mm"].sem, gdn["tr_mm"].by)
                parts(17, 18)
                for lv in range(1, LEVELS):
                    def product_p(c):
                        us, bank, n = CHAINS[c]
                        if lv == 1:
                            pe.wait_ge(gdn["t0"].sem, gdn["t0"].at(s, c))
                        elif (lv - 1, c) in XX:
                            pe.wait_ge(gdn["t"].sem, gdn["t"].at(s, XX[lv - 1, c]))
                        before = [(lv - 1, c)] + {0: [(lv - 1, 2)] if lv > 1 else [], 1: [], 2: [(lv, 0)]}[c]
                        pe.wait_ge(gdn["u"].sem, gdn["u"].at(s, max(ML[k] for k in before if k in ML)))
                        for k, u in enumerate(range(us.start, us.stop)):
                            mm = pe.matmul(msc[:, bank, col(k)], d_M[:, u, :], d_T[:, u, :], start=True, stop=True)
                        mm.then_inc(gdn["p_mm"].sem, gdn["p_mm"].by)

                    def turn_u(c):
                        us, bank, n = CHAINS[c]
                        if (lv, c) in XX:
                            pe.wait_ge(gdn["u"].sem, gdn["u"].at(s, ML[lv, c]))
                            if lv == 1 and c == 0:
                                pe.wait_ge(gdn["t0"].sem, gdn["t0"].at(s, 2))
                            other = {0: (lv - 1, 2), 2: (lv, 0)}.get(c)
                            if other in XX:
                                pe.wait_ge(gdn["t"].sem, gdn["t"].at(s, XX[other]))
                            for k, u in enumerate(range(us.start, us.stop)):
                                mm = pe.transpose(msc[:, bank + 1, col(k)], d_U[:, u, :], ident)
                            mm.then_inc(gdn["x_mm"].sem, gdn["x_mm"].by)

                    def product_y(c):
                        us, bank, n = CHAINS[c]
                        pe.wait_ge(gdn["p"].sem, gdn["p"].at(s, PX[lv, c]))
                        for k, u in enumerate(range(us.start, us.stop)):
                            mm = pe.matmul(msc[:, bank, col(k)], d_P[:, u, :], d_U[:, u, :], start=True, stop=True)
                        mm.then_inc(gdn["y_mm"].sem, gdn["y_mm"].by)
                    product_p(0)
                    product_p(1)
                    product_y(0)
                    product_y(1)
                    turn_u(0)
                    a, b = LEVEL_PARTS[lv]
                    if (lv, 2) in ML:
                        product_p(2)
                        turn_u(1)
                        parts(a, a + 1)
                        a += 1
                        product_y(2)
                        parts(a, b)
                        turn_u(2)
                    else:
                        turn_u(1)
                        parts(a, b)
                ks, qs, tw, o = (msc[:, j, 0:2 * P] for j in range(4))
                for t in range(PT):
                    if t == 0:
                        pe.wait_ge(gdn["s_zero"].sem, gdn["s_zero"].at(s))
                        pe.wait_ge(gdn["u"].sem, gdn["u"].at(s, ML[LEVELS - 1, 1]))
                    else:
                        pe.wait_ge(gdn["state"].sem, gdn["state"].at(s, t - 1))
                    both = d_s.rearrange("p v n -> p (v n)")
                    pe.matmul(ks, d_kq[:, 0, col(t)], both, start=True, stop=True)
                    pe.matmul(qs, d_kq[:, 1, col(t)], both, start=True, stop=True)\
                      .then_inc(gdn["ks_mm"].sem, gdn["ks_mm"].by)
                    if t in (1, 2):
                        v = t - 1
                        pe.wait_ge(d_sld.sem, d_sld.at(s))
                        out = msc[:, 3, 2 * P:4 * P].rearrange("p (a n) -> p a n", a=2)
                        for r in range(STREAMS):
                            c0 = r * SLEN
                            mm = pe.matmul(out[:, :, c0:c0 + SLEN], d_sin[:, v, r, :],
                                           d_kq[:, :, SEQ + c0:SEQ + c0 + SLEN], start=True, stop=True)
                        mm.then_inc(gdn["f_mm"].sem, gdn["f_mm"].by)
                    if t == 3:
                        pe.wait_ge(gdn["f"].sem, gdn["f"].at(s, 1))
                        for j in range(2):
                            for v in range(2):
                                mm = pe.transpose(msc[:, 3 - j, col(2 * j + v)], d_f[:, v, j, :], ident)
                        mm.then_inc(gdn["ks_mm"].sem, gdn["ks_mm"].by)
                    a, b, c, d = SEQ_PARTS[t]
                    parts(a, b)
                    pe.wait_ge(gdn["w"].sem, gdn["w"].at(s, t))
                    for v in range(2):
                        mm = pe.matmul(tw[:, col(v)], d_U[:, unit(v, t), :], d_w[:, v, :], start=True, stop=True)
                    mm.then_inc(gdn["tw_mm"].sem, gdn["tw_mm"].by)
                    parts(b, c)
                    pe.wait_ge(gdn["vn"].sem, gdn["vn"].at(s, t))
                    pe.wait_ge(gdn["att"].sem, gdn["att"].at(s, 1))
                    if t == PT - 1:
                        pe.wait_ge(gdn["w"].sem, gdn["w"].at(s, PT))
                    for v in range(2):
                        mm = pe.matmul(o[:, col(v)], d_at[:, unit(v, t), :], d_vn[:, v, :], start=True, stop=True)
                    mm.then_inc(gdn["o_mm"].sem, gdn["o_mm"].by)
                    pe.wait_ge(gdn["ke"].sem, gdn["ke"].at(s, t))
                    for v in range(2):
                        mm = pe.matmul(ks[:, col(v)], d_ke[:, v, :], d_vn[:, v, :], start=True, stop=True)
                    mm.then_inc(gdn["su_mm"].sem, gdn["su_mm"].by)
                    parts(c, d)
                pe.wait_ge(gdn["a"].sem, gdn["a"].at(s, PT))
                for v in range(2):
                    mm = pe.matmul(tw[:, col(v)], d_U[:, unit(v, PT), :], d_ws[:, v, :], start=True, stop=True)
                mm.then_inc(gdn["tw_mm"].sem, gdn["tw_mm"].by)
                parts(40, 41)
                pe.wait_ge(gdn["vn"].sem, gdn["vn"].at(s, PT))
                pe.wait_ge(gdn["o"].sem, gdn["o"].at(s, PT - 1))
                for v in range(2):
                    mm = pe.matmul(o[:, col(v)], d_at[:, unit(v, PT), :], d_vn[:, v, :], start=True, stop=True)
                mm.then_inc(gdn["o_mm"].sem, gdn["o_mm"].by)
                parts(41, 43)
                pe.wait_ge(gdn["ke"].sem, gdn["ke"].at(s, PT))
                pe.wait_ge(gdn["state"].sem, gdn["state"].at(s, PT - 1))

                def stream_update(v):
                    pe.wait_ge(gdn["vx"].sem, gdn["vx"].at(s, v))
                    for g in range(2):
                        mm = pe.matmul(msc[:, g, :], d_ke[:, v, :],
                                       d_vx[:, 4 * g:4 * g + 4, :].rearrange("p s n -> p (s n)"),
                                       start=True, stop=True)
                    mm.then_inc(gdn["ssu_mm"].sem, gdn["ssu_mm"].by)

                def turn_outputs(v):
                    for t in range(TT):
                        mm = pe.transpose(pair[1][:, col(t)], d_o[:, t, v, :], ident)
                    mm.then_inc(gdn["og_mm"].sem, gdn["og_mm"].by)
                stream_update(0)
                parts(43, 46)
                pe.wait_ge(gdn["on"].sem, gdn["on"].at(s))
                turn_outputs(0)
                parts(46, 48)
                pe.wait_ge(gdn["s_new"].sem, gdn["s_new"].at(s, 0))
                stream_update(1)
                pe.wait_ge(gdn["og"].sem, gdn["og"].at(s, 0))
                turn_outputs(1)
            for hf in range(2):
                gdn_loop(pe, hf, body)
                pe_projection(pe, proj_start(hf), gdn["split"], 4 * hf + 3)

        def proj_start(hf):
            return base["gdn", 0] + (4 + 4 * 6 if hf == 0 else CH_GDN - KT)

        def gdn_loop(eng, hf, body):
            n = GDN_KH // 2 - hf
            with eng.Fori(0, n) as i:
                body(hf, i)
            if hf:
                body(hf, n, last=True)

        def act_gdn(act, occ):
            b = base["gdn", 0]

            def conv_in(T, par, tilenum, first):
                act.wait_ge(tile_done.sem, tile_done.at(T))
                if not first:
                    act.wait_ge(conv_done.sem, conv_done.at(tilenum - 1))
                act.copy(d_xp[:, HIST:HIST + HALF], gem[:, par, 0, 0:HALF])
                act.copy(d_xp[:, HIST + HALF:XS0], gem[:, par, 1, 0:SEQ - HALF])
                act.copy(d_xp[:, XS0:XPW].rearrange("p (s n) -> p s n", s=STREAMS)[:, :, HIST:],
                                gem[:, par, 1, SEQ - HALF:HALF].rearrange("p (s n) -> p s n", s=STREAMS))\
                   .then_inc(evacuated[par].sem, evacuated[par].by)
                act_split(act, T, par)

            def conv_out(j, tilenum, freed=None):
                act.wait_ge(conv_step.sem, conv_step.at(tilenum, 3))
                if freed:
                    act.wait_ge(freed[0].sem, freed[0].at(*freed[1:]))
                act.activation(d_in[j][:, 0:SEQ], d_acc[:, 0:SEQ], ACT.Silu)
                act.activation(d_in[j][:, SEQ:TOK].rearrange("p (s n) -> p s n", s=STREAMS),
                                      d_acc[:, XS0:XPW].rearrange("p (s n) -> p s n", s=STREAMS)[:, :, 0:SLEN],
                                      ACT.Silu)\
                   .then_inc(conv_act.sem, conv_act.by)
            conv_in(b, 0, 0, True)
            conv_out(0, 0)
            act.wait_ge(gdn["gates"].sem, gdn["gates"].at(0, 0))
            act.activation(d_l, d_y, ACT.Abs).then_inc(gdn["gact"].sem, gdn["gact"].by)
            act.wait_ge(gdn["gact"].sem, gdn["gact"].at(0, 0))
            act.activation(d_l, d_l, ACT.Exp, scale=-1.0).then_inc(gdn["gact"].sem, gdn["gact"].by)
            act.wait_ge(gdn["gact"].sem, gdn["gact"].at(0, 1))
            act.activation(d_l, d_l, ACT.Ln, bias=ones[:, 0:1]).then_inc(gdn["gact"].sem, gdn["gact"].by)
            act.activation(d_adt[:, 0, :], d_adt[:, 0, :], ACT.Exp).then_inc(gdn["gact"].sem, gdn["gact"].by)
            act.wait_ge(gdn["gates"].sem, gdn["gates"].at(0, 1))
            act.activation(d_gq[:, 1], d_gq[:, 1], ACT.Exp, scale=-1.0).then_inc(gdn["gact"].sem, gdn["gact"].by)
            conv_in(b + 1, 1, 1, False)
            conv_out(1, 1)
            conv_in(b + 2, 0, 2, False)
            conv_out(2, 2)
            act.wait_ge(gdn["copied"].sem, gdn["copied"].at(0))
            act.activation(d_gq[:, 2], d_gq[:, 4], ACT.Exp, scale=-1.0).then_inc(gdn["cact"].sem, gdn["cact"].by)
            act.activation(d_gq[:, 3], d_gq[:, 3], ACT.Exp).then_inc(gdn["cact"].sem, gdn["cact"].by)
            act.activation(d_egs, msc[:, 3, 0:P].rearrange("p (s h) -> p s h", s=STREAMS), ACT.Exp)
            act.activation(d_gq[:, 6], d_glast, ACT.Exp).then_inc(gdn["cact"].sem, gdn["cact"].by)
            conv_in(b + 3, 1, 3, False)
            conv_out(3, 3)

            def body(hf, i, last=False):
                s = i + 4 * hf

                def conv_end(j):
                    if not last:
                        freed = (gdn["qk_mm"], s, j) if j < 2 else (gdn["v_mm"], s, j - 2)
                        conv_out(j, s * 4 + (4 + j), freed)

                def tile_out(j):
                    T = gdn_tile(hf, i, j, last)
                    if j < 4:
                        if not last:
                            conv_in(T, j % 2, s * 4 + (4 + j), False)
                        return
                    act.wait_ge(tile_done.sem, tile_done.at(T))
                    act.wait_ge(gdn["att"].sem, gdn["att"].at(s, 1))
                    act.activation(halves(d_z[j - 4]), slot(j % 2), ACT.Silu).then_inc(evacuated[j % 2].sem, evacuated[j % 2].by)
                    act_split(act, T, j % 2)
                for j in range(2):
                    act.wait_ge(gdn["qk_mm"].sem, gdn["qk_mm"].at(s, j))
                    for t in range(TT):
                        k = j * TT + t
                        if k:
                            act.wait_ge(gdn["sq"].sem, gdn["sq"].at(s, k - 1))
                        ins = act.activation(d_sqs, pair[j][:, col(t)], ACT.Square, accum_out=d_ss[:, k:k + 1])
                        ins.then_inc(gdn["sq"].sem, gdn["sq"].by)
                act.wait_ge(gdn["ss"].sem, gdn["ss"].at(s))
                act.activation(d_rs, d_ss, ACT.Sqrt).then_inc(gdn["std"].sem, gdn["std"].by)
                tile_out(0)
                for j in range(2):
                    act.wait_ge(gdn["v_mm"].sem, gdn["v_mm"].at(s, j))
                    act.copy(d_vt[:, j], tiles5(pair[j])).then_inc(gdn["v"].sem, gdn["v"].by)
                for j in range(2):
                    act.wait_ge(gdn["kq_mm"].sem, gdn["kq_mm"].at(s, j))
                    act.copy(d_kq[:, 1 - j, :], pair[j]).then_inc(gdn["kq"].sem, gdn["kq"].by)
                act.wait_ge(gdn["qkm_mm"].sem, gdn["qkm_mm"].at(s))
                act.copy(d_qk, pair[1]).then_inc(gdn["qkm"].sem, gdn["qkm"].by)
                for v in range(2):
                    act.wait_ge(gdn["dt_mm"].sem, gdn["dt_mm"].at(s, v))
                    for t in range(TT):
                        ins = act.activation(d_dt[:, unit(v, t), :], pair[v][:, col(t)], ACT.Exp,
                                             bias=num("ngc", t, v))
                    ins.then_inc(gdn["dt"].sem, gdn["dt"].by)
                tile_out(1)
                conv_end(0)
                for lv in range(1, LEVELS - 1):
                    for c, (us, bank, n) in enumerate(CHAINS):
                        if (lv, c) in XX:
                            act.wait_ge(gdn["x_mm"].sem, gdn["x_mm"].at(s, XX[lv, c]))
                            act.copy(d_T[:, us, :].rearrange("p u n -> p (u n)"),
                                     msc[:, bank + 1, 0:(us.stop - us.start) * P])\
                               .then_inc(gdn["t"].sem, gdn["t"].by)
                    if lv == 3:
                        conv_end(1)
                        tile_out(2)
                conv_end(2)
                act.wait_ge(gdn["y_mm"].sem, gdn["y_mm"].at(s, PX[LEVELS - 1, 1]))
                act.dma_start(d_sin, gdn_s[s]).then_inc(d_sld.sem, d_sld.by)
                tile_out(3)

                def squares(t):
                    for v in range(2):
                        k = 2 * t + v
                        act.wait_ge(gdn["o"].sem, gdn["o"].at(s, t))
                        if k:
                            act.wait_ge(gdn["osq"].sem, gdn["osq"].at(s, k - 1))
                        act.activation(d_sqs, d_o[:, t, v, :], ACT.Square, accum_out=d_os[:, k:k + 1])\
                           .then_inc(gdn["osq"].sem, gdn["osq"].by)

                def from_state(t):
                    act.wait_ge(gdn["ks_mm"].sem, gdn["ks_mm"].at(s, t))
                    for v in range(2):
                        src = msc[:, 1, col(v)] if t < PT else msc[:, 2, col(2 + v)]
                        ins = act.activation(d_o[:, t, v, :], src, ACT.Copy, scale=num("eg", t, v))
                    ins.then_inc(gdn["a"].sem, gdn["a"].by)

                def new_values(t):
                    act.wait_ge(gdn["tw_mm"].sem, gdn["tw_mm"].at(s, t))
                    for v in range(2):
                        ins = act.activation(d_vn[:, v, :], msc[:, 2, col(v)], ACT.Copy, scale=num("beta", t, v))
                    ins.then_inc(gdn["vn"].sem, gdn["vn"].by)
                act.wait_ge(gdn["att"].sem, gdn["att"].at(s, 1))
                for t in range(PT):
                    from_state(t)
                    if t in (1, 2):
                        v = t - 1
                        act.wait_ge(gdn["f_mm"].sem, gdn["f_mm"].at(s, v))
                        act.copy(d_f[:, v], msc[:, 3, 2 * P:4 * P].rearrange("p (a n) -> p a n", a=2))\
                           .then_inc(gdn["f"].sem, gdn["f"].by)
                    new_values(t)
                    if t:
                        squares(t - 1)
                    if t == 2:
                        conv_end(3)
                from_state(PT)
                new_values(PT)
                squares(3)
                squares(4)
                act.wait_ge(gdn["oss"].sem, gdn["oss"].at(s))
                act.activation(d_ors, d_os, ACT.Sqrt).then_inc(gdn["ostd"].sem, gdn["ostd"].by)
                tile_out(4)
                tile_out(5)
                act.wait_ge(gdn["s_new"].sem, gdn["s_new"].at(s, 1))
                act.dma_start(gdn_s_out[s], d_sin).then_inc(d_sst.sem, d_sst.by)
                act.dma_start(gdn_p_out[s], d_s).then_inc(d_sst.sem, d_sst.by)
            for hf in range(2):
                gdn_loop(act, hf, body)
                act_projection(act, ("gdn", 0), proj_start(hf), stats=hf == 1)

        def dve_gdn(dve, occ):
            b = base["gdn", 0]

            def conv(T, par, tilenum, head, j, first=False, taps=range(CONV)):
                if 0 in taps and not first:
                    dve.wait_ge(conv_act.sem, conv_act.at(tilenum - 1))
                seg = d_xp[:, XS0:XPW].rearrange("p (s n) -> p s n", s=STREAMS)
                old = hist[:, head, j * 24:(j + 1) * 24].rearrange("p (s n) -> p s n", s=STREAMS)
                if 0 in taps:
                    dve.tensor_copy(seg[:, :, 0:HIST], old).then_inc(gdn["conv_h"].sem, gdn["conv_h"].by)
                    dve.wait_ge(gdn["conv_h"].sem, gdn["conv_h"].at(tilenum))
                    dve.wait_ge(evacuated[par].sem, evacuated[par].at(half(T)))
                for r in taps:
                    tap = convw[:, head, j * CONV + r:j * CONV + r + 1]
                    src = d_xp[:, r:r + XPW - HIST]
                    dst = d_acc[:, 0:XPW - HIST]
                    if r == 0:
                        ins = dve.tensor_scalar(dst, src, tap, None, ALU.mult)
                    else:
                        dve.wait_ge(conv_step.sem, conv_step.at(tilenum, r - 1))
                        ins = dve.scalar_tensor_tensor(out=dst, in0=src, scalar=tap, in1=dst, op0=ALU.mult,
                                                       op1=ALU.add)
                    ins.then_inc(conv_step.sem, conv_step.by)
                if CONV - 1 not in taps:
                    return
                new = newh[:, head, j * 27:(j + 1) * 27].rearrange("p (s n) -> p s n", s=STREAMS + 1)
                dve.tensor_copy(new[:, 0, :], d_xp[:, SEQ:SEQ + HIST])
                dve.tensor_copy(new[:, 1:, :], seg[:, :, SLEN:SLEN + HIST]).then_inc(conv_done.sem, conv_done.by)

            dve.wait_ge(d_param.sem, 4 * 16)
            dve.memset(d_xp[:, 0:HIST], 0.0).then_inc(gdn["zero"].sem, gdn["zero"].by)
            dve.wait_ge(gdn["zero"].sem, gdn["zero"].at(0))
            conv(b, 0, 0, 0, 0, first=True)
            dve.wait_ge(gdn["ab_mm"].sem, gdn["ab_mm"].at(0))
            ab = msc[:, 0, 0:TT * 32].rearrange("p (t n) -> p t n", t=TT)
            dtb = d_adt[:, 1, :].unsqueeze(1).broadcast_to([P, TT, GDN_VH])
            dve.tensor_tensor(d_y, ab[:, :, 0:GDN_VH], dtb, ALU.add).then_inc(gdn["gates"].sem, gdn["gates"].by)
            dve.tensor_copy(d_gq[:, 1], ab[:, :, GDN_VH:]).then_inc(gdn["gates"].sem, gdn["gates"].by)
            dve.wait_ge(gdn["gact"].sem, gdn["gact"].at(0, 2))
            dve.scalar_tensor_tensor(out=d_y, in0=d_y, scalar=0.0, in1=d_l, op0=ALU.max, op1=ALU.add)\
               .then_inc(gdn["gates"].sem, gdn["gates"].by)
            dve.wait_ge(gdn["gates"].sem, gdn["gates"].at(0, 2))
            dve.wait_ge(gdn["gact"].sem, gdn["gact"].at(0, 3))
            dve.tensor_tensor(d_y, d_y, d_adt[:, 0, :].unsqueeze(1).broadcast_to([P, TT, GDN_VH]), ALU.mult)\
               .then_inc(gdn["gates"].sem, gdn["gates"].by)
            dve.wait_ge(gdn["gates"].sem, gdn["gates"].at(0, 3))
            dve.tensor_scalar(d_gq[:, 0], d_y, -1.0, None, ALU.mult).then_inc(gdn["gates"].sem, gdn["gates"].by)
            dve.wait_ge(gdn["gact"].sem, gdn["gact"].at(0, 4))
            dve.tensor_scalar(d_gq[:, 1], d_gq[:, 1], 1.0, None, ALU.add).then_inc(gdn["gates"].sem, gdn["gates"].by)
            dve.wait_ge(gdn["gates"].sem, gdn["gates"].at(0, 5))
            dve.reciprocal(d_gq[:, 1], d_gq[:, 1]).then_inc(gdn["gates"].sem, gdn["gates"].by)
            conv(b + 1, 1, 1, 0, 1)
            conv(b + 2, 0, 2, 0, 2)
            dve.wait_ge(gdn["cum_mm"].sem, gdn["cum_mm"].at(0))
            cum = msc[:, 1, 0:TH].rearrange("p (t h) -> p t h", t=TT)
            glast = msc[:, 2, 0:TH].rearrange("p (t h) -> p t h", t=TT)
            dve.tensor_scalar(d_gq[:, 4], cum, -1.0, None, ALU.mult)
            dve.tensor_copy(d_glast, glast).then_inc(gdn["cum"].sem, gdn["cum"].by)
            dve.wait_ge(gdn["cum"].sem, gdn["cum"].at(0))
            dve.tensor_tensor(d_gq[:, 3], d_glast, cum, ALU.subtract).then_inc(gdn["copied"].sem, gdn["copied"].by)
            dve.wait_ge(gdn["cact"].sem, gdn["cact"].at(0, 2))
            dve.tensor_scalar(d_gq[:, 5], d_gq[:, 2], -1.0, None, ALU.mult).then_inc(gdn["neg"].sem, gdn["neg"].by)
            dve.wait_ge(gdn["neg"].sem, gdn["neg"].at(0))
            conv(b + 3, 1, 3, 0, 3)
            dve.memset(d_os, 0.0).then_inc(gdn["s_new"].sem, gdn["s_new"].by)
            dve.memset(d_ors, 0.0).then_inc(gdn["og"].sem, gdn["og"].by)
            dve.memset(d_rs, 0.0).then_inc(d_sst.sem, d_sst.by)

            def body(hf, i, last=False):
                s = i + 4 * hf

                def convolve(j, taps=range(CONV)):
                    if not last:
                        conv(gdn_tile(hf, i, j, last), j % 2, s * 4 + (4 + j), s + 1, j, taps=taps)
                dve.tensor_copy(d_hegs, d_egs[:, :, bass.ds(s * 2, 2)])
                dve.tensor_copy(d_hq.rearrange("p a t h -> p (a t) h"),
                                       d_gq.rearrange("p a t h -> p (a t) h")[:, :, bass.ds(s * 2, 2)])\
                   .then_inc(gdn["hq"].sem, gdn["hq"].by)
                dve.wait_ge(gdn["sq"].sem, gdn["sq"].at(s, NU - 1))
                dve.tensor_scalar(d_ss, d_ss, L2_EPS, None, ALU.add).then_inc(gdn["ss"].sem, gdn["ss"].by)
                dve.wait_ge(gdn["std"].sem, gdn["std"].at(s))
                dve.reciprocal(d_rs, d_rs).then_inc(gdn["rs"].sem, gdn["rs"].by)
                dve.wait_ge(gdn["rs"].sem, gdn["rs"].at(s, 0))
                dve.tensor_scalar(d_rs[:, 0:TT], d_rs[:, 0:TT], float(P) ** -0.5, None, ALU.mult)\
                   .then_inc(gdn["rs"].sem, gdn["rs"].by)
                dve.wait_ge(gdn["rs"].sem, gdn["rs"].at(s, 1))
                dve.tensor_tensor(d_qt, tiles5(pair[0]), bc(d_rs[:, 0:TT], P), ALU.mult).then_inc(gdn["qt"].sem, gdn["qt"].by)
                dve.tensor_tensor(d_kt, tiles5(pair[1]), bc(d_rs[:, TT:NU], P), ALU.mult).then_inc(gdn["kt"].sem, gdn["kt"].by)
                dve.wait_ge(gdn["hq"].sem, gdn["hq"].at(s))
                convolve(0)
                dve.wait_ge(gdn["kk_mm"].sem, gdn["kk_mm"].at(s))
                dve.wait_ge(d_sst.sem, d_sst.at(s - 1, 1))
                for v in range(2):
                    pu, su = slice(4 * v, 4 * v + 4), 8 + v
                    beta = d_hq[:, 1, :, v]
                    dve.tensor_tensor(d_M[:, pu, :], tiles5(pair[0])[:, 0:PT, :], bc(beta[:, 0:PT], P), ALU.mult)
                    dve.tensor_scalar(d_M[:, su, :], pair[0][:, col(PT)], num("beta", PT, v), None, ALU.mult)\
                       .then_inc(gdn["kk"].sem, gdn["kk"].by)

                def chain(c):
                    us, bank, n = CHAINS[c]
                    nu = us.stop - us.start
                    return (us, over_tiles(ident, nu), *(
                        msc[:, bank + j, 0:nu * P].rearrange("p (u n) -> p u n", n=P) for j in range(2)))

                def blocks(level, c, out, src):
                    us = CHAINS[c][0]
                    return dve.tensor_tensor(out, src, over_tiles(const(C_MASK + level * P), us.stop - us.start),
                                             ALU.mult)

                def lower(c):
                    us, eye, out0, out1 = chain(c)
                    blocks(0, c, d_P[:, us, :], d_M[:, us, :]).then_inc(gdn["ml"].sem, gdn["ml"].by)
                    dve.wait_ge(gdn["ml"].sem, gdn["ml"].at(s, c))
                    dve.tensor_tensor(d_U[:, us, :], eye, d_P[:, us, :], ALU.subtract)\
                       .then_inc(gdn["u"].sem, gdn["u"].by)

                def turned(c):
                    us, eye, out0, out1 = chain(c)
                    dve.wait_ge(gdn["tr_mm"].sem, gdn["tr_mm"].at(s, c))
                    dve.tensor_tensor(d_T[:, us, :], eye, out1 if c == 2 else out0, ALU.subtract).then_inc(gdn["t0"].sem, gdn["t0"].by)
                for v in range(2):
                    pu, su = slice(4 * v, 4 * v + 4), 8 + v
                    dve.wait_ge(gdn["kk"].sem, gdn["kk"].at(s, v))
                    dve.wait_ge(gdn["dt"].sem, gdn["dt"].at(s, v))
                    dve.tensor_tensor(d_M[:, pu, :], d_M[:, pu, :], d_dt[:, pu, :], ALU.mult)
                    dve.tensor_tensor(d_M[:, su, :], d_M[:, su, :], d_dt[:, su, :], ALU.mult)\
                       .then_inc(gdn["m"].sem, gdn["m"].by)
                    dve.wait_ge(gdn["m"].sem, gdn["m"].at(s, v))
                    lower(v)
                lower(2)
                for c in range(3):
                    turned(c)
                dve.wait_ge(gdn["qkm"].sem, gdn["qkm"].at(s))
                qk5 = tiles5(d_qk)

                def attention(v):
                    pu, su = slice(4 * v, 4 * v + 4), 8 + v
                    dve.tensor_tensor(d_at[:, pu, :], d_dt[:, pu, :], qk5[:, 0:PT, :], ALU.mult)
                    dve.tensor_tensor(d_at[:, su, :], d_dt[:, su, :], qk5[:, PT, :], ALU.mult)\
                       .then_inc(gdn["att"].sem, gdn["att"].by)
                for lv in range(1, LEVELS):
                    def cut(c):
                        us, eye, out0, out1 = chain(c)
                        dve.wait_ge(gdn["p_mm"].sem, gdn["p_mm"].at(s, PX[lv, c]))
                        blocks(lv, c, d_P[:, us, :], out0).then_inc(gdn["p"].sem, gdn["p"].by)

                    def merge(c):
                        us, eye, out0, out1 = chain(c)
                        dve.wait_ge(gdn["y_mm"].sem, gdn["y_mm"].at(s, PX[lv, c]))
                        dve.tensor_tensor(d_U[:, us, :], d_U[:, us, :], out0, ALU.subtract)\
                           .then_inc(gdn["u"].sem, gdn["u"].by)
                    cut(0)
                    cut(1)
                    merge(0)
                    merge(1)
                    if (lv, 2) in ML:
                        cut(2)
                        merge(2)
                    if lv in (1, 3):
                        attention(lv // 2)
                    if lv == 2:
                        convolve(1)
                    if lv == 5:
                        convolve(2)
                dve.memset(d_s, 0.0).then_inc(gdn["s_zero"].sem, gdn["s_zero"].by)

                def key_ends(t):
                    dve.wait_ge(gdn["kt"].sem, gdn["kt"].at(s))
                    if t:
                        dve.wait_ge(gdn["su_mm"].sem, gdn["su_mm"].at(s, t - 1))
                    for v in range(2):
                        ins = dve.tensor_scalar(d_ke[:, v, :], d_kt[:, t, :], num("ke", t, v), None, ALU.mult)
                    ins.then_inc(gdn["ke"].sem, gdn["ke"].by)

                def less_old(t):
                    dve.wait_ge(gdn["ks_mm"].sem, gdn["ks_mm"].at(s, t))
                    for v in range(2):
                        out, src = (d_w, msc[:, 0, col(v)]) if t < PT else (d_ws, msc[:, 3, col(v)])
                        ins = dve.scalar_tensor_tensor(out=out[:, v, :], in0=src, scalar=num("neg_eg", t, v),
                                                       in1=d_vt[:, v, t, :], op0=ALU.mult, op1=ALU.add)
                    ins.then_inc(gdn["w"].sem, gdn["w"].by)

                def outputs(t):
                    dve.wait_ge(gdn["o_mm"].sem, gdn["o_mm"].at(s, t))
                    dve.wait_ge(gdn["a"].sem, gdn["a"].at(s, t))
                    dve.tensor_tensor(d_o[:, t], d_o[:, t],
                                      msc[:, 3, 0:2 * P].rearrange("p (v n) -> p v n", v=2), ALU.add)\
                       .then_inc(gdn["o"].sem, gdn["o"].by)

                def decay_stream(v):
                    dve.wait_ge(gdn["f_mm"].sem, gdn["f_mm"].at(s, v))
                    dve.tensor_tensor(d_sin[:, v], d_sin[:, v], bc(d_hegs[:, :, v], P), ALU.mult)\
                       .then_inc(gdn["s_dec"].sem, gdn["s_dec"].by)

                def spread_values(v):
                    src = d_vn[:, v, :].unsqueeze(1).broadcast_to([P, STREAMS, P])
                    dve.tensor_tensor(d_vx, src, bc(cs[:, C_M8:C_M8 + STREAMS], P), ALU.mult)\
                       .then_inc(gdn["vx"].sem, gdn["vx"].by)

                def new_stream(v):
                    dve.wait_ge(gdn["ssu_mm"].sem, gdn["ssu_mm"].at(s, v))
                    dve.wait_ge(gdn["s_dec"].sem, gdn["s_dec"].at(s, v))
                    dve.tensor_tensor(d_sin[:, v], d_sin[:, v],
                                      msc[:, 0:2, :].rearrange("p b (s n) -> p (b s) n", n=P), ALU.add)\
                       .then_inc(gdn["s_new"].sem, gdn["s_new"].by)

                def gate_outputs(v):
                    dve.wait_ge(gdn["og_mm"].sem, gdn["og_mm"].at(s, v))
                    dve.wait_ge(evacuated[v].sem, evacuated[v].at(half(gdn_tile(hf, i, 4 + v, last))))
                    dve.scalar_tensor_tensor(out=d_og[v], in0=pair[1], scalar=nrm[:, 2:3], in1=d_z[v],
                                             op0=ALU.mult, op1=ALU.mult)\
                       .then_inc(gdn["og"].sem, gdn["og"].by)
                    split_hidden(dve, d_og[v], i, v, s, gdn)
                for t in range(PT):
                    key_ends(t)
                    less_old(t)
                    if t == 0:
                        convolve(3, range(0, 2))
                    if t == 1:
                        convolve(3, range(2, CONV))
                    if t == 2:
                        decay_stream(0)
                    if t == 3:
                        less_old(PT)
                    outputs(t)
                    dve.wait_ge(gdn["su_mm"].sem, gdn["su_mm"].at(s, t))
                    if t == 0:
                        dve.wait_ge(gdn["s_zero"].sem, gdn["s_zero"].at(s))
                    else:
                        dve.wait_ge(gdn["state"].sem, gdn["state"].at(s, t - 1))
                    for v in range(2):
                        ins = dve.scalar_tensor_tensor(out=d_s[:, v, :], in0=d_s[:, v, :],
                                                       scalar=num("egl", t, v), in1=msc[:, 0, col(v)],
                                                       op0=ALU.mult, op1=ALU.add)
                    ins.then_inc(gdn["state"].sem, gdn["state"].by)
                key_ends(PT)
                decay_stream(1)
                dve.wait_ge(gdn["vn"].sem, gdn["vn"].at(s, PT))
                spread_values(0)
                outputs(PT)
                dve.wait_ge(gdn["osq"].sem, gdn["osq"].at(s, NU - 1))
                dve.tensor_scalar(d_os, d_os, 1.0 / P, RMS_EPS, ALU.mult, ALU.add).then_inc(gdn["oss"].sem, gdn["oss"].by)
                dve.wait_ge(gdn["ostd"].sem, gdn["ostd"].at(s))
                dve.reciprocal(d_ors, d_ors).then_inc(gdn["ors"].sem, gdn["ors"].by)
                dve.wait_ge(gdn["ors"].sem, gdn["ors"].at(s))
                flat_o = d_o.rearrange("p t v n -> p (t v) n")
                dve.tensor_tensor(flat_o, flat_o, bc(d_ors, P), ALU.mult).then_inc(gdn["on"].sem, gdn["on"].by)
                new_stream(0)
                spread_values(1)
                gate_outputs(0)
                new_stream(1)
                gate_outputs(1)
            for hf in range(2):
                gdn_loop(dve, hf, body)
                dve_down(dve, ("gdn", 0), proj_start(hf), ALPHA if hf == 0 else 1.0, stats=hf == 1)
        PE_OF = {"ffn": pe_ffn, "gla": pe_gla, "gdn": pe_gdn}
        ACT_OF = {"ffn": act_ffn, "gla": act_gla, "gdn": act_gdn}
        DVE_OF = {"ffn": dve_ffn, "gla": dve_gla, "gdn": dve_gdn}
        y_stored = Signal("y_stored", per=KT, by=16)
        block = ctx.enter_context(nc.Block())

        @block.sync
        def _(sp):
            load_start(sp)
            for dst, src in ((a_w1, w_a1), (a_w2[0:RANK, :], w_a2), (a_b[0:1, :], b_a)):
                sp.dma_start(dst, src).then_inc(a_param.sem, a_param.by)
            for dst, src in ((d_wab, w_ab), (d_adt, a_dt.broadcast_to([P, 2, GDN_VH])),
                             (convw[:], conv_w), (hist[:], hist_in)):
                sp.dma_start(dst, src).then_inc(d_param.sem, d_param.by)
            sp_supply(sp)
            for k in range(KT):
                sp.wait_ge(x_ready.sem, x_ready.at(LN_OF[PLAN[-1]], k))
                sp.dma_start(y_out[:, k, :], x[:, k, :]).then_inc(y_stored.sem, y_stored.by)
            sp.wait_ge(conv_done.sem, conv_done.at(4 * GDN_KH - 1))
            sp.dma_start(hist_out, newh[:]).then_inc(hist_stored.sem, hist_stored.by)
            sp.wait_ge(y_stored.sem, y_stored.at(0, KT - 1))
            sp.wait_ge(hist_stored.sem, hist_stored.at(0))
            sp.wait_ge(d_sst.sem, d_sst.at(GDN_KH - 1, 1))

        @block.gpsimd
        def _(pool):
            done = 0
            for n, ph in enumerate(PLAN):
                end = base[PLAN[n + 1]] + 2 if ph != PLAN[-1] else N_CHUNKS
                pool_supply(pool, done, end)
                done = end
                if ph != PLAN[-1]:
                    pool_ln(pool, ph)

        @block.scalar
        def _(act):
            act_split(act, -2, 0)
            act_split(act, -1, 1)
            for kind, occ in PLAN:
                ACT_OF[kind](act, occ)
                act_ln(act, (kind, occ))

        @block.vector
        def _(dve):
            for k in range(KT):
                dve.wait_ge(x_loaded[2 * k // KT].sem, x_loaded[2 * k // KT].at(0))
                dve.tensor_copy(xh[:, k, :], x[:, k, :]).then_inc(start_split.sem, start_split.by)
                dve.wait_ge(start_split.sem, start_split.at(k))
                dve.tensor_tensor(xl[:, k, :], x[:, k, :], xh[:, k, :].bitcast(F32), ALU.subtract)\
                   .then_inc(start_split.sem, start_split.by)
            dve.wait_ge(inputs_loaded.sem, 16 * N_IN)
            for kind, occ in PLAN:
                DVE_OF[kind](dve, occ)
                dve_ln(dve, (kind, occ))

        @block.tensor
        def _(pe):
            for kind, occ in PLAN:
                PE_OF[kind](pe, occ)
                pe_ln(pe, (kind, occ))


def chunk(w):
    k = w.shape[0] // P
    out = np.zeros((P, KT, P), w.dtype)
    out[:, :k] = w.reshape(k, P, P).transpose(1, 0, 2)
    return out.reshape(P, D)


def lay_weights(ins):
    out = np.zeros((N_CHUNKS, P, D), np.float32)
    n = 0

    def put(w, row, col, rows=D):
        nonlocal n
        out[n] = chunk(w[row:row + rows, col:col + P])
        n += 1

    def put_head(w, first, gates):
        for c in first:
            put(w, 0, c)
        for c in gates:
            put(w, 0, c)

    for kind, occ in PLAN:
        if kind == "ffn":
            name, layer = f"ffn{occ % 2 + 1}", occ // 2
            gu, dn, f0 = ins[name + "_w_gu"][layer], ins[name + "_w_d"][layer], 0
            for g in GROUPS:
                for f in range(f0, f0 + g):
                    put(gu, 0, f * P)
                    put(gu, 0, D_FF + f * P)
                for m in range(KT):
                    put(dn, f0 * P, m * P, g * P)
                f0 += g
        elif kind == "gla":
            w, wo = ins["gla_w_in"][0], ins["gla_w_o"][0]
            qkv = [(h * P, 512 + h * P, 1024 + 2 * h * P, 1024 + (2 * h + 1) * P) for h in range(GLA_HEADS)]
            put_head(w, qkv[0], ())
            for h in range(GLA_HEADS):
                put_head(w, (2048 + 2 * h * P, 2048 + (2 * h + 1) * P), qkv[h + 1] if h + 1 < GLA_HEADS else ())
            for m in range(KT):
                put(wo, 0, m * P)
        else:
            w, wo = ins["gdn_w_in"][0], ins["gdn_w_o"][0]
            qkv = [(h * P, 1024 + h * P, 2048 + 2 * h * P, 2048 + (2 * h + 1) * P) for h in range(GDN_KH)]
            put_head(w, qkv[0], ())
            for h in range(GDN_KH):
                put_head(w, qkv[h + 1] if h + 1 < GDN_KH else (), (4096 + 2 * h * P, 4096 + (2 * h + 1) * P))
                if h % 4 == 3:
                    for m in range(KT):
                        put(wo, (h // 4) * D, m * P)
    assert n == N_CHUNKS
    return out


def columns(a, n):
    return np.ascontiguousarray(np.moveaxis(a.reshape(a.shape[:-1] + (n, P)), -1, 0))


def kernel(**ins):
    import concourse.bacc as _bacc
    from concourse.bass_utils import run_bass_kernel_spmd as _run

    ins = {k: np.asarray(v) for k, v in ins.items()}
    tokens = np.concatenate([ins["x_prompt"].reshape(SEQ, D), ins["x_sample"].reshape(TOK - SEQ, D)], 0)
    ab = ins["gdn_w_in"][0][:, 6144:6176]
    conv = columns(ins["gdn_conv_w"][0], 32)
    hist = columns(ins["state_gdn_conv"][:, 0], 32)
    by_head = [[h, 8 + h, 16 + 2 * h, 17 + 2 * h] for h in range(GDN_KH)]
    norm = np.zeros((P, 4), np.float32)
    norm[:, 0:2] = columns(ins["gla_norm_g"][0], 2)
    norm[:, 2] = ins["gdn_norm_g"][0]
    arrays = {
        "wstream": lay_weights(ins),
        "x_in": columns(tokens, KT).transpose(0, 2, 1),
        "consts": constants(),
        "ln_cols": np.stack([columns(ins["ln_g"].reshape(6, D), KT), columns(ins["ln_b"].reshape(6, D), KT)], 2),
        "w_a1": ins["gla_w_a1"][0].reshape(KT, P, RANK).transpose(1, 0, 2),
        "w_a2": ins["gla_w_a2"][0],
        "b_a": ins["gla_b_a"],
        "norm_cols": norm,
        "w_ab": ab.reshape(KT, P, 32).transpose(1, 0, 2),
        "a_dt": np.stack([ins["gdn_a_log"], ins["gdn_dt_bias"]], 1),
        "conv_w": conv.transpose(0, 2, 1)[:, by_head].reshape(P, GDN_KH, 16),
        "hist_in": hist.transpose(0, 3, 1, 2)[:, by_head].reshape(P, GDN_KH, 96),
        "gla_s": ins["state_gla"][:, 0].transpose(1, 2, 0, 3),
        "gdn_s": ins["state_gdn"][:, 0].reshape(STREAMS, GDN_KH, 2, P, P).transpose(1, 3, 2, 0, 4),
    }
    outs = {
        "y_out": (P, KT, TOK), "gla_p_out": (4, P, 256), "gdn_p_out": (GDN_KH, P, 2, P),
        "hist_out": (P, GDN_KH, 108), "gla_s_out": (4, P, 8, 256), "gdn_s_out": (GDN_KH, P, 2, STREAMS, P),
    }
    arrays = {k: np.ascontiguousarray(v) for k, v in arrays.items()}
    nc = _bacc.Bacc("TRN2", target_bir_lowering=False, num_devices=1)
    args = [nc.dram_tensor(k, v.shape, mybir.dt.from_np(v.dtype), kind="ExternalInput").ap()
            for k, v in arrays.items()]
    args += [nc.dram_tensor(k, s, F32, kind="ExternalOutput").ap() for k, s in outs.items()]
    build(nc, *args)
    r = _run(nc, [arrays], core_ids=[0]).results[0]
    y = r["y_out"].transpose(2, 1, 0).reshape(TOK, D)
    flat = [c for head in by_head for c in head]
    hist_rows = np.empty((32, P, 9, 3), np.float32)
    hist_rows[flat] = r["hist_out"].reshape(P, 32, 9, 3).transpose(1, 0, 2, 3)
    hist_rows = hist_rows.transpose(2, 3, 0, 1).reshape(9, 1, 3, 32 * P)
    return (y[:SEQ].reshape(1, SEQ, D), y[SEQ:].reshape(STREAMS, SLEN, D),
            r["gla_p_out"].reshape(1, 1, 4, P, 256), r["gdn_p_out"].transpose(0, 2, 1, 3).reshape(1, 1, 16, P, P), hist_rows[0:1],
            r["gla_s_out"].transpose(2, 0, 1, 3)[:, None], r["gdn_s_out"].transpose(3, 0, 2, 1, 4).reshape(STREAMS, 1, 16, P, P),
            hist_rows[1:9])
```
